# Optimizing a Trainium2 kernel written in Bass

```python
import math
import jax, jax.numpy as jnp
from jax import lax
import numpy as np

D_MODEL = 1024
BATCH = 1
SEQ = 256
DEPTH = 2

N_MEM = 256
DN_HEADS = 4
DN_HEAD_DIM = 128
DN_WIDTH = DN_HEADS * DN_HEAD_DIM
DN_CONV = 4
DN_CHUNK = 64
DA_HEADS = 8
DA_HEAD_DIM = 64
DA_WIDTH = DA_HEADS * DA_HEAD_DIM
DA_BRANCHES = ((128, 1), (512, 4), (2048, 16))
DA_BLOCK = 128
MIX_WIDTH = DN_WIDTH + DA_WIDTH
AB_IN = 4 * DN_WIDTH + 2 * DN_HEADS + 3 * DA_WIDTH
SC_WIDTH = D_MODEL
SC_CONV = 3
XA_HEADS = 4
XA_HEAD_DIM = D_MODEL // XA_HEADS
N_EXPERTS = 16
N_GROUPS = 4
EXPERTS_PER_GROUP = N_EXPERTS // N_GROUPS
TOP_K = 2
D_EXPERT = D_MODEL // 2
DEEPNORM_ALPHA = (2 * DEPTH) ** 0.25
DEEPNORM_BETA = (8 * DEPTH) ** -0.25
LN_EPS = 1e-5
RMS_EPS = 1e-6
N_EVEN = (DEPTH + 1) // 2
N_ODD = DEPTH // 2

kernel_name = 'hybrid_deltanet_dilated_shortconv_moe'

def layer_norm(x, g, b):
    xf = x.astype(jnp.float32)
    mu = jnp.mean(xf, -1, keepdims=True)
    var = jnp.mean(jnp.square(xf - mu), -1, keepdims=True)
    return ((xf - mu) * lax.rsqrt(var + LN_EPS) * g.astype(jnp.float32) + b.astype(jnp.float32)).astype(x.dtype)

def causal_dwconv(x, w):
    k, c = w.shape
    return lax.conv_general_dilated(x, w[:, None, :].astype(x.dtype), window_strides=(1,), padding=[(k - 1, 0)], dimension_numbers=('NWC', 'WIO', 'NWC'), feature_group_count=c)

def l2norm(t):
    return t * lax.rsqrt(jnp.sum(t * t, -1, keepdims=True) + RMS_EPS)

def gated_delta_rule_chunked(q, k, v, g, beta):
    b, h, s, dk = q.shape
    dv = v.shape[-1]
    n = s // DN_CHUNK
    q, k, v = (t.reshape(b, h, n, DN_CHUNK, t.shape[-1]) for t in (q, k, v))
    g = jnp.cumsum(g.reshape(b, h, n, DN_CHUNK), -1)
    beta = beta.reshape(b, h, n, DN_CHUNK)
    incl = jnp.tril(jnp.ones((DN_CHUNK, DN_CHUNK), bool))
    strict = jnp.tril(jnp.ones((DN_CHUNK, DN_CHUNK), bool), -1)
    decay = jnp.exp(jnp.where(incl, g[..., :, None] - g[..., None, :], -jnp.inf))
    kb = k * beta[..., None]
    a_mat = jnp.where(strict, jnp.einsum('bhnik,bhnjk->bhnij', kb, k) * decay, 0.0)
    lower = a_mat + jnp.eye(DN_CHUNK, dtype=q.dtype)
    rhs = jnp.concatenate([v * beta[..., None], kb * jnp.exp(g)[..., None]], -1)
    sol = lax.linalg.triangular_solve(lower, rhs, left_side=True, lower=True, unit_diagonal=True)
    u, w = sol[..., :dv], sol[..., dv:]
    attn = jnp.where(incl, jnp.einsum('bhnik,bhnjk->bhnij', q, k) * decay, 0.0)
    q_dec = q * jnp.exp(g)[..., None]
    k_tail = k * jnp.exp(g[..., -1:] - g)[..., None]
    g_last = jnp.exp(g[..., -1])

    def step(state, xs):
        q_i, k_i, u_i, w_i, a_i, gl_i = xs
        v_new = u_i - jnp.einsum('bhck,bhkv->bhcv', w_i, state)
        o_i = jnp.einsum('bhck,bhkv->bhcv', q_i, state) + jnp.einsum('bhcj,bhjv->bhcv', a_i, v_new)
        state = state * gl_i[..., None, None] + jnp.einsum('bhck,bhcv->bhkv', k_i, v_new)
        return state, o_i

    xs = tuple(jnp.moveaxis(t, 2, 0) for t in (q_dec, k_tail, u, w, attn, g_last))
    _, o = lax.scan(step, jnp.zeros((b, h, dk, dv), q.dtype), xs)
    return jnp.moveaxis(o, 0, 2).reshape(b, h, s, dv)

def dilated_branch(q, k, v, window, dilation):
    b, h, s, dh = q.shape
    length = s // dilation
    span = window // dilation
    n_blk = -(-length // DA_BLOCK)
    padded = n_blk * DA_BLOCK

    def to_blocks(t):
        t = t.reshape(b, h, length, dilation, dh).transpose(0, 1, 3, 2, 4)
        t = jnp.pad(t, ((0, 0), (0, 0), (0, 0), (0, padded - length), (0, 0)))
        return t.reshape(b, h, dilation, n_blk, DA_BLOCK, dh)

    def with_prev(t):
        prev = jnp.pad(t, ((0, 0), (0, 0), (0, 0), (1, 0), (0, 0), (0, 0)))[:, :, :, :-1]
        return jnp.concatenate([prev, t], axis=4)

    qb = to_blocks(q)
    kw = with_prev(to_blocks(k))
    vw = with_prev(to_blocks(v))
    sc = jnp.einsum('bhrnqd,bhrnkd->bhrnqk', qb, kw) * (dh ** -0.5)
    qpos = jnp.arange(n_blk)[:, None] * DA_BLOCK + jnp.arange(DA_BLOCK)[None, :]
    kpos = (jnp.arange(n_blk)[:, None] - 1) * DA_BLOCK + jnp.arange(2 * DA_BLOCK)[None, :]
    dist = qpos[:, :, None] - kpos[:, None, :]
    valid = (dist >= 0) & (dist <= span) & (kpos[:, None, :] >= 0)
    sc = jnp.where(valid, sc, -jnp.inf)
    m = jnp.max(sc, -1, keepdims=True)
    p = jnp.exp(sc - m)
    den = jnp.sum(p, -1)
    o = jnp.einsum('bhrnqk,bhrnkd->bhrnqd', p, vw) / den[..., None]
    lse = m[..., 0] + jnp.log(den)
    o = o.reshape(b, h, dilation, padded, dh)[:, :, :, :length].transpose(0, 1, 3, 2, 4).reshape(b, h, s, dh)
    lse = lse.reshape(b, h, dilation, padded)[..., :length].transpose(0, 1, 3, 2).reshape(b, h, s)
    return o, lse

def dilated_attention(q, k, v):
    outs, lses = zip(*[dilated_branch(q, k, v, wnd, dil) for wnd, dil in DA_BRANCHES])
    wts = jax.nn.softmax(jnp.stack(lses), axis=0)
    return jnp.einsum('ibhs,ibhsd->bhsd', wts, jnp.stack(outs))

def mixer_ab(x, w_in, conv_w, a_log, dt_bias, norm_w, w_out):
    b, s, _ = x.shape
    f32 = jnp.float32
    qkv, z, beta_in, a_in, qkv_d = jnp.split(x @ w_in, [3 * DN_WIDTH, 4 * DN_WIDTH, 4 * DN_WIDTH + DN_HEADS, 4 * DN_WIDTH + 2 * DN_HEADS], axis=-1)
    qkv = jax.nn.silu(causal_dwconv(qkv, conv_w)).astype(f32)
    q, k, v = (t.reshape(b, s, DN_HEADS, DN_HEAD_DIM).transpose(0, 2, 1, 3) for t in jnp.split(qkv, 3, -1))
    q = l2norm(q) * (DN_HEAD_DIM ** -0.5)
    k = l2norm(k)
    beta = jax.nn.sigmoid(beta_in.astype(f32)).transpose(0, 2, 1)
    g = (-jnp.exp(a_log.astype(f32)) * jax.nn.softplus(a_in.astype(f32) + dt_bias.astype(f32))).transpose(0, 2, 1)
    o = gated_delta_rule_chunked(q, k, v, g, beta).transpose(0, 2, 1, 3)
    o = o * lax.rsqrt(jnp.mean(o * o, -1, keepdims=True) + RMS_EPS) * norm_w.astype(f32)
    o_a = (o * jax.nn.silu(z.astype(f32).reshape(b, s, DN_HEADS, DN_HEAD_DIM))).reshape(b, s, DN_WIDTH)
    qd, kd, vd = (t.astype(f32).reshape(b, s, DA_HEADS, DA_HEAD_DIM).transpose(0, 2, 1, 3) for t in jnp.split(qkv_d, 3, -1))
    o_b = dilated_attention(qd, kd, vd).transpose(0, 2, 1, 3).reshape(b, s, DA_WIDTH)
    return jnp.concatenate([o_a, o_b], -1).astype(x.dtype) @ w_out

def short_conv_mixer(x, w_in, conv_w, w_out):
    gate_b, gate_c, hid = jnp.split(x @ w_in, 3, axis=-1)
    return (gate_b * causal_dwconv(gate_c * hid, conv_w)) @ w_out

def memory_cross_attention(x, mem, w_q, w_kv, w_o):
    b, s, d = x.shape
    q = (x @ w_q).astype(jnp.float32).reshape(b, s, XA_HEADS, XA_HEAD_DIM)
    k, v = (t.astype(jnp.float32).reshape(b, -1, XA_HEADS, XA_HEAD_DIM) for t in jnp.split(mem @ w_kv, 2, -1))
    p = jax.nn.softmax(jnp.einsum('bshd,bmhd->bhsm', q, k) * (XA_HEAD_DIM ** -0.5), axis=-1)
    o = jnp.einsum('bhsm,bmhd->bshd', p, v).reshape(b, s, d).astype(x.dtype)
    return o @ w_o

def grouped_moe(x, router_w, router_b, w_gate, w_up, w_down):
    b, s, d = x.shape
    xt = x.reshape(b * s, d)
    scores = jax.nn.softmax((xt @ router_w).astype(jnp.float32), axis=-1)
    sel = scores + router_b.astype(jnp.float32)
    group_score = jnp.sum(lax.top_k(sel.reshape(-1, N_GROUPS, EXPERTS_PER_GROUP), TOP_K)[0], -1)
    group = jnp.argmax(group_score, -1)
    in_group = (jnp.arange(N_EXPERTS) // EXPERTS_PER_GROUP)[None, :] == group[:, None]
    _, idx = lax.top_k(jnp.where(in_group, sel, -jnp.inf), TOP_K)
    wts = jnp.take_along_axis(scores, idx, -1)
    wts = wts / jnp.sum(wts, -1, keepdims=True)
    gates = jnp.einsum('tk,tke->te', wts, jax.nn.one_hot(idx, N_EXPERTS, dtype=jnp.float32)).astype(x.dtype)
    y = jnp.zeros_like(xt)
    for e in range(N_EXPERTS):
        hdn = jax.nn.silu(xt @ w_gate[e]) * (xt @ w_up[e])
        y = y + gates[:, e:e + 1] * (hdn @ w_down[e])
    return y.reshape(b, s, d)

def setup_inputs(seed: int = 0) -> dict:
    key = jax.random.key(seed)
    ks = jax.random.split(key, 24)
    f32 = jnp.float32

    def nrm(k, shape, scale):
        return scale * jax.random.normal(k, shape, f32)

    d = D_MODEL
    dt = jnp.exp(jax.random.uniform(ks[5], (N_EVEN, DN_HEADS), f32, math.log(1e-3), math.log(1e-1)))
    return {
        'x': nrm(ks[0], (BATCH, SEQ, d), 1.0),
        'mem': nrm(ks[1], (BATCH, N_MEM, d), 1.0),
        'ab_w_in': nrm(ks[2], (N_EVEN, d, AB_IN), d ** -0.5),
        'ab_conv_w': nrm(ks[3], (N_EVEN, DN_CONV, 3 * DN_WIDTH), DN_CONV ** -0.5),
        'ab_a_log': jnp.log(jax.random.uniform(ks[4], (N_EVEN, DN_HEADS), f32, 1.0, 16.0)),
        'ab_dt_bias': dt + jnp.log(-jnp.expm1(-dt)),
        'ab_norm_w': 1.0 + nrm(ks[6], (N_EVEN, DN_HEAD_DIM), 0.02),
        'ab_w_out': nrm(ks[7], (N_EVEN, MIX_WIDTH, d), DEEPNORM_BETA * MIX_WIDTH ** -0.5),
        'sc_w_in': nrm(ks[8], (N_ODD, d, 3 * SC_WIDTH), d ** -0.5),
        'sc_conv_w': nrm(ks[9], (N_ODD, SC_CONV, SC_WIDTH), SC_CONV ** -0.5),
        'sc_w_out': nrm(ks[10], (N_ODD, SC_WIDTH, d), DEEPNORM_BETA * SC_WIDTH ** -0.5),
        'xa_w_q': nrm(ks[11], (DEPTH, d, d), d ** -0.5),
        'xa_w_kv': nrm(ks[12], (DEPTH, d, 2 * d), d ** -0.5),
        'xa_w_o': nrm(ks[13], (DEPTH, d, d), DEEPNORM_BETA * d ** -0.5),
        'router_w': nrm(ks[14], (d, N_EXPERTS), d ** -0.5),
        'router_b': nrm(ks[15], (N_EXPERTS,), 0.01),
        'moe_w_gate': nrm(ks[16], (DEPTH, N_EXPERTS, d, D_EXPERT), d ** -0.5),
        'moe_w_up': nrm(ks[17], (DEPTH, N_EXPERTS, d, D_EXPERT), d ** -0.5),
        'moe_w_down': nrm(ks[18], (DEPTH, N_EXPERTS, D_EXPERT, d), DEEPNORM_BETA * D_EXPERT ** -0.5),
        'ln_g': 1.0 + nrm(ks[19], (DEPTH, 3, d), 0.02),
        'ln_b': nrm(ks[20], (DEPTH, 3, d), 0.02),
    }

def reference(x, mem, ab_w_in, ab_conv_w, ab_a_log, ab_dt_bias, ab_norm_w, ab_w_out, sc_w_in, sc_conv_w, sc_w_out, xa_w_q, xa_w_kv, xa_w_o, router_w, router_b, moe_w_gate, moe_w_up, moe_w_down, ln_g, ln_b):
    h = x
    for layer in range(DEPTH):
        i = layer // 2
        if layer % 2 == 0:
            y = mixer_ab(h, ab_w_in[i], ab_conv_w[i], ab_a_log[i], ab_dt_bias[i], ab_norm_w[i], ab_w_out[i])
        else:
            y = short_conv_mixer(h, sc_w_in[i], sc_conv_w[i], sc_w_out[i])
        h = layer_norm(DEEPNORM_ALPHA * h + y, ln_g[layer, 0], ln_b[layer, 0])
        y = memory_cross_attention(h, mem, xa_w_q[layer], xa_w_kv[layer], xa_w_o[layer])
        h = layer_norm(DEEPNORM_ALPHA * h + y, ln_g[layer, 1], ln_b[layer, 1])
        y = grouped_moe(h, router_w, router_b, moe_w_gate[layer], moe_w_up[layer], moe_w_down[layer])
        h = layer_norm(DEEPNORM_ALPHA * h + y, ln_g[layer, 2], ln_b[layer, 2])
    return h


_drawn_inputs = setup_inputs


def setup_inputs(seed=0):
    import zlib

    import numpy as np

    out = dict(_drawn_inputs(seed))
    spreads = {}
    factors = {'ab_norm_w': 2.936}
    for name, (base, spread) in spreads.items():
        noise = np.random.default_rng([zlib.crc32(name.encode()), seed]).standard_normal(out[name].shape)
        drawn = base * np.exp(spread * noise) if base else spread * noise
        out[name] = __import__('jax').numpy.asarray(drawn.astype(out[name].dtype))
    for name, factor in factors.items():
        out[name] = (out[name] * factor).astype(out[name].dtype)
    return out
```

```python
from contextlib import ExitStack

import numpy as np

import concourse.bass as bass
from concourse import mybir

F32 = mybir.dt.float32
BF16 = mybir.dt.bfloat16
I32 = mybir.dt.int32
ALU = mybir.AluOpType
ACTF = mybir.ActivationFunctionType
AX = mybir.AxisListType.X

P = 128
PE, ACT, DVE, POOL = "pe", "act", "dve", "pool"
BANKS = 8
BANK = 512
NEG = -1.0e30


def trunk_steps():
    def transposed(kind, *who):
        return [(kind, *who, t, g) for t in range(2) for g in range(2)]

    def normed(l, s):
        out = []
        for t in range(2):
            out += [("ln_stats", l, s, t), ("ln_rstd", l, s, t), ("ln_norm", l, s, t)]
        for t in range(2):
            out += [("hT", l, s, t, g) for g in range(2)]
        return out + [("ln_h", l, s, t) for t in range(2)]

    def cross_kv(l):
        return ([("xk", l, m) for m in range(4)] + [("xv", l, half, t) for half in range(2) for t in range(2)])

    def cross(l):
        out = [("xq", l, m) for m in range(4)] + [("xs", l, 0), ("xn", l, 0)]
        for hd in range(4):
            if hd < 3:
                out += [("xs", l, hd + 1), ("xn", l, hd + 1)]
            out += [("xp", l, hd), ("xo", l, hd)]
        return out

    def projected(l, s):
        return [("y", l, s, half, t) for half in range(2) for t in range(2)]

    a = [("masks",), ("params",)] + transposed("xT") + [("ba",), ("gates",)]
    a += [("qkv", s, m) for s in (0, 1) for m in range(2)]
    a += [("sumsq",), ("cumsum",), ("cols",)]
    a += [("qkv", 2, m) for m in range(2)]
    a += [("rowg", t) for t in range(2)] + [("rowh", t) for t in range(2)]
    a += [("gram", t) for t in range(2)] + [("qk", t) for t in range(2)]
    a += transposed("memT")
    a += [("blk", 0, t) for t in range(2)]
    a += [("z", t) for t in range(2)]
    a += [("inv0", t) for t in range(2)] + [("ktok",)] + [("vtok", t) for t in range(2)]
    filler = [[("qd", 0), ("qd", 1)], [("kd", 0), ("kd", 1)], [("vd", 0), ("vd", 1)],
              []]
    filler += [[("d_scores", 0), ("d_scores", 1)], [("d_probs", 0)]]
    for k in range(1, 7):
        a += [("blk", k, t) for t in range(2)]
        a += [("inv_v", k, t) for t in range(2)]
        a += filler[k - 1]
        a += [("inv_u", k, t) for t in range(2)]
        if k < 6:
            a += [("inv_x", k, t) for t in range(2)]
    a += [("vnew", 0), ("d_pT", 0), ("d_probs", 1), ("d_scores", 2),
          ("state",), ("d_pT", 1), ("d_probs", 2), ("d_scores", 3), ("o", 0), ("d_pv", 0),
          ("kstate",), ("qstate",), ("d_pT", 2), ("d_probs", 3), ("d_scores", 4),
          ("vnew", 1), ("d_pT", 3), ("d_probs", 4), ("d_scores", 5), ("d_pv", 1), ("o", 1),
          ("onorm", 0), ("onorm", 1),
          ("d_pT", 4), ("d_probs", 5), ("d_scores", 6), ("d_pT", 5), ("d_probs", 6), ("d_scores", 7), ("d_pv", 2),
          ("oT", 0), ("oT", 1), ("d_pT", 6), ("d_probs", 7), ("d_pT", 7), ("d_pv", 3)]
    a += projected(0, 0) + cross_kv(0) + normed(0, 0) + cross(0) + projected(0, 1) + normed(0, 1)
    a += [("route", 0), ("route_soft", 0), ("route_top", 0), ("place", 0)]

    b = normed(0, 2)
    for half in range(2):
        b += [(kind, half, m) for kind in ("sc_c", "sc_h", "sc_b") for m in range(2)]
    b += projected(1, 0) + cross_kv(1) + normed(1, 0) + cross(1) + projected(1, 1) + normed(1, 1)
    b += [("route", 1), ("route_soft", 1), ("route_top", 1), ("place", 1)]

    c = [(kind, 1, 2, t) for t in range(2) for kind in ("ln_stats", "ln_rstd", "ln_norm", "ln_h")]
    c += [("store", t) for t in range(2)]
    return a, b, c


TAKES = {
    "masks": (POOL, DVE), "params": (PE, DVE), "ba": (PE, DVE), "gates": (DVE, ACT), "qkv": (PE, DVE, ACT),
    "sumsq": (POOL, PE, ACT), "cumsum": (PE, DVE), "cols": (DVE, ACT), "rowg": (PE, DVE, ACT), "rowh": (PE, DVE, ACT),
    "gram": (PE, DVE), "qk": (PE, DVE), "blk": (POOL,), "z": (PE, ACT), "inv0": (PE, DVE), "ktok": (PE, ACT),
    "vtok": (PE, ACT), "inv_v": (PE, ACT), "inv_u": (PE, DVE), "inv_x": (PE, DVE), "qd": (PE, ACT), "kd": (PE, ACT),
    "vd": (PE, DVE), "d_scores": (PE, DVE), "d_probs": (ACT, DVE), "d_pT": (PE, ACT), "d_pv": (PE, ACT),
    "vnew": (PE, ACT), "state": (PE, ACT), "kstate": (PE, DVE), "qstate": (PE, ACT), "o": (PE, DVE),
    "onorm": (ACT, DVE), "oT": (PE, DVE), "y": (PE, DVE), "ln_stats": (DVE,), "ln_rstd": (POOL,), "ln_norm": (DVE,),
    "ln_h": (POOL,), "xk": (PE, ACT), "xv": (PE, DVE), "xq": (PE, ACT), "xs": (PE, DVE, ACT), "xn": (DVE,), "xp": (PE, DVE),
    "xo": (PE, ACT), "route": (PE, DVE), "route_soft": (ACT, DVE), "route_top": (DVE,), "place": (PE, DVE),
    "sc_c": (PE, ACT), "sc_h": (PE, DVE), "sc_b": (PE, DVE), "store": (),
}
EMPTIES = {"qkv": DVE, "rowg": DVE, "rowh": DVE, "xs": ACT}


def takes(step):
    if step[0] in ("xT", "memT", "hT"):
        return (PE, ACT) if step[-1] == 0 else (PE, DVE)
    return TAKES[step[0]]


def empties(step):
    return EMPTIES.get(step[0]) or takes(step)[-1]


def trunk_kernel(nc, x, mem, ab_w_in, ab_conv_w, ab_a_log, ab_dt_bias, ab_norm_w, ab_w_out, sc_w_in, sc_conv_w,
                 sc_w_out, xa_w_q, xa_w_kv, xa_w_o, router_w, router_b, moe_w_gate, moe_w_up, moe_w_down,
                 ln_g, ln_b, out):
    _, T, D = x.shape
    NT = T // P
    KD = D // P
    DEPTH, E, _, F = moe_w_gate.shape
    NH = ab_a_log.shape[1]
    DH = ab_norm_w.shape[1]
    W = NH * DH
    NA = 8
    AH = W // NA
    XH = 4
    G = 4
    PAIRS = E // 2
    SLOTS = 64
    ALPHA = float((2 * DEPTH) ** 0.25)
    LN_EPS, RMS_EPS = 1e-5, 1e-6
    TAPS, STAPS = ab_conv_w.shape[1], sc_conv_w.shape[1]
    assert (T, D, DEPTH, E, F, NH, DH, NT) == (256, 1024, 2, 16, 512, 4, 128, 2)

    segments = trunk_steps()
    steps = [s for seg in segments for s in seg]
    count = {}
    totals = {e: 0 for e in (PE, ACT, DVE, POOL)}
    for s in steps:
        assert s not in count, s
        count[s] = {}
        for e in takes(s):
            totals[e] += 1
            count[s][e] = totals[e]
    bank_of, before = {}, {}
    for n, seg in enumerate(segments):
        filled = [s for s in seg if PE in takes(s)]
        for i, s in enumerate(filled):
            bank_of[s] = i % BANKS
            before[s] = filled[i - BANKS] if i >= BANKS else None
            if before[s] is None and n:
                before[s] = "experts"

    def cols(w, c0):
        return w[:, c0:c0 + BANK].rearrange("(k p) n -> p k n", p=P)

    XW = [xa_w_q[l] for l in range(DEPTH)]
    q0, z0, ba0, d0 = 0, 3 * W, 4 * W, 4 * W + 2 * NH
    slot_reader = {}
    stream = []

    def slot(src, *readers):
        for r in readers:
            slot_reader.setdefault(r, []).append(len(stream))
        stream.append((src, readers[-1]))

    def experts_slots(l):
        for _ in range(3 * E):
            stream.append(None)

    w_in = ab_w_in[0]
    slot(cols(w_in, 0), ("qkv", 0, 0), ("qkv", 0, 1))
    slot(cols(w_in, W), ("qkv", 1, 0), ("qkv", 1, 1))
    slot(cols(w_in, 2 * W), ("qkv", 2, 0), ("qkv", 2, 1))
    slot(cols(w_in, z0), ("z", 0), ("z", 1))
    slot(cols(w_in, d0), ("qd", 0), ("qd", 1))
    slot(cols(w_in, d0 + W), ("kd", 0), ("kd", 1))
    slot(cols(w_in, d0 + 2 * W), ("vd", 0), ("vd", 1))

    def out_slots(w, l, s):
        for half in range(2):
            slot(cols(w, half * BANK), ("y", l, s, half, 0), ("y", l, s, half, 1))

    def kv_slots(l):
        for m in range(2):
            slot(cols(xa_w_kv[l], m * BANK), ("xk", l, 2 * m), ("xk", l, 2 * m + 1))
        for half in range(2):
            slot(cols(xa_w_kv[l], D + half * BANK), ("xv", l, half, 0), ("xv", l, half, 1))

    def q_slots(l):
        for m in range(2):
            slot(cols(xa_w_q[l], m * BANK), ("xq", l, 2 * m), ("xq", l, 2 * m + 1))

    out_slots(ab_w_out[0], 0, 0)
    kv_slots(0)
    q_slots(0)
    out_slots(xa_w_o[0], 0, 1)
    first_expert_slot = [len(stream)]
    experts_slots(0)
    for half in range(2):
        for kind, part in (("sc_c", 1), ("sc_h", 2), ("sc_b", 0)):
            slot(cols(sc_w_in[0], part * D + half * BANK), (kind, half, 0), (kind, half, 1))
    out_slots(sc_w_out[0], 1, 0)
    kv_slots(1)
    q_slots(1)
    out_slots(xa_w_o[1], 1, 1)
    first_expert_slot.append(len(stream))
    experts_slots(1)
    RING = 6

    with ExitStack() as ctx:
        def sb(name, shape, dt=F32):
            return ctx.enter_context(nc.sbuf_tensor(name, shape, dt))

        def sem(name):
            return ctx.enter_context(nc.semaphore(name))

        ps = ctx.enter_context(nc.psum_tensor("ps", [P, BANKS, BANK], F32))

        ring = sb("ring", [P, RING, KD * BANK])
        h = sb("h", [P, NT, D])
        hn = sb("hn", [P, NT, D])
        hT = sb("hT", [P, KD, T])
        memT = sb("memT", [P, KD, T])
        gain = sb("gain", [P, 2, D])
        ident = sb("ident", [P, P])
        ones = sb("ones", [P, P])
        upto = sb("upto", [P, P])
        below = sb("below", [P, P])
        slot_no = sb("slot_no", [P, SLOTS])
        par_rows = sb("par_rows", [P, 2, P])
        par = sb("par", [P, 2, P])
        small = sb("small", [P, 16])
        wba = sb("wba", [P, KD, 2 * NH])
        wr = sb("wr", [P, KD, E])
        rb = sb("rb", [P, E])
        dtb = sb("dtb", [P, 2, NH])
        normw = sb("normw", [P, DH])
        ARENA = 15900
        arena = sb("arena", [P, ARENA])
        taken = [0]

        def carve(*shape, at=None):
            n = int(np.prod(shape))
            o = taken[0] if at is None else at
            taken[0] = max(taken[0], o + n)
            assert taken[0] <= ARENA, taken[0]
            v = arena[:, o:o + n]
            if len(shape) == 2:
                v = v.rearrange("p (a b) -> p a b", a=shape[0])
            if len(shape) == 3:
                v = v.rearrange("p (a b c) -> p a b c", a=shape[0], b=shape[1])
            return v

        qkv = carve(12, T)
        at_x = taken[0]
        X = carve(NT, NH, P)
        U = carve(NT, NH, P)
        sq = carve(8, T, at=at_x)
        st = carve(NH, P, at=at_x)
        r1 = carve(NH, P, at=at_x + NH * P)
        zs = carve(NT, W)
        qdT = carve(4, T)
        vd = carve(NT, W)
        ktok = carve(NH, P)
        vb = carve(NT, NH, P)
        DU = carve(NT, NH, P)
        DL = carve(NT, NH, P)
        at_b = taken[0]
        Bm = carve(NT, NH, P)
        o_sb = carve(NT, NH, P, at=at_b)
        at_v = taken[0]
        Vt = carve(NT, NH, P)
        tmpo = carve(NH, P, at=at_v)
        sqo = carve(NH, P, at=at_v + NH * P)
        vn = DL
        dp = [carve(384) for _ in range(2)]
        dpT = [carve(384) for _ in range(2)]
        ba = carve(NT, 2 * NH)
        beta = carve(NT, NH)
        ga, gb, graw, gcol, hcol, bk, rk, qs, eg, egq, nc1 = (carve(NT, NH) for _ in range(11))
        lss = carve(NT, 8)
        glast, kdec, ea = (carve(NH) for _ in range(3))
        rms = carve(NT, NH)
        dmx = [carve(2) for _ in range(2)]
        dden = [carve(2) for _ in range(2)]
        drec = [carve(2) for _ in range(2)]
        memtok = h0 = None
        kdz = gain.rearrange("p a b -> p (a b)").rearrange("p (a b) -> p a b", a=NA)
        catT = hn.rearrange("p a b -> p (a b)").rearrange("p (a b) -> p a b", a=KD)
        memtok = carve(NT, D, at=at_b)
        levels = sb("levels", [P, 7, P], BF16)
        times = sb("times", [P, 384], BF16)
        shut = sb("shut", [P, 384], BF16)
        shutU = dpT[0][:, 0:P]
        shutL = dpT[1][:, 0:P]
        di = carve(384, at=at_x).bitcast(I32)
        dj = carve(384, at=at_x + 384).bitcast(I32)
        df = carve(384, at=at_x + 768)
        dg = carve(384, at=at_x + 1152)

        taken_ab = taken[0]
        taken[0] = 0
        xkT = carve(KD, T)
        xv = carve(NT, D)
        lnb = carve(NT, 2, 6)
        lnm = carve(NT, 4)
        at_sc = taken[0]
        xqT = carve(KD, T)
        xoT = carve(KD, T)
        xpr = [carve(NT, T) for _ in range(2)]
        xpT = [carve(NT, T) for _ in range(2)]
        xmx = [carve(NT) for _ in range(2)]
        xden = [carve(NT) for _ in range(2)]
        xrec = [carve(NT) for _ in range(2)]
        sc_y = carve(KD, T, at=at_sc)
        sc_u = carve(4, T, at=at_sc + KD * T)
        sc_a = carve(4, T, at=at_sc + (KD + 4) * T)
        taken[0] = at_sc
        onehot = carve(NT, 2, SLOTS)
        gated = carve(NT, 2, SLOTS)
        gatedT = carve(T)
        xg = carve(D)
        xgT = carve(KD, P)
        silu = carve(F)
        hid = carve(F)
        hidT = carve(4, P)
        outp = carve(D)
        lg = carve(NT, E)
        sc = carve(NT, E)
        sel = carve(NT, E)
        gates = carve(NT, E)
        ta, tb, tc, oh1, posm = (carve(NT, E) for _ in range(5))
        hi, lo = carve(NT * G, 2), carve(NT * G, 2)
        g1, g2, g3, g4 = (carve(NT, G) for _ in range(4))
        s1, s2 = carve(NT), carve(NT)
        maxc = carve(4)
        gidx = sb("gidx", [P, NT, G])
        eidx = sb("eidx", [P, NT, E])
        rounds = sb("rounds", [P, 1], I32)
        nexp = sb("nexp", [P, 1])

        steps_sem = {PE: sem("pe_steps"), ACT: sem("act_steps"), DVE: sem("dve_steps"), POOL: sem("pool_steps")}
        dve_own, act_own, pool_own = sem("dve_own"), sem("act_own"), sem("pool_own")
        slot_full = [sem(f"slot_full{i}") for i in range(RING)]
        x_in, mem_in, rows_in, wba_in, vec_in, gain_in = (
            sem(n) for n in ("x_in", "mem_in", "rows_in", "wba_in", "vec_in", "gain_in"))
        decay_in = sem("decay_in")
        stored = sem("stored")
        ex_pe, ex_act, ex_dve = sem("ex_pe"), sem("ex_act"), sem("ex_dve")
        of = [{n: sem(f"of{l}_{n}") for n in ("slots", "pe", "act", "dve", "shift", "end")} for l in range(DEPTH)]

        def at(engine, step):
            return steps_sem[engine], count[step][engine]

        PE_PAIR, ACT_PAIR, DVE_PAIR = 14, 6, 10
        PE_ALL, ACT_ALL, DVE_ALL = PAIRS * PE_PAIR, PAIRS * ACT_PAIR, PAIRS * DVE_PAIR + 1

        def first(p):
            return isinstance(p, int) and p == 0

        def last(p):
            return isinstance(p, int) and p == PAIRS - 1

        def n_pe(l, kind, p):
            if kind in ("X0", "X1", "XT0", "XT1") and first(p):
                return l * PE_ALL + 1 + ("X0", "X1", "XT0", "XT1").index(kind)
            if kind in ("G", "U"):
                return l * PE_ALL + PE_PAIR * p + (4 if first(p) else 0) + (1 if kind == "G" else 2)
            if kind[0] == "Y":
                if last(p):
                    return l * PE_ALL + PE_ALL - 4 + 1 + int(kind[1])
                return l * PE_ALL + PE_PAIR * (p + 1) + 3 + int(kind[1])
            if kind[0] == "X":
                return l * PE_ALL + PE_PAIR * (p - 1) + {"X0": 7, "X1": 8, "XT0": 11, "XT1": 12}[kind]
            return (l * PE_ALL + PE_PAIR * p + {"HT": 9, "PT": 10, "O0": 13, "O1": 14}[kind]
                    - ({"HT": 2, "PT": 2, "O0": 4, "O1": 4}[kind] if last(p) else 0))

        def n_act(l, kind, p):
            if kind in ("X0", "XT0") and first(p):
                return l * ACT_ALL + 1 + ("X0", "XT0").index(kind)
            if kind in ("X0", "XT0"):
                return l * ACT_ALL + ACT_PAIR * (p - 1) + {"X0": 4, "XT0": 6}[kind]
            return (l * ACT_ALL + ACT_PAIR * p + {"silu": 3, "HT": 5, "O0": 7, "O1": 8}[kind]
                    - ({"silu": 0, "HT": 1, "O0": 2, "O1": 2}[kind] if last(p) else 0))

        def n_dve(l, kind, p):
            if first(p) and kind in ("onehot", "X1", "XT1", "scaled"):
                return l * DVE_ALL + 1 + ("onehot", "X1", "XT1", "scaled").index(kind)
            if kind in ("onehot", "X1", "XT1"):
                return l * DVE_ALL + DVE_PAIR * (p - 1) + {"onehot": 2, "X1": 8, "XT1": 10}[kind] + (
                    4 if kind == "onehot" and isinstance(p, int) and p == 1 else 0)
            if kind[0] == "Y":
                if last(p):
                    return l * DVE_ALL + DVE_ALL - 4 + 1 + int(kind[1])
                return (l * DVE_ALL + DVE_PAIR * (p + 1) + 4 + int(kind[1])
                        - (1 if isinstance(p, int) and p == PAIRS - 2 else 0))
            return (l * DVE_ALL + DVE_PAIR * p + {"gated": 1, "hid": 3, "PT": 9}[kind]
                    + (4 if first(p) and kind != "PT" else 0)
                    - ({"gated": 0, "hid": 1, "PT": 2}[kind] if last(p) else 0))

        BK = {"G": 0, "U": 1, "X0": 2, "X1": 3, "XT0": 2, "XT1": 3, "HT": 4, "PT": 5, "O0": 6, "O1": 7,
              "Y0": 4, "Y1": 5, "Y2": 6, "Y3": 7}

        def ring_at(l, part, j):
            return (first_expert_slot[l] + 2 * part + j) % RING

        def uses_before(l, part, j):
            return (first_expert_slot[l] + 2 * part + j) // RING

        def wide(v):
            return v.rearrange("p (k n) -> p k n", k=KD)

        def tall(v):
            return v.rearrange("p (k n) -> p k n", k=4)

        block = ctx.enter_context(nc.Block())

        @block.sync
        def _(sp):
            def expert_src(l, part, e):
                w = (moe_w_gate, moe_w_up, moe_w_down)[part]
                return w[l, e].rearrange("(k p) n -> p k n", p=P)

            def expert_dst(l, part, j):
                s = ring[:, ring_at(l, part, j), :]
                return tall(s) if part == 2 else wide(s)

            def load_pair(l, p, free):
                for part in range(3):
                    if free:
                        sp.wait_ge(ex_pe, n_pe(l, ("G", "U", "O1")[part], p - 1))
                    for j in range(2):
                        if not free:
                            sp.wait_ge(*at(PE, stream[first_expert_slot[l] + 2 * part + j - RING][1]))
                        sp.dma_start(expert_dst(l, part, j), expert_src(l, part, 2 * p + j)).then_inc(
                            slot_full[ring_at(l, part, j)], 16)

            def overflow(l):
                sp.wait_ge(*at(DVE, ("place", l)))
                nr = sp.value_load(rounds[0:1, 0:1], min_val=1, max_val=4)
                with sp.If(nr > 1):
                    sp.wait_ge(ex_pe, (l + 1) * PE_ALL)
                    with sp.Fori(1, nr) as b:
                        with sp.Fori(0, PAIRS) as p:
                            i = (b - 1) * PAIRS + p
                            sp.wait_ge(of[l]["dve"], i * 9 + 1)
                            for part in range(3):
                                for j in range(2):
                                    sp.dma_start(expert_dst(l, part, j), expert_src(l, part, 2 * p + j)).then_inc(
                                        of[l]["slots"], 16)
                    sp.wait_ge(of[l]["end"], 1)

            l = -1
            i = 0
            while i < len(stream):
                if stream[i] is None:
                    l += 1
                    load_pair(l, 0, False)
                    load_pair(l, 1, True)
                    with sp.Fori(2, PAIRS) as p:
                        load_pair(l, p, True)
                    overflow(l)
                    i += 3 * E
                    continue
                if i >= RING:
                    if stream[i - RING] is None:
                        j = i - RING - first_expert_slot[l]
                        part = (j % 6) // 2
                        sp.wait_ge(ex_pe, n_pe(l, ("G", "U", "O1")[part], PAIRS - 1))
                    else:
                        sp.wait_ge(*at(PE, stream[i - RING][1]))
                sp.dma_start(wide(ring[:, i % RING, :]), stream[i][0]).then_inc(slot_full[i % RING], 16)
                i += 1
            for t in range(NT):
                sp.wait_ge(*at(POOL, ("ln_h", 1, 2, t)))
                sp.dma_start(out[0].rearrange("(t p) d -> p t d", p=P)[:, t, :], h[:, t, :]).then_inc(stored, 16)
            sp.wait_ge(stored, 16 * NT)

        @block.gpsimd
        def _(pool):
            own = [0]

            def link(ins):
                own[0] += 1
                ins.then_inc(pool_own, 1)
                pool.wait_ge(pool_own, own[0])

            def done(ins):
                ins.then_inc(steps_sem[POOL], 1)

            pool.dma_start(memtok, mem[0].rearrange("(t p) d -> p t d", p=P)).then_inc(mem_in, 16)
            pool.dma_start(wr[:], router_w.rearrange("(k p) e -> p k e", p=P)).then_inc(vec_in, 16)
            pool.dma_start(rb[:], router_b.unsqueeze(0).to_broadcast([P, E])).then_inc(vec_in, 16)
            pool.dma_start(normw[:], ab_norm_w[0:1, :].to_broadcast([P, DH])).then_inc(vec_in, 16)
            for step in steps:
                if POOL not in takes(step):
                    continue
                kind = step[0]
                if kind == "masks":
                    nc.gpsimd.memset(ones[:], 1.0)
                    nc.gpsimd.memset(shutL, 0.0)
                    nc.gpsimd.memset(nexp[:], -0.5)
                    nc.gpsimd.iota(slot_no[:], [[1, SLOTS]], base=0, channel_multiplier=0,
                                   allow_small_or_imprecise_dtypes=True)
                    nc.gpsimd.iota(gidx[:], [[0, NT], [-1, G]], base=G, channel_multiplier=0,
                                   allow_small_or_imprecise_dtypes=True)
                    nc.gpsimd.iota(eidx[:], [[0, NT], [-1, E]], base=E, channel_multiplier=0,
                                   allow_small_or_imprecise_dtypes=True)
                    nc.gpsimd.iota(di[:, 0:P], [[0, P]], base=0, channel_multiplier=1)
                    nc.gpsimd.iota(dj[:, 0:2 * P], [[-1, 2 * P]], base=P, channel_multiplier=1)
                    link(nc.gpsimd.iota(dj[:, 2 * P:3 * P], [[-1, P]], base=0, channel_multiplier=1))
                    nc.gpsimd.affine_select(out=ident[:], in_=ones[:], compare_op=ALU.is_equal, fill=0.0, base=0,
                                            pattern=[[-1, P]], channel_multiplier=1)
                    nc.gpsimd.affine_select(out=upto[:], in_=ones[:], compare_op=ALU.is_ge, fill=0.0, base=0,
                                            pattern=[[1, P]], channel_multiplier=-1)
                    nc.gpsimd.affine_select(out=below[:], in_=ones[:], compare_op=ALU.is_gt, fill=0.0, base=0,
                                            pattern=[[1, P]], channel_multiplier=-1)
                    nc.gpsimd.affine_select(out=shutU, in_=shutL, compare_op=ALU.is_ge, fill=NEG, base=0,
                                            pattern=[[1, P]], channel_multiplier=-1)
                    link(nc.gpsimd.iota(di[:, P:2 * P], [[1, P]], base=0, channel_multiplier=0))
                    done(nc.gpsimd.affine_select(out=shutL, in_=shutL, compare_op=ALU.is_gt, fill=NEG, base=0,
                                                 pattern=[[-1, P]], channel_multiplier=1))
                elif kind == "sumsq":
                    pool.wait_ge(*at(DVE, ("masks",)))
                    pool.wait_ge(*at(ACT, ("qkv", 1, 1)))
                    for i in range(4):
                        v = sq[:, 2 * i:2 * i + 2, :]
                        ins = nc.gpsimd.tensor_tensor(v, qkv[:, 2 * i:2 * i + 2, :], qkv[:, 2 * i:2 * i + 2, :], ALU.mult)
                    done(ins)
                elif kind == "blk":
                    _, k, t = step
                    pool.wait_ge(*at(DVE, ("gram", t)))
                    if k == 0:
                        pool.wait_ge(mem_in, 16)
                        for tt in range(NT):
                            pool.wait_ge(*at(PE, ("memT", tt, 1)))
                    else:
                        pool.wait_ge(*at(PE, ("inv_v", k - 1, t) if k > 1 else ("inv0", t)))
                        pool.wait_ge(*at(DVE, ("inv0", t)))
                    done(nc.gpsimd.tensor_tensor(Bm[:, t], DL[:, t],
                                                 levels[:, k:k + 1, :].to_broadcast([P, NH, P]), ALU.mult))
                elif kind == "ln_rstd":
                    _, l, s, t = step
                    pool.wait_ge(*at(DVE, ("ln_stats", l, s, t)))
                    done(nc.gpsimd.tensor_tensor(lnm[:, t, 2:3], lnm[:, t, 3:4], nexp[:], ALU.pow))
                elif kind == "ln_h":
                    _, l, s, t = step
                    pool.wait_ge(*at(DVE, ("ln_norm", l, s, t)))
                    pool.wait_ge(gain_in, 32 * (3 * l + s + 1))
                    link(nc.gpsimd.tensor_tensor(h[:, t, :], hn[:, t, :], gain[:, 0, :], ALU.mult))
                    done(nc.gpsimd.tensor_tensor(h[:, t, :], h[:, t, :], gain[:, 1, :], ALU.add))
            assert own[0] < 4096

        @block.scalar
        def _(act):
            own = [0]

            def link(ins):
                own[0] += 1
                ins.then_inc(act_own, 1)
                act.wait_ge(act_own, own[0])

            def done(ins):
                ins.then_inc(steps_sem[ACT], 1)

            def gains(l, s):
                for i, w in enumerate((ln_g, ln_b)):
                    act.dma_start(gain[:, i, :], w[l, s:s + 1, :].to_broadcast([P, D])).then_inc(gain_in, 16)

            act.dma_start(h[:], x[0].rearrange("(t p) d -> p t d", p=P)).then_inc(x_in, 16)
            act.dma_start(wba[:], ab_w_in[0][:, ba0:ba0 + 2 * NH].rearrange("(k p) n -> p k n", p=P)).then_inc(wba_in, 16)
            act.dma_start(par_rows[0:TAPS * 12, 0, :],
                          ab_conv_w[0].rearrange("a (c p) -> (a c) p", p=P)).then_inc(rows_in, 16)
            act.dma_start(par_rows[48:48 + STAPS * KD, 0, :],
                          sc_conv_w[0].rearrange("a (c p) -> (a c) p", p=P)).then_inc(rows_in, 16)
            act.dma_start(par_rows[0:48, 1, :], ln_g.rearrange("l s (k p) -> (l s k) p", p=P)).then_inc(rows_in, 16)
            act.dma_start(par_rows[48:96, 1, :], ln_b.rearrange("l s (k p) -> (l s k) p", p=P)).then_inc(rows_in, 16)
            act.dma_start(dtb[:, 0, :], ab_dt_bias[0:1, :].to_broadcast([P, NH])).then_inc(decay_in, 16)
            act.dma_start(dtb[:, 1, :], ab_a_log[0:1, :].to_broadcast([P, NH])).then_inc(decay_in, 16)

            def experts(l):
                def gather_out(p):
                    act.wait_ge(ex_pe, n_pe(l, "X0", p))
                    nc.scalar.activation(xg[:, 0:BANK], ps[:, BK["X0"], :], ACTF.Copy).then_inc(ex_act, 1)

                def gatherT_out(p):
                    act.wait_ge(ex_pe, n_pe(l, "XT0", p))
                    for k in range(4):
                        ins = nc.scalar.activation(xgT[:, k, :], ps[:, BK["XT0"], k * P:(k + 1) * P], ACTF.Identity,
                                                   bias=bias_col(l, 1, k), scale=gain_col(l, 1, k))
                    ins.then_inc(ex_act, 1)

                def pair(p):
                    act.wait_ge(ex_pe, n_pe(l, "G", p))
                    if not first(p):
                        act.wait_ge(ex_dve, n_dve(l, "hid", p - 1))
                    nc.scalar.activation(silu, ps[:, BK["G"], :], ACTF.Silu).then_inc(ex_act, 1)
                    if not last(p):
                        gather_out(p + 1)
                    act.wait_ge(ex_pe, n_pe(l, "HT", p))
                    nc.scalar.activation(hidT, ps[:, BK["HT"], :].rearrange("p (a b) -> p a b", a=4),
                                         ACTF.Copy).then_inc(ex_act, 1)
                    if not last(p):
                        gatherT_out(p + 1)
                    for half in range(2):
                        act.wait_ge(ex_pe, n_pe(l, f"O{half}", p))
                        nc.scalar.activation(outp[:, half * BANK:(half + 1) * BANK], ps[:, BK[f"O{half}"], :],
                                             ACTF.Copy).then_inc(ex_act, 1)

                gather_out(0)
                gatherT_out(0)
                pair(0)
                with act.Fori(1, PAIRS - 1) as p:
                    pair(p)
                pair(PAIRS - 1)
                act.wait_ge(*at(DVE, ("place", l)))
                nr = act.value_load(rounds[0:1, 0:1], min_val=1, max_val=4)
                with act.If(nr > 1):
                    with act.Fori(1, nr) as b:
                        with act.Fori(0, PAIRS) as p:
                            act.wait_ge(of[l]["pe"], ((b - 1) * PAIRS + p) * 7 + 4)
                            nc.scalar.activation(silu, ps[:, BK["G"], :], ACTF.Silu).then_inc(of[l]["act"], 1)

            def gain_col(l, s, k):
                c = (3 * l + s) * KD + k
                return par[:, 1, c:c + 1]

            def bias_col(l, s, k):
                c = 48 + (3 * l + s) * KD + k
                return par[:, 1, c:c + 1]

            def psum(step):
                return ps[:, bank_of[step], :]

            for n, seg in enumerate(segments):
                if n:
                    experts(n - 1)
                for step in seg:
                    kind = step[0]
                    if ACT not in takes(step):
                        continue
                    if PE in takes(step):
                        act.wait_ge(*at(PE, step))
                    if kind in ("xT", "memT"):
                        _, t, g = step
                        dst = (hT if kind == "xT" else memT)[:, 4 * g:4 * g + 4, t * P:(t + 1) * P]
                        done(nc.scalar.activation(dst, psum(step).rearrange("p (a b) -> p a b", a=4), ACTF.Copy))
                    elif kind == "hT":
                        _, l, s, t, g = step
                        act.wait_ge(*at(DVE, ("params",)))
                        for k in range(4):
                            ins = nc.scalar.activation(hT[:, 4 * g + k, t * P:(t + 1) * P], psum(step)[:, k * P:(k + 1) * P],
                                                       ACTF.Identity, bias=bias_col(l, s, 4 * g + k),
                                                       scale=gain_col(l, s, 4 * g + k))
                        done(ins)
                    elif kind == "gates":
                        act.wait_ge(*at(DVE, ("ba",)))
                        nc.scalar.activation(beta, ba[:, :, 0:NH], ACTF.Exp, scale=-1.0)
                        nc.scalar.activation(ea, dtb[:, 1, :], ACTF.Exp)
                        link(nc.scalar.activation(ga, gb, ACTF.Exp, scale=-1.0))
                        done(nc.scalar.activation(ga, ga, ACTF.Ln, bias=ones[:, 0:1]))
                    elif kind == "qkv":
                        _, s, m = step
                        act.wait_ge(*at(DVE, step))
                        v = qkv[:, 4 * s + 2 * m:4 * s + 2 * m + 2, :]
                        done(nc.scalar.activation(v, v, ACTF.Silu))
                    elif kind == "sumsq":
                        done(nc.scalar.activation(lss, psum(step)[:, 0:NT * 8].rearrange("p (a b) -> p a b", a=NT),
                                                  ACTF.Ln, bias=small[:, 0:1]))
                    elif kind == "cols":
                        act.wait_ge(*at(DVE, ("cumsum",)))
                        act.wait_ge(*at(ACT, ("sumsq",)))
                        nc.scalar.activation(rk, lss[:, :, NH:2 * NH], ACTF.Exp, scale=-0.5)
                        nc.scalar.activation(qs, lss[:, :, 0:NH], ACTF.Exp, scale=-0.5)
                        done(nc.scalar.activation(eg, gcol, ACTF.Exp))
                    elif kind in ("rowg", "rowh"):
                        _, t = step
                        act.wait_ge(*at(DVE, step))
                        m, col = (DU, hcol) if kind == "rowg" else (DL, gcol)
                        for hd in range(NH):
                            ins = nc.scalar.activation(m[:, t, hd, :], m[:, t, hd, :], ACTF.Exp, bias=col[:, t, hd:hd + 1])
                        done(ins)
                    elif kind == "z":
                        done(nc.scalar.activation(zs[:, step[1], :], psum(step), ACTF.Silu))
                    elif kind == "ktok":
                        act.wait_ge(*at(DVE, ("rowg", 0)))
                        link(nc.scalar.activation(kdec, kdec, ACTF.Exp))
                        for hd in range(NH):
                            ins = nc.scalar.activation(ktok[:, hd, :], psum(step)[:, hd * P:(hd + 1) * P], ACTF.Copy,
                                                       scale=kdec[:, hd:hd + 1])
                        done(ins)
                    elif kind == "vtok":
                        _, t = step
                        act.wait_ge(*at(DVE, ("gates",)))
                        for hd in range(NH):
                            ins = nc.scalar.activation(vb[:, t, hd, :], psum(step)[:, hd * P:(hd + 1) * P], ACTF.Copy,
                                                       scale=beta[:, t, hd:hd + 1])
                        done(ins)
                    elif kind == "inv_v":
                        _, k, t = step
                        if k == 1:
                            for tt in range(NT):
                                act.wait_ge(*at(PE, ("memT", tt, 1)))
                        done(nc.scalar.activation(Vt[:, t], psum(step).rearrange("p (a b) -> p a b", a=NH), ACTF.Copy))
                    elif kind == "qd":
                        _, m = step
                        done(nc.scalar.activation(qdT[:, 2 * m:2 * m + 2, :], psum(step).rearrange("p (a b) -> p a b", a=2),
                                                  ACTF.Copy, scale=float(AH) ** -0.5))
                    elif kind == "kd":
                        _, m = step
                        act.wait_ge(*at(DVE, ("masks",)))
                        src = psum(step).rearrange("p (a b) -> p a b", a=2)
                        nc.scalar.activation(kdz[0:AH, 4 * m:4 * m + 4:2, :], src[0:AH], ACTF.Copy)
                        done(nc.scalar.activation(kdz[AH:P, 4 * m + 1:4 * m + 4:2, :], src[AH:P], ACTF.Copy))
                    elif kind == "d_probs":
                        _, hd = step
                        act.wait_ge(*at(DVE, ("d_scores", hd)))
                        b = hd % 2
                        nc.scalar.activation(dp[b][:, 0:2 * P], dp[b][:, 0:2 * P], ACTF.Exp, bias=dmx[b][:, 1:2])
                        done(nc.scalar.activation(dp[b][:, 2 * P:3 * P], dp[b][:, 2 * P:3 * P], ACTF.Exp, bias=dmx[b][:, 0:1]))
                    elif kind == "d_pT":
                        _, hd = step
                        if hd >= 2:
                            act.wait_ge(*at(PE, ("d_pv", (hd - 2) // 2)))
                        done(nc.scalar.activation(dpT[hd % 2][:, :], psum(step)[:, 0:3 * P], ACTF.Copy))
                    elif kind == "d_pv":
                        _, hp = step
                        ins = nc.scalar.activation(catT[:, NH + hp, :], psum(step)[:, 0:T], ACTF.Copy)
                        done(ins)
                        if hp == 3:
                            act.wait_ge(*at(PE, ("d_scores", NA - 1)))
                            gains(0, 0)
                    elif kind == "vnew":
                        _, c = step
                        done(nc.scalar.activation(vn[:, c], psum(step).rearrange("p (a b) -> p a b", a=NH), ACTF.Copy))
                    elif kind == "state":
                        done(nc.scalar.activation(st, psum(step).rearrange("p (a b) -> p a b", a=NH), ACTF.Copy))
                    elif kind == "qstate":
                        act.wait_ge(*at(DVE, ("cols",)))
                        act.wait_ge(*at(PE, ("inv_x", 5, 1)))
                        act.wait_ge(*at(PE, ("inv_u", 6, 1)))
                        for hd in range(NH):
                            ins = nc.scalar.activation(tmpo[:, hd, :], psum(step)[:, hd * P:(hd + 1) * P], ACTF.Copy,
                                                       scale=egq[:, 1, hd:hd + 1])
                        done(ins)
                    elif kind == "onorm":
                        _, c = step
                        act.wait_ge(*at(DVE, ("o", c)))
                        if c == 0:
                            act.wait_ge(*at(DVE, ("o", 1)))
                        for hd in range(NH):
                            ins = nc.scalar.activation(sqo[:, hd, :], o_sb[:, c, hd, :], ACTF.Square,
                                                       accum_out=rms[:, c, hd:hd + 1])
                        link(ins)
                        link(nc.scalar.activation(rms[:, c, :], rms[:, c, :], ACTF.Ln, scale=1.0 / DH, bias=small[:, 0:1]))
                        done(nc.scalar.activation(rms[:, c, :], rms[:, c, :], ACTF.Exp, scale=-0.5))
                    elif kind == "xk":
                        _, l, m = step
                        done(nc.scalar.activation(xkT[:, 2 * m:2 * m + 2, :], psum(step).rearrange("p (a b) -> p a b", a=2),
                                                  ACTF.Copy))
                    elif kind == "xq":
                        _, l, m = step
                        done(nc.scalar.activation(xqT[:, 2 * m:2 * m + 2, :], psum(step).rearrange("p (a b) -> p a b", a=2),
                                                  ACTF.Copy, scale=float(D // XH) ** -0.5))
                    elif kind == "xs":
                        _, l, hd = step
                        act.wait_ge(*at(DVE, step))
                        b = hd % 2
                        if hd >= 2:
                            act.wait_ge(*at(PE, ("xp", l, hd - 2)))
                        for t in range(NT):
                            ins = nc.scalar.activation(xpr[b][:, t, :], psum(step)[:, t * T:(t + 1) * T], ACTF.Exp,
                                                       bias=xmx[b][:, t:t + 1], accum_out=xden[b][:, t:t + 1])
                        done(ins)
                    elif kind == "xo":
                        _, l, hd = step
                        done(nc.scalar.activation(xoT[:, 2 * hd:2 * hd + 2, :], psum(step).rearrange("p (a b) -> p a b", a=2),
                                                  ACTF.Copy))
                        if hd == 0:
                            for t in range(NT):
                                act.wait_ge(*at(POOL, ("ln_h", l, 0, t)))
                            gains(l, 1)
                    elif kind == "route_soft":
                        _, l = step
                        act.wait_ge(*at(DVE, ("route", l)))
                        done(nc.scalar.activation(sc, lg, ACTF.Exp))
                        for t in range(NT):
                            act.wait_ge(*at(POOL, ("ln_h", l, 1, t)))
                        gains(l, 2)
                    elif kind == "sc_c":
                        _, half, m = step
                        if half:
                            act.wait_ge(*at(DVE, ("sc_h", 0, 1)))
                        if (half, m) == (0, 0):
                            for t in range(NT):
                                act.wait_ge(*at(DVE, ("hT", 0, 2, t, 1)))
                        done(nc.scalar.activation(sc_u[:, 2 * m:2 * m + 2, :], psum(step).rearrange("p (a b) -> p a b", a=2),
                                                  ACTF.Copy))
                        if (half, m) == (1, 1):
                            for t in range(NT):
                                act.wait_ge(*at(POOL, ("ln_h", 0, 2, t)))
                            gains(1, 0)
                    else:
                        raise AssertionError(kind)

        @block.vector
        def _(dve):
            own = [0]
            V = nc.vector

            def link(ins):
                own[0] += 1
                ins.then_inc(dve_own, 1)
                dve.wait_ge(dve_own, own[0])

            def done(ins):
                ins.then_inc(steps_sem[DVE], 1)

            def gain_col(l, s, k):
                c = (3 * l + s) * KD + k
                return par[:, 1, c:c + 1]

            def bias_col(l, s, k):
                c = 48 + (3 * l + s) * KD + k
                return par[:, 1, c:c + 1]

            def psum(step):
                return ps[:, bank_of[step], :]

            def over_slots(v):
                return v.unsqueeze(3).to_broadcast([P, NT, 2, SLOTS])

            def slots_over():
                return slot_no[:].unsqueeze(1).unsqueeze(1).to_broadcast([P, NT, 2, SLOTS])

            def build_onehot(p):
                return V.tensor_tensor(onehot, slots_over(), over_slots(posm[:, :, bass.ds(2 * p, 2)]), ALU.is_equal)

            def gathered_cols(l, bank, k0):
                for k in range(4):
                    ins = V.tensor_scalar(xgT[:, k0 + k, :], ps[:, bank, k * P:(k + 1) * P],
                                          gain_col(l, 1, k0 + k), bias_col(l, 1, k0 + k), ALU.mult, ALU.add)
                return ins

            def experts(l):
                def gather_out(p):
                    dve.wait_ge(ex_pe, n_pe(l, "X1", p))
                    V.tensor_copy(xg[:, BANK:D], ps[:, BK["X1"], :]).then_inc(ex_dve, 1)

                def gatherT_out(p):
                    dve.wait_ge(ex_pe, n_pe(l, "XT1", p))
                    gathered_cols(l, BK["XT1"], 4).then_inc(ex_dve, 1)

                def add_out(p):
                    for i in range(4):
                        t, half = i // 2, i % 2
                        dve.wait_ge(ex_pe, n_pe(l, f"Y{i}", p))
                        hv = h[:, t, half * BANK:(half + 1) * BANK]
                        V.tensor_tensor(hv, hv, ps[:, BK[f"Y{i}"], :], ALU.add).then_inc(ex_dve, 1)

                def pair(p):
                    if not first(p):
                        dve.wait_ge(ex_pe, n_pe(l, "PT", p - 1))
                    dve.wait_ge(ex_dve, n_dve(l, "onehot", p))
                    V.tensor_tensor(gated, onehot, over_slots(gates[:, :, bass.ds(2 * p, 2)]),
                                    ALU.mult).then_inc(ex_dve, 1)
                    if not last(p):
                        dve.wait_ge(ex_dve, n_dve(l, "gated", p))
                        dve.wait_ge(ex_pe, n_pe(l, "X1", p))
                        build_onehot(p + 1).then_inc(ex_dve, 1)
                    dve.wait_ge(ex_act, n_act(l, "silu", p))
                    dve.wait_ge(ex_pe, n_pe(l, "U", p))
                    V.tensor_tensor(hid, silu, ps[:, BK["U"], :], ALU.mult).then_inc(ex_dve, 1)
                    if not first(p):
                        add_out(p - 1)
                    if not last(p):
                        gather_out(p + 1)
                    dve.wait_ge(ex_pe, n_pe(l, "PT", p))
                    V.tensor_copy(gatedT, ps[:, BK["PT"], 0:T]).then_inc(ex_dve, 1)
                    if not last(p):
                        gatherT_out(p + 1)

                build_onehot(0).then_inc(ex_dve, 1)
                gather_out(0)
                gatherT_out(0)
                for t in range(NT):
                    dve.wait_ge(*at(POOL, ("ln_h", l, 1, t)))
                V.tensor_scalar(h[:], h[:], ALPHA, None, ALU.mult).then_inc(ex_dve, 1)
                dve.wait_ge(ex_dve, n_dve(l, "scaled", 0))
                pair(0)
                with dve.Fori(1, PAIRS - 1) as p:
                    pair(p)
                pair(PAIRS - 1)
                add_out(PAIRS - 1)
                dve.wait_ge(ex_dve, (l + 1) * DVE_ALL)

                nr = dve.value_load(rounds[0:1, 0:1], min_val=1, max_val=4)
                with dve.If(nr > 1):
                    o = of[l]
                    V.memset(maxc[:, 1:2], 0.0).then_inc(o["dve"], 1)
                    with dve.Fori(1, nr) as b:
                        V.tensor_scalar(posm, posm, float(-SLOTS), None, ALU.add).then_inc(o["shift"], 1)
                        with dve.Fori(0, PAIRS) as p:
                            i = (b - 1) * PAIRS + p
                            n_o, n_p = i * 9 + 1, i * 7
                            dve.wait_ge(o["shift"], b)
                            build_onehot(p)
                            V.tensor_tensor(gated, slots_over(), over_slots(posm[:, :, bass.ds(2 * p, 2)]),
                                            ALU.is_equal).then_inc(o["dve"], 1)
                            dve.wait_ge(o["dve"], n_o + 1)
                            V.tensor_tensor(gated, gated, over_slots(gates[:, :, bass.ds(2 * p, 2)]),
                                            ALU.mult).then_inc(o["dve"], 1)
                            dve.wait_ge(o["pe"], n_p + 1)
                            V.tensor_copy(xg.rearrange("p (a b) -> p a b", a=2), ps[:, 2:4, :]).then_inc(o["dve"], 1)
                            dve.wait_ge(o["pe"], n_p + 2)
                            gathered_cols(l, BK["XT0"], 0)
                            gathered_cols(l, BK["XT1"], 4).then_inc(o["dve"], 1)
                            dve.wait_ge(o["pe"], n_p + 3)
                            V.tensor_copy(gatedT, ps[:, BK["PT"], 0:T]).then_inc(o["dve"], 1)
                            dve.wait_ge(o["act"], i + 1)
                            dve.wait_ge(o["pe"], n_p + 4)
                            V.tensor_tensor(hid, silu, ps[:, BK["U"], :], ALU.mult).then_inc(o["dve"], 1)
                            dve.wait_ge(o["pe"], n_p + 5)
                            V.tensor_copy(hidT, ps[:, BK["HT"], :].rearrange("p (a b) -> p a b", a=4)).then_inc(o["dve"], 1)
                            dve.wait_ge(o["pe"], n_p + 6)
                            V.tensor_copy(outp.rearrange("p (a b) -> p a b", a=2), ps[:, 6:8, :]).then_inc(o["dve"], 1)
                            dve.wait_ge(o["pe"], n_p + 7)
                            for t in range(NT):
                                ins = V.tensor_tensor(h[:, t, :].rearrange("p (a b) -> p a b", a=2),
                                                      h[:, t, :].rearrange("p (a b) -> p a b", a=2), ps[:, 4 + 2 * t:6 + 2 * t, :], ALU.add)
                            ins.then_inc(o["dve"], 1)
                    V.memset(maxc[:, 0:1], 0.0).then_inc(o["end"], 1)

            for n, seg in enumerate(segments):
                if n:
                    experts(n - 1)
                for step in seg:
                    if DVE not in takes(step):
                        continue
                    kind = step[0]
                    if PE in takes(step):
                        dve.wait_ge(*at(PE, step))
                    if kind == "masks":
                        V.memset(small[:, 0:1], RMS_EPS)
                        V.memset(gain[:], 0.0)
                        dve.wait_ge(*at(POOL, step))
                        link(V.tensor_tensor(di[:, 0:P], di[:, 0:P], di[:, P:2 * P], ALU.bitwise_xor))
                        for k in range(7):
                            link(V.tensor_scalar(di[:, P:2 * P], di[:, 0:P], k, None, ALU.logical_shift_right))
                            link(V.tensor_scalar(levels[:, k, :], di[:, P:2 * P], 1, None, ALU.is_equal))
                        link(V.tensor_scalar(di[:, :], dj[:, :], 3, None, ALU.bitwise_and))
                        link(V.tensor_scalar(df, di[:, :], 0, None, ALU.is_equal))
                        link(V.tensor_scalar(di[:, :], dj[:, :], 15, None, ALU.bitwise_and))
                        link(V.tensor_scalar(dg, di[:, :], 0, None, ALU.is_equal))
                        link(V.tensor_tensor(df, df, dg, ALU.add))
                        link(V.tensor_scalar(dg, dj[:, :], P, None, ALU.is_le))
                        link(V.tensor_tensor(df, df, dg, ALU.add))
                        link(V.tensor_scalar(dg, dj[:, :], 0, None, ALU.is_ge))
                        link(V.tensor_tensor(df, df, dg, ALU.mult))
                        V.tensor_copy(times[:], df)
                        done(V.tensor_scalar(shut[:], df, 0.0, NEG, ALU.is_equal, ALU.mult))
                    elif kind == "params":
                        V.tensor_copy(par[:, 0, 0:72], psum(step)[:, 0:72])
                        done(V.tensor_copy(par[:, 1, 0:96], psum(step)[:, P:P + 96]))
                    elif kind in ("xT", "memT"):
                        _, t, g = step
                        dst = (hT if kind == "xT" else memT)[:, 4 * g:4 * g + 4, t * P:(t + 1) * P]
                        done(V.tensor_copy(dst, psum(step).rearrange("p (a b) -> p a b", a=4)))
                    elif kind == "hT":
                        _, l, s, t, g = step
                        for k in range(4):
                            ins = V.tensor_scalar(hT[:, 4 * g + k, t * P:(t + 1) * P], psum(step)[:, k * P:(k + 1) * P],
                                                  gain_col(l, s, 4 * g + k), bias_col(l, s, 4 * g + k), ALU.mult, ALU.add)
                        done(ins)
                    elif kind == "ba":
                        link(V.tensor_copy(ba, psum(step)[:, 0:NT * 2 * NH].rearrange("p (a b) -> p a b", a=NT)))
                        dve.wait_ge(decay_in, 32)
                        link(V.tensor_tensor(ba[:, :, NH:], ba[:, :, NH:], dtb[:, 0:1, :].to_broadcast([P, NT, NH]), ALU.add))
                        done(V.scalar_tensor_tensor(gb, ba[:, :, NH:], -1.0, ba[:, :, NH:], ALU.mult, ALU.max))
                    elif kind == "gates":
                        dve.wait_ge(*at(ACT, step))
                        link(V.tensor_scalar(beta, beta, 1.0, None, ALU.add))
                        V.reciprocal(beta, beta)
                        link(V.scalar_tensor_tensor(gb, ba[:, :, NH:], 0.0, ga, ALU.max, ALU.add))
                        done(V.scalar_tensor_tensor(graw, gb, -1.0, ea.unsqueeze(1).to_broadcast([P, NT, NH]),
                                                    ALU.mult, ALU.mult))
                    elif kind == "qkv":
                        _, s, m = step
                        dve.wait_ge(*at(DVE, ("params",)))
                        for i in range(2):
                            c = 4 * s + 2 * m + i
                            src, dst = psum(step)[:, i * T:(i + 1) * T], qkv[:, c, :]

                            def tap(k):
                                return par[:, 0, k * 12 + c:k * 12 + c + 1]
                            link(V.tensor_scalar(dst, src, tap(TAPS - 1), None, ALU.mult))
                            for k in range(1, TAPS):
                                ins = V.scalar_tensor_tensor(dst[:, k:], src[:, :T - k], tap(TAPS - 1 - k), dst[:, k:],
                                                             ALU.mult, ALU.add)
                                if k < TAPS - 1 or i == 0:
                                    link(ins)
                        done(ins)
                    elif kind == "cumsum":
                        done(V.tensor_copy(gcol, psum(step)[:, 0:NT * NH].rearrange("p (a b) -> p a b", a=NT)))
                    elif kind == "cols":
                        dve.wait_ge(*at(ACT, step))
                        dve.wait_ge(*at(DVE, ("cumsum",)))
                        V.scalar_tensor_tensor(hcol, lss[:, :, NH:2 * NH], -0.5, gcol, ALU.mult, ALU.subtract)
                        link(V.tensor_scalar(qs, qs, float(DH) ** -0.5, None, ALU.mult))
                        link(V.tensor_tensor(bk, beta, rk, ALU.mult))
                        V.scalar_tensor_tensor(nc1, bk, -1.0, eg, ALU.mult, ALU.mult)
                        done(V.tensor_tensor(egq, eg, qs, ALU.mult))
                    elif kind == "rowg":
                        _, t = step
                        if t == 0:
                            link(V.tensor_copy(glast, psum(step)[:, P - 1:NH * P:P]))
                            dve.wait_ge(*at(DVE, ("cols",)))
                            V.tensor_tensor(kdec, glast, hcol[:, 0, :], ALU.add)
                        done(V.tensor_tensor(DU[:, t], psum(step).rearrange("p (a b) -> p a b", a=NH),
                                             shutU.unsqueeze(1).to_broadcast([P, NH, P]), ALU.add))
                    elif kind == "rowh":
                        _, t = step
                        done(V.tensor_tensor(DL[:, t], psum(step).rearrange("p (a b) -> p a b", a=NH),
                                             shutL.unsqueeze(1).to_broadcast([P, NH, P]), ALU.add))
                    elif kind == "gram":
                        _, t = step
                        dve.wait_ge(*at(ACT, ("rowh", t)))
                        for hd in range(NH):
                            ins = V.scalar_tensor_tensor(DL[:, t, hd, :], psum(step)[:, hd * P:(hd + 1) * P],
                                                         bk[:, t, hd:hd + 1], DL[:, t, hd, :], ALU.mult, ALU.mult)
                        done(ins)
                    elif kind == "qk":
                        _, t = step
                        dve.wait_ge(*at(ACT, ("rowg", t)))
                        done(V.tensor_tensor(DU[:, t], psum(step).rearrange("p (a b) -> p a b", a=NH), DU[:, t], ALU.mult))
                    elif kind == "inv0":
                        _, t = step
                        dve.wait_ge(*at(PE, ("sumsq",)))
                        dve.wait_ge(*at(POOL, ("blk", 0, t)))
                        eye = ident[:].unsqueeze(1).to_broadcast([P, NH, P])
                        V.scalar_tensor_tensor(X[:, t], Bm[:, t], -1.0, eye, ALU.mult, ALU.add)
                        done(V.scalar_tensor_tensor(U[:, t], psum(step).rearrange("p (a b) -> p a b", a=NH), -1.0, eye,
                                                    ALU.mult, ALU.add))
                    elif kind in ("inv_u", "inv_x"):
                        _, k, t = step
                        m = U if kind == "inv_u" else X
                        prev = ("inv0", t) if k == 1 else (kind, k - 1, t)
                        dve.wait_ge(*at(DVE, prev))
                        done(V.tensor_tensor(m[:, t], m[:, t], psum(step).rearrange("p (a b) -> p a b", a=NH), ALU.subtract))
                    elif kind == "vd":
                        done(V.tensor_copy(vd[:, step[1], :], psum(step)))
                    elif kind == "d_scores":
                        _, hd = step
                        b = hd % 2
                        dve.wait_ge(*at(DVE, ("masks",)))
                        if hd >= 2:
                            dve.wait_ge(*at(PE, ("d_pT", hd - 2)))
                        link(V.tensor_tensor(dp[b][:, :], psum(step)[:, 0:3 * P], shut[:], ALU.add))
                        V.tensor_reduce(dmx[b][:, 1:2], dp[b][:, 0:2 * P], AX, ALU.max, negate=True)
                        done(V.tensor_reduce(dmx[b][:, 0:1], dp[b][:, 2 * P:3 * P], AX, ALU.max, negate=True))
                    elif kind == "d_probs":
                        _, hd = step
                        b = hd % 2
                        dve.wait_ge(*at(ACT, step))
                        v1, v0 = dp[b][:, 0:2 * P], dp[b][:, 2 * P:3 * P]
                        V.scalar_tensor_tensor(v1, v1, 1.0, times[:, 0:2 * P], ALU.mult, ALU.mult, accum_out=dden[b][:, 1:2])
                        link(V.scalar_tensor_tensor(v0, v0, 1.0, times[:, 2 * P:3 * P], ALU.mult, ALU.mult,
                                                    accum_out=dden[b][:, 0:1]))
                        link(V.reciprocal(drec[b], dden[b]))
                        V.tensor_scalar(v1, v1, drec[b][:, 1:2], None, ALU.mult)
                        done(V.tensor_scalar(v0, v0, drec[b][:, 0:1], None, ALU.mult))
                    elif kind == "kstate":
                        dve.wait_ge(*at(ACT, ("vtok", 1)))
                        for hd in range(NH):
                            ins = V.scalar_tensor_tensor(r1[:, hd, :], psum(step)[:, hd * P:(hd + 1) * P],
                                                         nc1[:, 1, hd:hd + 1], vb[:, 1, hd, :], ALU.mult, ALU.add)
                        done(ins)
                    elif kind == "o":
                        _, c = step
                        if c:
                            dve.wait_ge(*at(ACT, ("qstate",)))
                        else:
                            for t in range(NT):
                                dve.wait_ge(*at(PE, ("inv_v", 6, t)))
                        for hd in range(NH):
                            src, scale = psum(step)[:, hd * P:(hd + 1) * P], qs[:, c, hd:hd + 1]
                            if c:
                                ins = V.scalar_tensor_tensor(o_sb[:, c, hd, :], src, scale, tmpo[:, hd, :], ALU.mult, ALU.add)
                            else:
                                ins = V.tensor_scalar(o_sb[:, c, hd, :], src, scale, None, ALU.mult)
                        done(ins)
                    elif kind == "onorm":
                        _, c = step
                        dve.wait_ge(*at(ACT, ("z", c)))
                        if c == 0:
                            dve.wait_ge(vec_in, 48)
                        zv = zs[:, c, :].rearrange("p (a b) -> p a b", a=NH)
                        link(V.tensor_tensor(zv, zv, normw[:].unsqueeze(1).to_broadcast([P, NH, DH]), ALU.mult))
                        dve.wait_ge(*at(ACT, step))
                        for hd in range(NH):
                            ins = V.scalar_tensor_tensor(o_sb[:, c, hd, :], o_sb[:, c, hd, :], rms[:, c, hd:hd + 1],
                                                         zv[:, hd, :], ALU.mult, ALU.mult)
                        done(ins)
                    elif kind == "oT":
                        _, t = step
                        done(V.tensor_copy(catT[:, 0:NH, t * P:(t + 1) * P], psum(step).rearrange("p (a b) -> p a b", a=NH)))
                    elif kind == "y":
                        _, l, s, half, t = step
                        if (l, s) != (0, 0):
                            dve.wait_ge(*at(POOL, ("ln_h", l, s - 1, t) if s else ("ln_h", l - 1, 2, t)))
                        hv = h[:, t, half * BANK:(half + 1) * BANK]
                        link(V.scalar_tensor_tensor(hv, hv, ALPHA, psum(step), ALU.mult, ALU.add))
                        done(V.bn_stats(lnb[:, t, half, :], hv))
                    elif kind == "ln_stats":
                        _, l, s, t = step
                        if s == 2:
                            V.bn_stats(lnb[:, t, 0, :], h[:, t, 0:BANK])
                            link(V.bn_stats(lnb[:, t, 1, :], h[:, t, BANK:D]))
                        else:
                            dve.wait_ge(*at(DVE, ("y", l, s, 1, t)))
                        link(V.bn_aggr(lnm[:, t, 0:2], lnb[:, t].rearrange("p a b -> p (a b)")))
                        done(V.tensor_scalar(lnm[:, t, 3:4], lnm[:, t, 1:2], LN_EPS, None, ALU.add))
                    elif kind == "ln_norm":
                        _, l, s, t = step
                        dve.wait_ge(*at(POOL, ("ln_rstd", l, s, t)))
                        if (l, s) == (0, 0):
                            dve.wait_ge(*at(PE, ("y", 0, 0, 1, 1)))
                        done(V.tensor_scalar(hn[:, t, :], h[:, t, :], lnm[:, t, 0:1], lnm[:, t, 2:3], ALU.subtract, ALU.mult))
                    elif kind == "xv":
                        _, l, half, t = step
                        done(V.tensor_copy(xv[:, t, half * BANK:(half + 1) * BANK], psum(step)))
                    elif kind == "xs":
                        _, l, hd = step
                        if hd >= 2:
                            dve.wait_ge(*at(ACT, ("xs", l, hd - 2)))
                        done(V.tensor_reduce(xmx[hd % 2], psum(step).rearrange("p (a b) -> p a b", a=NT), AX, ALU.max,
                                             negate=True))
                    elif kind == "xn":
                        _, l, hd = step
                        b = hd % 2
                        dve.wait_ge(*at(ACT, ("xs", l, hd)))
                        link(V.reciprocal(xrec[b], xden[b]))
                        V.tensor_scalar(xpr[b][:, 0, :], xpr[b][:, 0, :], xrec[b][:, 0:1], None, ALU.mult)
                        done(V.tensor_scalar(xpr[b][:, 1, :], xpr[b][:, 1, :], xrec[b][:, 1:2], None, ALU.mult))
                    elif kind == "xp":
                        _, l, hd = step
                        b = hd % 2
                        if hd >= 2:
                            dve.wait_ge(*at(PE, ("xo", l, hd - 2)))
                        done(V.tensor_copy(xpT[b], psum(step).rearrange("p (a b) -> p a b", a=NT)))
                    elif kind == "route":
                        _, l = step
                        link(V.tensor_copy(lg, psum(step)[:, 0:NT * E].rearrange("p (a b) -> p a b", a=NT)))
                        link(V.tensor_reduce(s1, lg, AX, ALU.max))
                        done(V.tensor_tensor(lg, lg, s1.unsqueeze(2).to_broadcast([P, NT, E]), ALU.subtract))
                    elif kind == "route_soft":
                        dve.wait_ge(*at(ACT, step))
                        link(V.tensor_reduce(s1, sc, AX, ALU.add))
                        link(V.reciprocal(s2, s1))
                        link(V.tensor_tensor(sc, sc, s2.unsqueeze(2).to_broadcast([P, NT, E]), ALU.mult))
                        dve.wait_ge(vec_in, 48)
                        done(V.tensor_tensor(sel, sc, rb[:].unsqueeze(1).to_broadcast([P, NT, E]), ALU.add))
                    elif kind == "route_top":
                        _, l = step
                        dve.wait_ge(*at(DVE, ("route_soft", l)))
                        four = sel.rearrange("p t (g a b) -> p (t g) a b", g=G, b=2)
                        V.tensor_tensor(hi, four[:, :, :, 0], four[:, :, :, 1], ALU.max)
                        link(V.tensor_tensor(lo, four[:, :, :, 0], four[:, :, :, 1], ALU.min))
                        fl = lambda v: v.rearrange("p a b -> p (a b)")
                        V.tensor_tensor(fl(g1), hi[:, :, 0], hi[:, :, 1], ALU.max)
                        V.tensor_tensor(fl(g2), hi[:, :, 0], hi[:, :, 1], ALU.min)
                        link(V.tensor_tensor(fl(g3), lo[:, :, 0], lo[:, :, 1], ALU.max))
                        link(V.tensor_tensor(g2, g2, g3, ALU.max))
                        link(V.tensor_tensor(g1, g1, g2, ALU.add))

                        def first_max(mark, v, weights, n, top, tmp):
                            link(V.tensor_reduce(top, v, AX, ALU.max))
                            link(V.tensor_tensor(tmp, v, top.unsqueeze(2).to_broadcast([P, NT, n]), ALU.is_equal))
                            link(V.tensor_tensor(tmp, tmp, weights, ALU.mult))
                            link(V.tensor_reduce(top, tmp, AX, ALU.max))
                            link(V.tensor_tensor(mark, tmp, top.unsqueeze(2).to_broadcast([P, NT, n]), ALU.is_equal))

                        first_max(g4, g1, gidx[:], G, s1, g3)
                        inside = fl(g4).unsqueeze(2).to_broadcast([P, NT * G, E // G])
                        by4 = lambda v: v.rearrange("p t (g a) -> p (t g) a", g=G)
                        link(V.tensor_tensor(by4(ta), by4(sel), inside, ALU.mult))
                        link(V.tensor_scalar(g3, g4, 1.0, -NEG, ALU.subtract, ALU.mult))
                        link(V.tensor_tensor(by4(ta), by4(ta), fl(g3).unsqueeze(2).to_broadcast([P, NT * G, E // G]), ALU.add))
                        first_max(oh1, ta, eidx[:], E, s1, tb)
                        link(V.scalar_tensor_tensor(ta, oh1, NEG, ta, ALU.mult, ALU.add))
                        first_max(tc, ta, eidx[:], E, s1, tb)
                        link(V.tensor_tensor(oh1, oh1, tc, ALU.add))
                        link(V.tensor_tensor(tb, sc, oh1, ALU.mult))
                        link(V.tensor_reduce(s1, tb, AX, ALU.add))
                        link(V.reciprocal(s2, s1))
                        done(V.tensor_tensor(gates, tb, s2.unsqueeze(2).to_broadcast([P, NT, E]), ALU.mult))
                    elif kind == "place":
                        _, l = step
                        pv = psum(step)[:, 0:NT * E].rearrange("p (a b) -> p a b", a=NT)
                        link(V.scalar_tensor_tensor(posm, pv, 1.0, oh1, ALU.add, ALU.mult))
                        V.tensor_scalar(posm, posm, 1.0, None, ALU.subtract)
                        link(V.tensor_reduce(maxc[:, 0:1], psum(step)[:, NT * E:(NT + 1) * E], AX, ALU.max))
                        for i in range(1, 4):
                            ins = V.tensor_scalar(maxc[:, i:i + 1], maxc[:, 0:1], float(i * SLOTS), None, ALU.is_gt)
                        link(ins)
                        link(V.tensor_reduce(maxc[:, 0:1], maxc[:, 1:4], AX, ALU.add))
                        done(V.tensor_scalar(rounds[:], maxc[:, 0:1], 1.0, None, ALU.add))
                    elif kind == "sc_h":
                        _, half, m = step
                        dve.wait_ge(*at(ACT, ("sc_c", half, m)))
                        u = sc_u[:, 2 * m:2 * m + 2, :]
                        link(V.tensor_tensor(u, u, psum(step).rearrange("p (a b) -> p a b", a=2), ALU.mult))
                        for i in range(2):
                            c = 2 * m + i

                            def tap(k):
                                return par[:, 0, 48 + k * KD + 4 * half + c:48 + k * KD + 4 * half + c + 1]
                            src, dst = sc_u[:, c, :], sc_a[:, c, :]
                            link(V.tensor_scalar(dst, src, tap(STAPS - 1), None, ALU.mult))
                            for k in range(1, STAPS):
                                ins = V.scalar_tensor_tensor(dst[:, k:], src[:, :T - k], tap(STAPS - 1 - k), dst[:, k:],
                                                             ALU.mult, ALU.add)
                                if k < STAPS - 1 or i == 0:
                                    link(ins)
                        done(ins)
                    elif kind == "sc_b":
                        _, half, m = step
                        dve.wait_ge(*at(DVE, ("sc_h", half, m)))
                        done(V.tensor_tensor(sc_y[:, 4 * half + 2 * m:4 * half + 2 * m + 2, :],
                                             psum(step).rearrange("p (a b) -> p a b", a=2),
                                             sc_a[:, 2 * m:2 * m + 2, :], ALU.mult))
                    else:
                        raise AssertionError(kind)

        @block.tensor
        def _(pe):
            M = nc.tensor.matmul

            def done(ins):
                ins.then_inc(steps_sem[PE], 1)

            def arrived(step):
                for n in slot_reader[step]:
                    pe.wait_ge(slot_full[n % RING], 16 * (n // RING + 1))
                return wide(ring[:, slot_reader[step][-1] % RING, :])

            def chain(dst, pairs):
                for i, (a, b) in enumerate(pairs):
                    ins = M(dst, a, b, start=i == 0, stop=i == len(pairs) - 1)
                return ins

            def heads(dst, stationary, moving):
                for hd in range(NH):
                    ins = M(dst[:, hd * P:(hd + 1) * P], stationary(hd), moving(hd), start=True, stop=True)
                return ins

            def transposes(dst, srcs):
                for i, src in enumerate(srcs):
                    ins = nc.tensor.transpose(dst[:, i * P:(i + 1) * P], src, ident[:])
                return ins

            def by_feature(step, m, lhs, rhs):
                w = arrived(step)
                b = ps[:, bank_of[step], :]
                for i in range(2):
                    c = (2 * (m % 2) + i) * P
                    ins = chain(b[:, i * T:(i + 1) * T], [(w[:, k, c:c + P], rhs[:, k, :]) for k in range(KD)])
                done(ins)

            def by_token(step, src, t):
                w = arrived(step)
                done(chain(ps[:, bank_of[step], :], [(src[:, k, t * P:(t + 1) * P], w[:, k, :]) for k in range(KD)]))

            def have_hT(l, s):
                for t in range(NT):
                    pe.wait_ge(*at(ACT, ("hT", l, s, t, 0)))
                    pe.wait_ge(*at(DVE, ("hT", l, s, t, 1)))

            def slot_of(l, part, j):
                s = ring[:, ring_at(l, part, j), :]
                return tall(s) if part == 2 else wide(s)

            def gather(half, ):
                return chain(ps[:, BK[f"X{half}"], :],
                             [(onehot[:, t].rearrange("p a b -> p (a b)"), hn[:, t, half * BANK:(half + 1) * BANK])
                              for t in range(NT)])

            def gather_T(half):
                return transposes(ps[:, BK[f"XT{half}"], :],
                                  [xg[:, (4 * half + k) * P:(4 * half + k + 1) * P] for k in range(4)])

            def up_product(l, part):
                b = ps[:, BK["GU"[part]], :]
                for k in range(KD):
                    for j in range(2):
                        r = slice(j * SLOTS, (j + 1) * SLOTS)
                        ins = M(b[r, :], xgT[:, k, r], slot_of(l, part, j)[:, k, :], start=k == 0, stop=k == KD - 1)
                return ins

            def down_product(l, half):
                b = ps[:, BK[f"O{half}"], :]
                for k in range(4):
                    for j in range(2):
                        r = slice(j * SLOTS, (j + 1) * SLOTS)
                        ins = M(b[r, :], hidT[:, k, r], slot_of(l, 2, j)[:, k, half * BANK:(half + 1) * BANK],
                                start=k == 0, stop=k == 3)
                return ins

            def hidden_T():
                return transposes(ps[:, BK["HT"], :], [hid[:, k * P:(k + 1) * P] for k in range(4)])

            def gated_T():
                return transposes(ps[:, BK["PT"], :], [gated[:, t].rearrange("p a b -> p (a b)") for t in range(NT)])

            def scatter(i):
                t, half = i // 2, i % 2
                return M(ps[:, BK[f"Y{i}"], :], gatedT[:, t * P:(t + 1) * P], outp[:, half * BANK:(half + 1) * BANK],
                         start=True, stop=True)

            def experts(l):
                def weights(p, part):
                    for j in range(2):
                        pe.wait_ge(slot_full[ring_at(l, part, j)], 16 * (p + (uses_before(l, part, j) + 1)))

                def gathered(p):
                    pe.wait_ge(ex_dve, n_dve(l, "onehot", p))
                    if not first(p):
                        pe.wait_ge(ex_act, n_act(l, "XT0", p - 1))
                        pe.wait_ge(ex_dve, n_dve(l, "XT1", p - 1))
                    gather(0).then_inc(ex_pe, 1)
                    gather(1).then_inc(ex_pe, 1)

                def gathered_T(p):
                    pe.wait_ge(ex_act, n_act(l, "X0", p))
                    pe.wait_ge(ex_dve, n_dve(l, "X1", p))
                    gather_T(0).then_inc(ex_pe, 1)
                    gather_T(1).then_inc(ex_pe, 1)

                def scattered(p):
                    pe.wait_ge(ex_act, n_act(l, "O1", p))
                    pe.wait_ge(ex_dve, n_dve(l, "PT", p))
                    for i in range(4):
                        scatter(i).then_inc(ex_pe, 1)

                def pair(p):
                    pe.wait_ge(ex_act, n_act(l, "XT0", p))
                    pe.wait_ge(ex_dve, n_dve(l, "XT1", p))
                    weights(p, 0)
                    up_product(l, 0).then_inc(ex_pe, 1)
                    weights(p, 1)
                    up_product(l, 1).then_inc(ex_pe, 1)
                    if not first(p):
                        scattered(p - 1)
                    if not last(p):
                        gathered(p + 1)
                    pe.wait_ge(ex_dve, n_dve(l, "hid", p))
                    if not first(p):
                        pe.wait_ge(ex_dve, n_dve(l, "Y0", p - 1))
                    hidden_T().then_inc(ex_pe, 1)
                    if not first(p):
                        pe.wait_ge(ex_dve, n_dve(l, "Y1", p - 1))
                    gated_T().then_inc(ex_pe, 1)
                    if not last(p):
                        gathered_T(p + 1)
                    pe.wait_ge(ex_act, n_act(l, "HT", p))
                    weights(p, 2)
                    for half in range(2):
                        if not first(p):
                            pe.wait_ge(ex_dve, n_dve(l, f"Y{2 + half}", p - 1))
                        down_product(l, half).then_inc(ex_pe, 1)

                for s in segments[l][-12:]:
                    if PE in takes(s):
                        pe.wait_ge(*at(empties(s), s))
                gathered(0)
                gathered_T(0)
                pair(0)
                with pe.Fori(1, PAIRS - 1) as p:
                    pair(p)
                pair(PAIRS - 1)
                scattered(PAIRS - 1)
                pe.wait_ge(*at(DVE, ("place", l)))
                nr = pe.value_load(rounds[0:1, 0:1], min_val=1, max_val=4)
                with pe.If(nr > 1):
                    o = of[l]
                    pe.wait_ge(ex_dve, (l + 1) * DVE_ALL)
                    with pe.Fori(1, nr) as b:
                        with pe.Fori(0, PAIRS) as p:
                            i = (b - 1) * PAIRS + p
                            n_d = i * 9 + 1
                            pe.wait_ge(o["dve"], n_d + 2)
                            gather(0)
                            gather(1).then_inc(o["pe"], 1)
                            pe.wait_ge(o["dve"], n_d + 3)
                            gather_T(0)
                            gather_T(1).then_inc(o["pe"], 1)
                            pe.wait_ge(o["dve"], n_d + 4)
                            gated_T().then_inc(o["pe"], 1)
                            pe.wait_ge(o["dve"], n_d + 5)
                            pe.wait_ge(o["slots"], (i + 1) * 96)
                            up_product(l, 0)
                            up_product(l, 1).then_inc(o["pe"], 1)
                            pe.wait_ge(o["dve"], n_d + 6)
                            hidden_T().then_inc(o["pe"], 1)
                            pe.wait_ge(o["dve"], n_d + 7)
                            down_product(l, 0)
                            down_product(l, 1).then_inc(o["pe"], 1)
                            pe.wait_ge(o["dve"], n_d + 8)
                            for k in range(4):
                                ins = scatter(k)
                            ins.then_inc(o["pe"], 1)

            for n, seg in enumerate(segments):
                if n:
                    experts(n - 1)
                for step in seg:
                    if PE not in takes(step):
                        continue
                    kind = step[0]
                    b = ps[:, bank_of[step], :]
                    prev = before[step]
                    if prev == "experts":
                        pass
                    elif prev is not None:
                        pe.wait_ge(*at(empties(prev), prev))
                    if kind == "params":
                        pe.wait_ge(*at(POOL, ("masks",)))
                        pe.wait_ge(rows_in, 64)
                        rows = TAPS * 12 + STAPS * KD
                        nc.tensor.transpose(b[:, 0:rows], par_rows[0:rows, 0, :], ident[0:rows, 0:rows])
                        done(nc.tensor.transpose(b[:, P:P + 96], par_rows[0:96, 1, :], ident[0:96, 0:96]))
                    elif kind == "xT":
                        _, t, g = step
                        pe.wait_ge(x_in, 16)
                        done(transposes(b, [h[:, t, (4 * g + k) * P:(4 * g + k + 1) * P] for k in range(4)]))
                    elif kind == "memT":
                        _, t, g = step
                        pe.wait_ge(mem_in, 16)
                        done(transposes(b, [memtok[:, t, (4 * g + k) * P:(4 * g + k + 1) * P] for k in range(4)]))
                    elif kind == "ba":
                        pe.wait_ge(wba_in, 16)
                        for t in range(NT):
                            pe.wait_ge(*at(ACT, ("xT", t, 0)))
                            pe.wait_ge(*at(DVE, ("xT", t, 1)))
                        for t in range(NT):
                            ins = chain(b[:, t * 2 * NH:(t + 1) * 2 * NH],
                                        [(hT[:, k, t * P:(t + 1) * P], wba[:, k, :]) for k in range(KD)])
                        done(ins)
                    elif kind == "qkv":
                        by_feature(step, step[2], None, hT)
                    elif kind in ("qd", "kd"):
                        by_feature(step, step[1], None, hT)
                    elif kind in ("z", "vd"):
                        by_token(step, hT, step[1])
                    elif kind == "sumsq":
                        pe.wait_ge(*at(POOL, step))
                        for t in range(NT):
                            for i in range(8):
                                ins = M(b[:, 8 * t + i:8 * t + i + 1], sq[:, i, t * P:(t + 1) * P], ones[:, 0:1],
                                        start=True, stop=True)
                        done(ins)
                    elif kind == "cumsum":
                        pe.wait_ge(*at(DVE, ("gates",)))
                        done(M(b[:, 0:NT * NH], upto[:], graw.rearrange("p a b -> p (a b)"), start=True, stop=True))
                    elif kind == "rowg":
                        t = step[1]
                        done(heads(b, lambda hd: graw[:, t, hd:hd + 1].to_broadcast([P, P]), lambda hd: upto[:]))
                    elif kind == "rowh":
                        t = step[1]
                        pe.wait_ge(*at(DVE, ("cols",)))
                        done(heads(b, lambda hd: hcol[:, t, hd:hd + 1].to_broadcast([P, P]), lambda hd: ident[:]))
                    elif kind == "gram":
                        t = step[1]
                        kv = lambda hd: qkv[:, NH + hd, t * P:(t + 1) * P]
                        done(heads(b, kv, kv))
                    elif kind == "qk":
                        t = step[1]
                        done(heads(b, lambda hd: qkv[:, NH + hd, t * P:(t + 1) * P],
                                   lambda hd: qkv[:, hd, t * P:(t + 1) * P]))
                    elif kind == "inv0":
                        t = step[1]
                        pe.wait_ge(*at(POOL, ("blk", 0, t)))
                        done(transposes(b, [Bm[:, t, hd, :] for hd in range(NH)]))
                    elif kind == "ktok":
                        done(transposes(b, [qkv[:, NH + hd, 0:P] for hd in range(NH)]))
                    elif kind == "vtok":
                        t = step[1]
                        pe.wait_ge(*at(ACT, ("qkv", 2, 1)))
                        done(transposes(b, [qkv[:, 2 * NH + hd, t * P:(t + 1) * P] for hd in range(NH)]))
                    elif kind == "inv_v":
                        _, k, t = step
                        pe.wait_ge(*at(POOL, ("blk", k, t)))
                        pe.wait_ge(*at(DVE, ("inv0", t) if k == 1 else ("inv_u", k - 1, t)))
                        done(heads(b, lambda hd: Bm[:, t, hd, :], lambda hd: U[:, t, hd, :]))
                    elif kind == "inv_u":
                        _, k, t = step
                        pe.wait_ge(*at(ACT, ("inv_v", k, t)))
                        pe.wait_ge(*at(DVE, ("inv0", t) if k == 1 else ("inv_x", k - 1, t)))
                        done(heads(b, lambda hd: X[:, t, hd, :], lambda hd: Vt[:, t, hd, :]))
                    elif kind == "inv_x":
                        _, k, t = step
                        done(heads(b, lambda hd: Vt[:, t, hd, :], lambda hd: X[:, t, hd, :]))
                    elif kind == "vnew":
                        _, c = step
                        pe.wait_ge(*at(DVE, ("inv_u", 6, c)))
                        if c:
                            pe.wait_ge(*at(DVE, ("kstate",)))
                        else:
                            pe.wait_ge(*at(ACT, ("vtok", 0)))
                        rhs = r1 if c else vb[:, 0]
                        done(heads(b, lambda hd: U[:, c, hd, :], lambda hd: rhs[:, hd, :]))
                    elif kind == "state":
                        pe.wait_ge(*at(ACT, ("vnew", 0)))
                        done(heads(b, lambda hd: ktok[:, hd, :], lambda hd: vn[:, 0, hd, :]))
                    elif kind == "kstate":
                        pe.wait_ge(*at(ACT, ("state",)))
                        done(heads(b, lambda hd: qkv[:, NH + hd, P:T], lambda hd: st[:, hd, :]))
                    elif kind == "qstate":
                        done(heads(b, lambda hd: qkv[:, hd, P:T], lambda hd: st[:, hd, :]))
                    elif kind == "o":
                        c = step[1]
                        pe.wait_ge(*at(ACT, ("vnew", c)))
                        pe.wait_ge(*at(DVE, ("qk", c)))
                        done(heads(b, lambda hd: DU[:, c, hd, :], lambda hd: vn[:, c, hd, :]))
                    elif kind == "oT":
                        t = step[1]
                        pe.wait_ge(*at(DVE, ("onorm", t)))
                        done(transposes(b, [o_sb[:, t, hd, :] for hd in range(NH)]))
                    elif kind == "d_scores":
                        hd = step[1]
                        m = hd // 4
                        pe.wait_ge(*at(ACT, ("qd", m)))
                        pe.wait_ge(*at(ACT, ("kd", m)))
                        M(b[:, 0:T], qdT[:, hd // 2, P:T], kdz[:, hd, :], start=True, stop=True)
                        done(M(b[:, T:T + P], qdT[:, hd // 2, 0:P], kdz[:, hd, 0:P], start=True, stop=True))
                    elif kind == "d_pT":
                        hd = step[1]
                        pe.wait_ge(*at(DVE, ("d_probs", hd)))
                        v = dp[hd % 2]
                        done(transposes(b, [v[:, 2 * P:3 * P], v[:, 0:P], v[:, P:2 * P]]))
                    elif kind == "d_pv":
                        hp = step[1]
                        for j in range(2):
                            hd = 2 * hp + j
                            pe.wait_ge(*at(ACT, ("d_pT", hd)))
                            if hp == 0:
                                pe.wait_ge(*at(DVE, ("vd", j)))
                            r = slice(j * AH, (j + 1) * AH)
                            M(b[r, 0:T], vd[:, 0, hd * AH:(hd + 1) * AH], dpT[j][:, 0:T], start=True, stop=False)
                            ins = M(b[r, P:T], vd[:, 1, hd * AH:(hd + 1) * AH], dpT[j][:, T:T + P], start=False, stop=True)
                        done(ins)
                    elif kind == "y":
                        _, l, s, half, t = step
                        if (l, s) == (0, 0):
                            src = catT
                            for tt in range(NT):
                                pe.wait_ge(*at(DVE, ("oT", tt)))
                            pe.wait_ge(*at(ACT, ("d_pv", 3)))
                        elif s == 0:
                            src = sc_y
                            pe.wait_ge(*at(DVE, ("sc_b", 1, 1)))
                        else:
                            src = xoT
                            pe.wait_ge(*at(ACT, ("xo", l, XH - 1)))
                        by_token(step, src, t)
                    elif kind == "hT":
                        _, l, s, t, g = step
                        pe.wait_ge(*at(DVE, ("ln_norm", l, s, t)))
                        done(transposes(b, [hn[:, t, (4 * g + k) * P:(4 * g + k + 1) * P] for k in range(4)]))
                    elif kind == "xk":
                        for t in range(NT):
                            pe.wait_ge(*at(ACT, ("memT", t, 0)))
                            pe.wait_ge(*at(DVE, ("memT", t, 1)))
                        by_feature(step, step[2], None, memT)
                    elif kind == "xv":
                        by_token(step, memT, step[3])
                    elif kind == "xq":
                        have_hT(step[1], 0)
                        by_feature(step, step[2], None, hT)
                    elif kind == "xs":
                        _, l, hd = step
                        pe.wait_ge(*at(ACT, ("xk", l, hd)))
                        pe.wait_ge(*at(ACT, ("xq", l, hd)))
                        for t in range(NT):
                            ins = chain(b[:, t * T:(t + 1) * T],
                                        [(xqT[:, 2 * hd + i, t * P:(t + 1) * P], xkT[:, 2 * hd + i, :]) for i in range(2)])
                        done(ins)
                    elif kind == "xp":
                        _, l, hd = step
                        pe.wait_ge(*at(DVE, ("xn", l, hd)))
                        v = xpr[hd % 2]
                        done(transposes(b, [v[:, t, mt * P:(mt + 1) * P] for mt in range(NT) for t in range(NT)]))
                    elif kind == "xo":
                        _, l, hd = step
                        pe.wait_ge(*at(DVE, ("xp", l, hd)))
                        for half in range(2):
                            for t in range(NT):
                                pe.wait_ge(*at(DVE, ("xv", l, half, t)))
                        for i in range(2):
                            c = (2 * hd + i) * P
                            ins = chain(b[:, i * T:(i + 1) * T],
                                        [(xv[:, mt, c:c + P], xpT[hd % 2][:, mt, :]) for mt in range(NT)])
                        done(ins)
                    elif kind == "route":
                        l = step[1]
                        have_hT(l, 1)
                        pe.wait_ge(vec_in, 48)
                        for t in range(NT):
                            ins = chain(b[:, t * E:(t + 1) * E], [(hT[:, k, t * P:(t + 1) * P], wr[:, k, :]) for k in range(KD)])
                        done(ins)
                    elif kind == "place":
                        pe.wait_ge(*at(DVE, ("route_top", step[1])))
                        M(b[:, 0:E], below[:], oh1[:, 0, :], start=True, stop=True)
                        chain(b[:, E:2 * E], [(below[:], oh1[:, 1, :]), (ones[:], oh1[:, 0, :])])
                        done(chain(b[:, 2 * E:3 * E], [(ones[:], oh1[:, 0, :]), (ones[:], oh1[:, 1, :])]))
                    elif kind in ("sc_c", "sc_h", "sc_b"):
                        have_hT(0, 2)
                        by_feature(step, step[2], None, hT)
                    else:
                        raise AssertionError(kind)


_INS = ["x", "mem", "ab_w_in", "ab_conv_w", "ab_a_log", "ab_dt_bias", "ab_norm_w", "ab_w_out", "sc_w_in", "sc_conv_w",
        "sc_w_out", "xa_w_q", "xa_w_kv", "xa_w_o", "router_w", "router_b", "moe_w_gate", "moe_w_up", "moe_w_down",
        "ln_g", "ln_b"]


def kernel(**inputs):
    import concourse.bacc as bacc
    from concourse.bass_utils import run_bass_kernel_spmd

    nc = bacc.Bacc("TRN2", target_bir_lowering=False, num_devices=1)
    arrays, args = {}, []
    for name in _INS:
        a = np.ascontiguousarray(inputs[name])
        arrays[f"in_{name}"] = a
        args.append(nc.dram_tensor(f"in_{name}", a.shape, mybir.dt.from_np(a.dtype), kind="ExternalInput").ap())
    shape = inputs["x"].shape
    result = nc.dram_tensor("out_h", shape, F32, kind="ExternalOutput").ap()
    trunk_kernel(nc, *args, result)
    r = run_bass_kernel_spmd(nc, [arrays], core_ids=[0])
    return r.results[0]["out_h"]
```

```python
from contextlib import ExitStack

import numpy as np

import concourse.bass as bass
from concourse import mybir

F32 = mybir.dt.float32
BF16 = mybir.dt.bfloat16
I32 = mybir.dt.int32
ALU = mybir.AluOpType
ACTF = mybir.ActivationFunctionType
AX = mybir.AxisListType.X

P = 128
PE, ACT, DVE, POOL = "pe", "act", "dve", "pool"
BANKS = 8
BANK = 512
NEG = -1.0e30


def trunk_steps():
    def transposed(kind, *who):
        return [(kind, *who, t, g) for t in range(2) for g in range(2)]

    def normed(l, s):
        out = []
        for t in range(2):
            out += [("ln_stats", l, s, t), ("ln_rstd", l, s, t), ("ln_norm", l, s, t)]
        for t in range(2):
            out += [("hT", l, s, t, g) for g in range(2)]
        return out + [("ln_h", l, s, t) for t in range(2)]

    def cross_kv(l):
        return ([("xk", l, m) for m in range(4)] + [("xv", l, half, t) for half in range(2) for t in range(2)])

    def cross(l):
        return [("xq", l, 0), ("xq", l, 1), ("xs", l, 0), ("xq", l, 2), ("xn", l, 0), ("xs", l, 1), ("xp", l, 0),
                ("xq", l, 3), ("xo", l, 0), ("xn", l, 1), ("xs", l, 2), ("xp", l, 1), ("xs", l, 3), ("xo", l, 1),
                ("xn", l, 2), ("xp", l, 2), ("y_first", l, 1, 0, 0), ("xn", l, 3), ("xo", l, 2), ("xp", l, 3),
                ("y_first", l, 1, 1, 0), ("xo", l, 3)]

    def projected(l, s):
        return [("y", l, s, half, t) for half in range(2) for t in range(2)]

    def projected_normed(l, s, *between):
        def ln(t):
            return [("ln_stats", l, s, t), ("ln_rstd", l, s, t), ("ln_norm", l, s, t)]

        def hT(t):
            return [("hT", l, s, t, g) for g in range(2)]
        return ([("y", l, s, 0, 0), ("y", l, s, 1, 0)] + ln(0) + [("y", l, s, 0, 1)] + hT(0) + [("y", l, s, 1, 1)] + ln(1)
                + list(between) + hT(1) + [("ln_h", l, s, t) for t in range(2)])

    a = [("ident",)] + transposed("xT") + [("masks",), ("params",), ("qkv", 0, 0), ("ba",), ("gates",), ("levels",), ("qkv", 0, 1), ("qkv", 1, 0), ("qkv", 1, 1), ("qkv", 2, 0), ("cumsum",),
          ("qkv", 2, 1), ("qd", 0), ("sumsq",), ("cols",), ("qd", 1)]
    a += [("rowg", t) for t in range(2)] + [("rowh", t) for t in range(2)]
    a += [("gram", t) for t in range(2)] + [("qk", t) for t in range(2)]
    a += transposed("memT")
    a += [("blk", 0, t) for t in range(2)]
    a += [("kd", 0)]
    a += [("inv0", t) for t in range(2)] + [("ktok",)] + [("vtok", t) for t in range(2)]
    heads = [[("kd", 1), ("d_scores", 0)],
             [("d_probs", 0), ("d_scores", 1), ("vd", 0)],
             [("d_pT", 0), ("d_probs", 1), ("d_scores", 2), ("vd", 1)],
             [("d_pT", 1), ("d_probs", 2), ("d_scores", 3), ("d_pv", 0)],
             [("d_pT", 2), ("d_probs", 3), ("d_scores", 4)],
             [("d_pT", 3), ("d_probs", 4), ("d_scores", 5), ("d_pv", 1)]]
    for k in range(1, 7):
        a += [("blk", k, t) for t in range(2)]
        a += [("inv_v", k, t) for t in range(2)]
        a += heads[k - 1]
        a += [("inv_u", k, t) for t in range(2)]
        if k < 6:
            a += [("inv_x", k, t) for t in range(2)]
    a += [("d_pT", 4), ("d_probs", 5), ("d_scores", 6), ("vnew", 0), ("state",), ("o", 0), ("kstate",), ("qstate",),
          ("d_pT", 5), ("d_probs", 6), ("osq", 0), ("z", 0), ("d_pv", 2), ("d_scores", 7), ("vnew", 1), ("d_pT", 6),
          ("o", 1), ("d_probs", 7), ("onorm", 0), ("osq", 1), ("z", 1), ("oT", 0), ("d_pT", 7), ("y_first", 0, 0, 0, 0),
          ("onorm", 1), ("d_pv", 3), ("y_first", 0, 0, 0, 1), ("oT", 1)]
    ln, kv = normed(0, 0), cross_kv(0)
    a += projected(0, 0) + ln[:6] + kv[:-1] + ln[6:] + kv[-1:] + cross(0)
    a += projected_normed(0, 1, ("xk", 1, 0)) + [("route", 0), ("route_t", 0), ("route_soft", 0), ("xk", 1, 1),
                                                 ("route_top", 0), ("weights", 0), ("place", 0)]

    ln = normed(0, 2)
    b = ln[:6] + [("xk", 1, 2)] + ln[6:] + [("xk", 1, 3)]
    for half in range(2):
        b += [(kind, half, m) for kind in ("sc_c", "sc_h", "sc_b") for m in range(2)]
    b += [("xv", 1, 0, 0), ("xv", 1, 0, 1)] + projected_normed(1, 0, ("xv", 1, 1, 0)) + [("xv", 1, 1, 1)]
    b += cross(1) + projected_normed(1, 1)
    b += [(kind, 1) for kind in ("route", "route_t", "route_soft", "route_top", "weights", "place")]

    c = [(kind, 1, 2, t) for kind in ("ln_stats", "ln_rstd") for t in range(2)] + [("last", t) for t in range(2)]
    return a, b, c


TAKES = {
    "ident": (POOL,), "masks": (POOL,), "levels": (DVE,), "last": (DVE,), "params": (PE, DVE), "ba": (PE, DVE), "gates": (DVE, ACT), "qkv": (PE, DVE, ACT),
    "sumsq": (POOL, PE, ACT), "cumsum": (PE, DVE), "cols": (DVE, ACT), "rowg": (PE, DVE, ACT), "rowh": (PE, DVE, ACT),
    "gram": (PE, DVE), "qk": (PE, DVE), "blk": (POOL,), "z": (PE, ACT), "inv0": (PE, DVE), "ktok": (PE, ACT),
    "vtok": (PE, ACT), "inv_v": (PE, ACT), "inv_u": (PE, DVE), "inv_x": (PE, DVE), "qd": (PE, ACT), "kd": (PE, ACT),
    "vd": (PE, DVE), "d_scores": (PE, DVE), "d_probs": (ACT, DVE), "d_pT": (PE, ACT), "d_pv": (PE, ACT),
    "vnew": (PE, ACT), "state": (PE, ACT), "kstate": (PE, DVE), "qstate": (PE, ACT), "o": (PE, DVE),
    "osq": (ACT,), "onorm": (DVE,), "oT": (PE, DVE), "y_first": (PE,), "y": (PE, DVE), "ln_stats": (DVE,), "ln_rstd": (POOL,), "ln_norm": (DVE,),
    "ln_h": (POOL,), "xk": (PE, ACT), "xv": (PE, DVE), "xq": (PE, ACT), "xs": (PE, DVE, ACT), "xn": (DVE,), "xp": (PE, DVE),
    "xo": (PE, ACT), "route": (PE, DVE), "route_t": (PE, DVE), "weights": (DVE,), "route_soft": (ACT, DVE), "route_top": (DVE,), "place": (PE, DVE),
    "sc_c": (PE, ACT), "sc_h": (PE, DVE), "sc_b": (PE, DVE),
}
EMPTIES = {"qkv": DVE, "rowg": DVE, "rowh": DVE, "xs": ACT}


def takes(step):
    if step[0] in ("xT", "memT", "hT"):
        return (PE, ACT) if step[-1] == 0 else (PE, DVE)
    return TAKES[step[0]]


def empties(step):
    return EMPTIES.get(step[0]) or takes(step)[-1]


def trunk_kernel(nc, x, mem, ab_w_in, ab_conv_w, ab_a_log, ab_dt_bias, ab_norm_w, ab_w_out, sc_w_in, sc_conv_w,
                 sc_w_out, xa_w_q, xa_w_kv, xa_w_o, router_w, router_b, moe_w_gate, moe_w_up, moe_w_down,
                 ln_g, ln_b, out):
    _, T, D = x.shape
    NT = T // P
    KD = D // P
    DEPTH, E, _, F = moe_w_gate.shape
    NH = ab_a_log.shape[1]
    DH = ab_norm_w.shape[1]
    W = NH * DH
    NA = 8
    AH = W // NA
    XH = 4
    G = 4
    PAIRS = E // 2
    SLOTS = 64
    ALPHA = float((2 * DEPTH) ** 0.25)
    LN_EPS, RMS_EPS = 1e-5, 1e-6
    TAPS, STAPS = ab_conv_w.shape[1], sc_conv_w.shape[1]
    assert (T, D, DEPTH, E, F, NH, DH, NT) == (256, 1024, 2, 16, 512, 4, 128, 2)

    segments = trunk_steps()
    steps = [s for seg in segments for s in seg]
    count = {}
    totals = {e: 0 for e in (PE, ACT, DVE, POOL)}
    for s in steps:
        assert s not in count, s
        count[s] = {}
        for e in takes(s):
            totals[e] += 1
            count[s][e] = totals[e]
    bank_of, before = {}, {}
    for n, seg in enumerate(segments):
        filled = [s for s in seg if PE in takes(s) and s[0] != "y_first"]
        for i, s in enumerate(filled):
            bank_of[s] = i % BANKS
            before[s] = filled[i - BANKS] if i >= BANKS else None
            if before[s] is None and n:
                before[s] = "experts"
        for s in seg:
            if s[0] == "y_first":
                y = ("y", *s[1:])
                bank_of[s], before[s] = bank_of[y], before[y]
                assert seg.index(before[y]) < seg.index(s) < seg.index(y)

    def cols(w, c0):
        return w[:, c0:c0 + BANK].rearrange("(k p) n -> p k n", p=P)

    XW = [xa_w_q[l] for l in range(DEPTH)]
    q0, z0, ba0, d0 = 0, 3 * W, 4 * W, 4 * W + 2 * NH
    slot_reader = {}
    stream = []

    def slot(src, *readers):
        for r in readers:
            slot_reader.setdefault(r, []).append(len(stream))
        stream.append((src, readers[-1]))

    def experts_slots(l):
        for _ in range(3 * E):
            stream.append(None)

    w_in = ab_w_in[0]
    slot(cols(w_in, 0), ("qkv", 0, 0), ("qkv", 0, 1))
    slot(cols(w_in, W), ("qkv", 1, 0), ("qkv", 1, 1))
    slot(cols(w_in, 2 * W), ("qkv", 2, 0), ("qkv", 2, 1))
    slot(cols(w_in, d0), ("qd", 0), ("qd", 1))
    slot(cols(w_in, d0 + W), ("kd", 0), ("kd", 1))
    slot(cols(w_in, d0 + 2 * W), ("vd", 0), ("vd", 1))
    slot(cols(w_in, z0), ("z", 0), ("z", 1))

    def out_slots(w, l, s):
        for half in range(2):
            slot(cols(w, half * BANK), ("y", l, s, half, 0), ("y", l, s, half, 1))

    def k_slot(l, m):
        slot(cols(xa_w_kv[l], m * BANK), ("xk", l, 2 * m), ("xk", l, 2 * m + 1))

    def v_slot(l, half):
        slot(cols(xa_w_kv[l], D + half * BANK), ("xv", l, half, 0), ("xv", l, half, 1))

    def q_slots(l):
        for m in range(2):
            slot(cols(xa_w_q[l], m * BANK), ("xq", l, 2 * m), ("xq", l, 2 * m + 1))

    out_slots(ab_w_out[0], 0, 0)
    k_slot(0, 0)
    k_slot(0, 1)
    v_slot(0, 0)
    v_slot(0, 1)
    q_slots(0)
    out_slots(xa_w_o[0], 0, 1)
    k_slot(1, 0)
    first_expert_slot = [len(stream)]
    experts_slots(0)
    k_slot(1, 1)
    for half in range(2):
        for kind, part in (("sc_c", 1), ("sc_h", 2), ("sc_b", 0)):
            slot(cols(sc_w_in[0], part * D + half * BANK), (kind, half, 0), (kind, half, 1))
    v_slot(1, 0)
    out_slots(sc_w_out[0], 1, 0)
    v_slot(1, 1)
    q_slots(1)
    out_slots(xa_w_o[1], 1, 1)
    first_expert_slot.append(len(stream))
    experts_slots(1)
    RING = 6

    with ExitStack() as ctx:
        def sb(name, shape, dt=F32):
            return ctx.enter_context(nc.sbuf_tensor(name, shape, dt))

        def sem(name):
            return ctx.enter_context(nc.semaphore(name))

        ps = ctx.enter_context(nc.psum_tensor("ps", [P, BANKS, BANK], F32))

        ring = sb("ring", [P, RING, KD * BANK])
        h = sb("h", [P, NT, D])
        hn = sb("hn", [P, NT, D])
        hT = sb("hT", [P, KD, T])
        memT = sb("memT", [P, KD, T])
        gain = sb("gain", [P, 2, D])
        ident = sb("ident", [P, P])
        ones = sb("ones", [P, P])
        upto = sb("upto", [P, P])
        below = sb("below", [P, P])
        slot_no = sb("slot_no", [P, SLOTS])
        par_rows = sb("par_rows", [P, 2, P])
        par = sb("par", [P, 2, P])
        small = sb("small", [P, 16])
        wba = sb("wba", [P, KD, 2 * NH])
        wr = sb("wr", [P, KD, E])
        rb = sb("rb", [P, E])
        dtb = sb("dtb", [P, 2, NH])
        normw = sb("normw", [P, DH])
        ARENA = 15900
        arena = sb("arena", [P, ARENA])
        taken = [0]

        def carve(*shape, at=None):
            n = int(np.prod(shape))
            o = taken[0] if at is None else at
            taken[0] = max(taken[0], o + n)
            assert taken[0] <= ARENA, taken[0]
            v = arena[:, o:o + n]
            if len(shape) == 2:
                v = v.rearrange("p (a b) -> p a b", a=shape[0])
            if len(shape) == 3:
                v = v.rearrange("p (a b c) -> p a b c", a=shape[0], b=shape[1])
            return v

        qkv = carve(12, T)
        at_x = taken[0]
        X = carve(NT, NH, P)
        U = carve(NT, NH, P)
        sq = carve(8, T, at=at_x)
        st = carve(NH, P, at=at_x)
        r1 = carve(NH, P, at=at_x + NH * P)
        zs = carve(NT, W)
        qdT = carve(4, T)
        vd = carve(NT, W)
        ktok = carve(NH, P)
        vb = carve(NT, NH, P)
        DU = carve(NT, NH, P)
        DL = carve(NT, NH, P)
        at_b = taken[0]
        Bm = carve(NT, NH, P)
        o_sb = carve(NT, NH, P, at=at_b)
        at_v = taken[0]
        Vt = carve(NT, NH, P)
        tmpo = carve(NH, P, at=at_v)
        sqo = carve(NH, P, at=at_v + NH * P)
        vn = DL
        dp = [carve(384) for _ in range(2)]
        dpT = [carve(384) for _ in range(2)]
        ba = carve(NT, 2 * NH)
        beta = carve(NT, NH)
        ga, gb, graw, gcol, hcol, bk, rk, qs, eg, egq, nc1 = (carve(NT, NH) for _ in range(11))
        lss = carve(NT, 8)
        glast, kdec, ea = (carve(NH) for _ in range(3))
        rms = carve(NT, NH)
        dmx = [carve(2) for _ in range(2)]
        dden = [carve(2) for _ in range(2)]
        drec = [carve(2) for _ in range(2)]
        kdz = gain.rearrange("p a b -> p (a b)").rearrange("p (a b) -> p a b", a=NA)
        catT = hn.rearrange("p a b -> p (a b)").rearrange("p (a b) -> p a b", a=KD)
        memtok = carve(NT, D, at=at_b)
        levels = sb("levels", [P, 7, P], BF16)
        times = sb("times", [P, 384], BF16)
        shut = sb("shut", [P, 384], BF16)
        shutU = dpT[0][:, 0:P]
        shutL = dpT[1][:, 0:P]
        di = carve(384, at=at_x).bitcast(I32)
        dj = carve(384, at=at_x + 384).bitcast(I32)
        df = carve(384, at=at_x + 768)
        dg = carve(384, at=at_x + 1152)

        taken_ab = taken[0]
        taken[0] = 0
        xkT = carve(KD, T)
        xv = carve(NT, D)
        lnb = carve(NT, 2, 6)
        lnm = carve(NT, 4)
        at_sc = taken[0]
        xoT = carve(KD, T)
        xqT = carve(KD, T)
        xpr = [carve(NT, T) for _ in range(2)]
        xpT = [carve(NT, T) for _ in range(2)]
        xmx = [carve(NT) for _ in range(2)]
        xden = [carve(NT) for _ in range(2)]
        xrec = [carve(NT) for _ in range(2)]
        sc_y = carve(KD, T, at=at_sc)
        sc_u = carve(4, T, at=at_sc + KD * T)
        sc_a = carve(4, T, at=at_sc + (KD + 4) * T)
        taken[0] = at_sc
        onehot = carve(NT, 2, SLOTS)
        gated = carve(NT, 2, SLOTS)
        gatedT = carve(T)
        hidT = carve(4, P)
        silu = carve(F, at=KD * T)
        hid = carve(F, at=KD * T + F)
        outp = carve(D, at=KD * T + 2 * F)
        spare = hT[:].rearrange("p k t -> p (k t)")
        xg = spare[:, 0:D]
        xgT = spare[:, D:2 * D].rearrange("p (k t) -> p k t", k=KD)
        lg = carve(NT, E)
        sc = carve(NT, E)
        sel = carve(NT, E)
        gates = carve(NT, E)
        ta, tb, tc, oh1, posm = (carve(NT, E) for _ in range(5))
        hi, lo = carve(NT * G, 2), carve(NT * G, 2)
        g1, g2, g3, g4 = (carve(NT, G) for _ in range(4))
        s1, s2 = carve(NT), carve(NT)
        maxc = carve(4)
        lgT = carve(T)
        at_odd = ARENA - 2 * KD * BANK
        assert taken[0] <= at_odd, (taken[0], at_odd)
        odd_gate = carve(2, KD * BANK, at=at_odd)
        gidx = sb("gidx", [P, NT, G])
        eidx = sb("eidx", [P, NT, E])
        rounds = sb("rounds", [P, 1], I32)
        nexp = sb("nexp", [P, 1])

        steps_sem = {PE: sem("pe_steps"), ACT: sem("act_steps"), DVE: sem("dve_steps"), POOL: sem("pool_steps")}
        dve_own, act_own, pool_own = sem("dve_own"), sem("act_own"), sem("pool_own")
        slot_full = [sem(f"slot_full{i}") for i in range(RING)]
        odd_full = [sem(f"odd_full{j}") for j in range(2)]
        right_full = [sem(f"right_full{j}") for j in range(2)]
        first_full = sem("first_full")
        x_in = [sem(f"x_in{t}") for t in range(NT)]
        mem_in, rows_in, wba_in, vec_in, gain_in = (
            sem(n) for n in ("mem_in", "rows_in", "wba_in", "vec_in", "gain_in"))
        decay_in = sem("decay_in")
        stored = sem("stored")
        rounds_known = sem("rounds_known")
        ex_pe, ex_act, ex_dve = sem("ex_pe"), sem("ex_act"), sem("ex_dve")
        of = [{n: sem(f"of{l}_{n}") for n in ("slots", "pe", "act", "dve", "shift", "end")} for l in range(DEPTH)]

        def at(engine, step):
            return steps_sem[engine], count[step][engine]

        PE_PAIR, ACT_PAIR, DVE_PAIR = 14, 6, 10
        PE_ALL, ACT_ALL, DVE_ALL = PAIRS * PE_PAIR, PAIRS * ACT_PAIR, PAIRS * DVE_PAIR + 1

        def first(p):
            return isinstance(p, int) and p == 0

        def last(p):
            return isinstance(p, int) and p == PAIRS - 1

        def n_pe(l, kind, p):
            if kind in ("X0", "X1", "XT0", "XT1") and first(p):
                return l * PE_ALL + 1 + ("X0", "X1", "XT0", "XT1").index(kind)
            if kind in ("G", "U"):
                return l * PE_ALL + PE_PAIR * p + (4 if first(p) else 0) + (1 if kind == "G" else 2)
            if kind[0] == "Y":
                if last(p):
                    return l * PE_ALL + PE_ALL - 4 + 1 + int(kind[1])
                return l * PE_ALL + PE_PAIR * (p + 1) + 3 + int(kind[1])
            if kind[0] == "X":
                return l * PE_ALL + PE_PAIR * (p - 1) + {"X0": 7, "X1": 8, "XT0": 11, "XT1": 12}[kind]
            return (l * PE_ALL + PE_PAIR * p + {"HT": 9, "PT": 10, "O0": 13, "O1": 14}[kind]
                    - ({"HT": 2, "PT": 2, "O0": 4, "O1": 4}[kind] if last(p) else 0))

        def n_act(l, kind, p):
            if kind in ("X0", "XT0") and first(p):
                return l * ACT_ALL + 1 + ("X0", "XT0").index(kind)
            if kind in ("X0", "XT0"):
                return l * ACT_ALL + ACT_PAIR * (p - 1) + {"X0": 4, "XT0": 6}[kind]
            return (l * ACT_ALL + ACT_PAIR * p + {"silu": 3, "HT": 5, "O0": 7, "O1": 8}[kind]
                    - ({"silu": 0, "HT": 1, "O0": 2, "O1": 2}[kind] if last(p) else 0))

        def n_dve(l, kind, p):
            if first(p) and kind in ("onehot", "X1", "XT1", "scaled"):
                return l * DVE_ALL + 1 + ("onehot", "X1", "XT1", "scaled").index(kind)
            if kind in ("onehot", "X1", "XT1"):
                return l * DVE_ALL + DVE_PAIR * (p - 1) + {"onehot": 2, "X1": 8, "XT1": 10}[kind] + (
                    4 if kind == "onehot" and isinstance(p, int) and p == 1 else 0)
            if kind[0] == "Y":
                if last(p):
                    return l * DVE_ALL + DVE_ALL - 4 + 1 + int(kind[1])
                return (l * DVE_ALL + DVE_PAIR * (p + 1) + 4 + int(kind[1])
                        - (1 if isinstance(p, int) and p == PAIRS - 2 else 0))
            return (l * DVE_ALL + DVE_PAIR * p + {"gated": 1, "hid": 3, "PT": 9}[kind]
                    + (4 if first(p) and kind != "PT" else 0)
                    - ({"gated": 0, "hid": 1, "PT": 2}[kind] if last(p) else 0))

        BK = {"G": 0, "U": 1, "X0": 2, "X1": 3, "XT0": 2, "XT1": 3, "HT": 4, "PT": 5, "O0": 6, "O1": 7,
              "Y0": 4, "Y1": 5, "Y2": 6, "Y3": 7}

        def ring_at(l, part, j):
            return (first_expert_slot[l] + 2 * part + j) % RING

        fill_no, uses_before, fills = {}, {}, [0] * RING
        for n, entry in enumerate(stream):
            if entry is not None:
                fills[n % RING] += 1
                fill_no[n] = fills[n % RING]
            elif n in first_expert_slot:
                l = first_expert_slot.index(n)
                for part in range(3):
                    for j in range(2):
                        uses_before[l, part, j] = fills[ring_at(l, part, j)]
                        fills[ring_at(l, part, j)] += PAIRS if part else PAIRS // 2

        def wide(v):
            return v.rearrange("p (k n) -> p k n", k=KD)

        def tall(v):
            return v.rearrange("p (k n) -> p k n", k=4)

        block = ctx.enter_context(nc.Block())

        @block.sync
        def _(sp):
            def expert_src(l, part, e):
                w = (moe_w_gate, moe_w_up, moe_w_down)[part]
                return w[l, e].rearrange("(k p) n -> p k n", p=P)

            def expert_dst(l, part, j):
                s = ring[:, ring_at(l, part, j), :]
                return tall(s) if part == 2 else wide(s)

            def load(l, part, p, odd=False):
                for j in range(2):
                    if first(p):
                        sp.wait_ge(*at(PE, stream[first_expert_slot[l] + 2 * part + j - RING][1]))
                    dst, full = (wide(odd_gate[:, j, :]), odd_full[j]) if odd else (
                        expert_dst(l, part, j), slot_full[ring_at(l, part, j)])
                    sp.dma_start(dst, expert_src(l, part, 2 * p + j)).then_inc(full, 16)

            def load_down(l, p):
                for half in range(2):
                    c = slice(half * BANK, (half + 1) * BANK)
                    for j in range(2):
                        if first(p) and half == 0:
                            sp.wait_ge(*at(PE, stream[first_expert_slot[l] + 4 + j - RING][1]))
                        full = right_full[j] if half else slot_full[ring_at(l, 2, j)]
                        sp.dma_start(expert_dst(l, 2, j)[:, :, c], expert_src(l, 2, 2 * p + j)[:, :, c]).then_inc(full, 16)

            def load_next(l, p, odd):
                if not last(p):
                    sp.wait_ge(ex_pe, n_pe(l, "G", p - 1))
                    load(l, 0, p + 1, not odd)
                sp.wait_ge(ex_pe, n_pe(l, "U", p - 1))
                load(l, 1, p)
                sp.wait_ge(ex_pe, n_pe(l, "O1", p - 1))
                load_down(l, p)

            def overflow(l):
                sp.wait_ge(rounds_known, l + 1)
                nr = sp.value_load(rounds[0:1, 0:1], min_val=1, max_val=4)
                with sp.If(nr > 1):
                    sp.wait_ge(ex_pe, (l + 1) * PE_ALL)
                    with sp.Fori(1, nr) as b:
                        with sp.Fori(0, PAIRS) as p:
                            i = (b - 1) * PAIRS + p
                            sp.wait_ge(of[l]["dve"], i * 9 + 1)
                            for part in range(3):
                                for j in range(2):
                                    sp.dma_start(expert_dst(l, part, j), expert_src(l, part, 2 * p + j)).then_inc(
                                        of[l]["slots"], 16)
                    sp.wait_ge(of[l]["end"], 1)

            for t in range(NT):
                sp.dma_start(h[:, t, :], x[0].rearrange("(t p) d -> p t d", p=P)[:, t, :]).then_inc(x_in[t], 16)
            sp.dma_start(wba[:], ab_w_in[0][:, ba0:ba0 + 2 * NH].rearrange("(k p) n -> p k n", p=P)).then_inc(wba_in, 16)
            l = -1
            i = 0
            while i < len(stream):
                if i == 4:
                    sp.dma_start(memtok, mem[0].rearrange("(t p) d -> p t d", p=P)).then_inc(mem_in, 16)
                if stream[i] is None:
                    l += 1
                    load(l, 0, 0)
                    load(l, 1, 0)
                    sp.wait_ge(*at(PE, ("xo", l, XH - 1)))
                    load(l, 0, 1, True)
                    load_down(l, 0)
                    load_next(l, 1, True)
                    with sp.Fori(1, PAIRS // 2 - 1) as q:
                        load_next(l, 2 * q, False)
                        load_next(l, 2 * q + 1, True)
                    load_next(l, PAIRS - 2, False)
                    load_next(l, PAIRS - 1, True)
                    overflow(l)
                    i += 3 * E
                    continue
                if i >= RING:
                    if stream[i - RING] is None:
                        j = i - RING - first_expert_slot[l]
                        part = (j % 6) // 2
                        sp.wait_ge(ex_pe, n_pe(l, ("G", "U", "O1")[part], PAIRS - 1 if part else PAIRS - 2))
                    else:
                        sp.wait_ge(*at(PE, stream[i - RING][1]))
                dst, src = wide(ring[:, i % RING, :]), stream[i][0]
                if i == 0:
                    sp.dma_start(dst[:, :, 0:T], src[:, :, 0:T]).then_inc(slot_full[0], 16)
                    sp.dma_start(dst[:, :, T:], src[:, :, T:]).then_inc(first_full, 16)
                else:
                    sp.dma_start(dst, src).then_inc(slot_full[i % RING], 16)
                i += 1
            for t in range(NT):
                sp.wait_ge(*at(DVE, ("last", t)))
                sp.dma_start(out[0].rearrange("(t p) d -> p t d", p=P)[:, t, :], h[:, t, :]).then_inc(stored, 16)
            sp.wait_ge(stored, 16 * NT)

        @block.gpsimd
        def _(pool):
            own = [0]

            def link(ins):
                own[0] += 1
                ins.then_inc(pool_own, 1)
                pool.wait_ge(pool_own, own[0])

            def done(ins):
                ins.then_inc(steps_sem[POOL], 1)

            for step in steps:
                if POOL not in takes(step):
                    continue
                kind = step[0]
                if kind == "ident":
                    link(nc.gpsimd.memset(ones[:], 1.0))
                    done(nc.gpsimd.affine_select(out=ident[:], in_=ones[:], compare_op=ALU.is_equal, fill=0.0, base=0,
                                                 pattern=[[-1, P]], channel_multiplier=1))
                    pool.dma_start(wr[:], router_w.rearrange("(k p) e -> p k e", p=P)).then_inc(vec_in, 16)
                    pool.dma_start(rb[:], router_b.unsqueeze(0).to_broadcast([P, E])).then_inc(vec_in, 16)
                    pool.dma_start(normw[:], ab_norm_w[0:1, :].to_broadcast([P, DH])).then_inc(vec_in, 16)
                elif kind == "masks":
                    nc.gpsimd.memset(shutL, 0.0)
                    nc.gpsimd.memset(nexp[:], -0.5)
                    nc.gpsimd.iota(slot_no[:], [[1, SLOTS]], base=1, channel_multiplier=0,
                                   allow_small_or_imprecise_dtypes=True)
                    nc.gpsimd.iota(gidx[:], [[0, NT], [-1, G]], base=G, channel_multiplier=0,
                                   allow_small_or_imprecise_dtypes=True)
                    nc.gpsimd.iota(eidx[:], [[0, NT], [-1, E]], base=E, channel_multiplier=0,
                                   allow_small_or_imprecise_dtypes=True)
                    nc.gpsimd.iota(di[:, 0:P], [[0, P]], base=0, channel_multiplier=1)
                    nc.gpsimd.iota(dj[:, 0:2 * P], [[-1, 2 * P]], base=P, channel_multiplier=1)
                    link(nc.gpsimd.iota(dj[:, 2 * P:3 * P], [[-1, P]], base=0, channel_multiplier=1))
                    nc.gpsimd.affine_select(out=upto[:], in_=ones[:], compare_op=ALU.is_ge, fill=0.0, base=0,
                                            pattern=[[1, P]], channel_multiplier=-1)
                    nc.gpsimd.affine_select(out=below[:], in_=ones[:], compare_op=ALU.is_gt, fill=0.0, base=0,
                                            pattern=[[1, P]], channel_multiplier=-1)
                    nc.gpsimd.affine_select(out=shutU, in_=shutL, compare_op=ALU.is_ge, fill=NEG, base=0,
                                            pattern=[[1, P]], channel_multiplier=-1)
                    link(nc.gpsimd.iota(di[:, P:2 * P], [[1, P]], base=0, channel_multiplier=0))
                    done(nc.gpsimd.affine_select(out=shutL, in_=shutL, compare_op=ALU.is_gt, fill=NEG, base=0,
                                                 pattern=[[-1, P]], channel_multiplier=1))
                elif kind == "sumsq":
                    pool.wait_ge(*at(DVE, ("levels",)))
                    pool.wait_ge(*at(ACT, ("qkv", 1, 1)))
                    for i in range(4):
                        v = sq[:, 2 * i:2 * i + 2, :]
                        ins = nc.gpsimd.tensor_tensor(v, qkv[:, 2 * i:2 * i + 2, :], qkv[:, 2 * i:2 * i + 2, :], ALU.mult)
                    done(ins)
                elif kind == "blk":
                    _, k, t = step
                    pool.wait_ge(*at(DVE, ("gram", t)))
                    if k == 0:
                        pool.wait_ge(mem_in, 16)
                        for tt in range(NT):
                            pool.wait_ge(*at(PE, ("memT", tt, 1)))
                    else:
                        pool.wait_ge(*at(PE, ("inv_v", k - 1, t) if k > 1 else ("inv0", t)))
                        pool.wait_ge(*at(DVE, ("inv0", t)))
                    done(nc.gpsimd.tensor_tensor(Bm[:, t], DL[:, t],
                                                 levels[:, k:k + 1, :].to_broadcast([P, NH, P]), ALU.mult))
                elif kind == "ln_rstd":
                    _, l, s, t = step
                    pool.wait_ge(*at(DVE, ("ln_stats", l, s, t)))
                    done(nc.gpsimd.tensor_tensor(lnm[:, t, 2:3], lnm[:, t, 3:4], nexp[:], ALU.pow))
                elif kind == "ln_h":
                    _, l, s, t = step
                    pool.wait_ge(*at(DVE, ("ln_norm", l, s, t)))
                    pool.wait_ge(gain_in, 32 * (3 * l + s + 1))
                    link(nc.gpsimd.tensor_tensor(h[:, t, :], hn[:, t, :], gain[:, 0, :], ALU.mult))
                    done(nc.gpsimd.tensor_tensor(h[:, t, :], h[:, t, :], gain[:, 1, :], ALU.add))
            assert own[0] < 4096

        @block.scalar
        def _(act):
            own = [0]

            def link(ins):
                own[0] += 1
                ins.then_inc(act_own, 1)
                act.wait_ge(act_own, own[0])

            def done(ins):
                ins.then_inc(steps_sem[ACT], 1)

            def gains(l, s):
                for i, w in enumerate((ln_g, ln_b)):
                    act.dma_start(gain[:, i, :], w[l, s:s + 1, :].to_broadcast([P, D])).then_inc(gain_in, 16)

            act.dma_start(par_rows[0:TAPS * 12, 0, :],
                          ab_conv_w[0].rearrange("a (c p) -> (a c) p", p=P)).then_inc(rows_in, 16)
            act.dma_start(par_rows[48:48 + STAPS * KD, 0, :],
                          sc_conv_w[0].rearrange("a (c p) -> (a c) p", p=P)).then_inc(rows_in, 16)
            act.dma_start(par_rows[0:48, 1, :], ln_g.rearrange("l s (k p) -> (l s k) p", p=P)).then_inc(rows_in, 16)
            act.dma_start(par_rows[48:96, 1, :], ln_b.rearrange("l s (k p) -> (l s k) p", p=P)).then_inc(rows_in, 16)
            act.dma_start(dtb[:, 0, :], ab_dt_bias[0:1, :].to_broadcast([P, NH])).then_inc(decay_in, 16)
            act.dma_start(dtb[:, 1, :], ab_a_log[0:1, :].to_broadcast([P, NH])).then_inc(decay_in, 16)

            def experts(l):
                def gather_out(p):
                    act.wait_ge(ex_pe, n_pe(l, "X0", p))
                    nc.scalar.activation(xg[:, 0:BANK], ps[:, BK["X0"], :], ACTF.Copy).then_inc(ex_act, 1)

                def gatherT_out(p):
                    act.wait_ge(ex_pe, n_pe(l, "XT0", p))
                    for k in range(4):
                        ins = nc.scalar.activation(xgT[:, k, :], ps[:, BK["XT0"], k * P:(k + 1) * P], ACTF.Identity,
                                                   bias=bias_col(l, 1, k), scale=gain_col(l, 1, k))
                    ins.then_inc(ex_act, 1)

                def pair(p):
                    act.wait_ge(ex_pe, n_pe(l, "G", p))
                    if not first(p):
                        act.wait_ge(ex_dve, n_dve(l, "hid", p - 1))
                    nc.scalar.activation(silu, ps[:, BK["G"], :], ACTF.Silu).then_inc(ex_act, 1)
                    if not last(p):
                        gather_out(p + 1)
                    act.wait_ge(ex_pe, n_pe(l, "HT", p))
                    nc.scalar.activation(hidT, ps[:, BK["HT"], :].rearrange("p (a b) -> p a b", a=4),
                                         ACTF.Copy).then_inc(ex_act, 1)
                    if not last(p):
                        gatherT_out(p + 1)
                    for half in range(2):
                        act.wait_ge(ex_pe, n_pe(l, f"O{half}", p))
                        nc.scalar.activation(outp[:, half * BANK:(half + 1) * BANK], ps[:, BK[f"O{half}"], :],
                                             ACTF.Copy).then_inc(ex_act, 1)

                gather_out(0)
                gatherT_out(0)
                pair(0)
                with act.Fori(1, PAIRS - 1) as p:
                    pair(p)
                pair(PAIRS - 1)
                act.wait_ge(rounds_known, l + 1)
                nr = act.value_load(rounds[0:1, 0:1], min_val=1, max_val=4)
                with act.If(nr > 1):
                    with act.Fori(1, nr) as b:
                        with act.Fori(0, PAIRS) as p:
                            act.wait_ge(of[l]["pe"], ((b - 1) * PAIRS + p) * 7 + 4)
                            nc.scalar.activation(silu, ps[:, BK["G"], :], ACTF.Silu).then_inc(of[l]["act"], 1)

            def gain_col(l, s, k):
                c = (3 * l + s) * KD + k
                return par[:, 1, c:c + 1]

            def bias_col(l, s, k):
                c = 48 + (3 * l + s) * KD + k
                return par[:, 1, c:c + 1]

            def psum(step):
                return ps[:, bank_of[step], :]

            for n, seg in enumerate(segments):
                if n:
                    experts(n - 1)
                for step in seg:
                    kind = step[0]
                    if ACT not in takes(step):
                        continue
                    if PE in takes(step):
                        act.wait_ge(*at(PE, step))
                    if kind in ("xT", "memT"):
                        _, t, g = step
                        dst = (hT if kind == "xT" else memT)[:, 4 * g:4 * g + 4, t * P:(t + 1) * P]
                        done(nc.scalar.activation(dst, psum(step).rearrange("p (a b) -> p a b", a=4), ACTF.Copy))
                    elif kind == "hT":
                        _, l, s, t, g = step
                        act.wait_ge(*at(DVE, ("params",)))
                        for k in range(4):
                            ins = nc.scalar.activation(hT[:, 4 * g + k, t * P:(t + 1) * P], psum(step)[:, k * P:(k + 1) * P],
                                                       ACTF.Identity, bias=bias_col(l, s, 4 * g + k),
                                                       scale=gain_col(l, s, 4 * g + k))
                        done(ins)
                    elif kind == "gates":
                        act.wait_ge(*at(DVE, ("ba",)))
                        nc.scalar.activation(beta, ba[:, :, 0:NH], ACTF.Exp, scale=-1.0)
                        nc.scalar.activation(ea, dtb[:, 1, :], ACTF.Exp)
                        link(nc.scalar.activation(ga, gb, ACTF.Exp, scale=-1.0))
                        done(nc.scalar.activation(ga, ga, ACTF.Ln, bias=ones[:, 0:1]))
                    elif kind == "qkv":
                        _, s, m = step
                        act.wait_ge(*at(DVE, step))
                        v = qkv[:, 4 * s + 2 * m:4 * s + 2 * m + 2, :]
                        done(nc.scalar.activation(v, v, ACTF.Silu))
                    elif kind == "sumsq":
                        done(nc.scalar.activation(lss, psum(step)[:, 0:NT * 8].rearrange("p (a b) -> p a b", a=NT),
                                                  ACTF.Ln, bias=small[:, 0:1]))
                    elif kind == "cols":
                        act.wait_ge(*at(DVE, ("cumsum",)))
                        act.wait_ge(*at(ACT, ("sumsq",)))
                        nc.scalar.activation(rk, lss[:, :, NH:2 * NH], ACTF.Exp, scale=-0.5)
                        nc.scalar.activation(qs, lss[:, :, 0:NH], ACTF.Exp, scale=-0.5)
                        done(nc.scalar.activation(eg, gcol, ACTF.Exp))
                    elif kind in ("rowg", "rowh"):
                        _, t = step
                        act.wait_ge(*at(DVE, step))
                        m, col = (DU, hcol) if kind == "rowg" else (DL, gcol)
                        for hd in range(NH):
                            ins = nc.scalar.activation(m[:, t, hd, :], m[:, t, hd, :], ACTF.Exp, bias=col[:, t, hd:hd + 1])
                        done(ins)
                    elif kind == "z":
                        done(nc.scalar.activation(zs[:, step[1], :], psum(step), ACTF.Silu))
                    elif kind == "ktok":
                        act.wait_ge(*at(DVE, ("rowg", 0)))
                        link(nc.scalar.activation(kdec, kdec, ACTF.Exp))
                        for hd in range(NH):
                            ins = nc.scalar.activation(ktok[:, hd, :], psum(step)[:, hd * P:(hd + 1) * P], ACTF.Copy,
                                                       scale=kdec[:, hd:hd + 1])
                        done(ins)
                    elif kind == "vtok":
                        _, t = step
                        act.wait_ge(*at(DVE, ("gates",)))
                        for hd in range(NH):
                            ins = nc.scalar.activation(vb[:, t, hd, :], psum(step)[:, hd * P:(hd + 1) * P], ACTF.Copy,
                                                       scale=beta[:, t, hd:hd + 1])
                        done(ins)
                    elif kind == "inv_v":
                        _, k, t = step
                        if k == 1:
                            for tt in range(NT):
                                act.wait_ge(*at(PE, ("memT", tt, 1)))
                        done(nc.scalar.activation(Vt[:, t], psum(step).rearrange("p (a b) -> p a b", a=NH), ACTF.Copy))
                    elif kind == "qd":
                        _, m = step
                        done(nc.scalar.activation(qdT[:, 2 * m:2 * m + 2, :], psum(step).rearrange("p (a b) -> p a b", a=2),
                                                  ACTF.Copy, scale=float(AH) ** -0.5))
                    elif kind == "kd":
                        _, m = step
                        act.wait_ge(*at(DVE, ("levels",)))
                        src = psum(step).rearrange("p (a b) -> p a b", a=2)
                        nc.scalar.activation(kdz[0:AH, 4 * m:4 * m + 4:2, :], src[0:AH], ACTF.Copy)
                        done(nc.scalar.activation(kdz[AH:P, 4 * m + 1:4 * m + 4:2, :], src[AH:P], ACTF.Copy))
                    elif kind == "d_probs":
                        _, hd = step
                        act.wait_ge(*at(DVE, ("d_scores", hd)))
                        b = hd % 2
                        nc.scalar.activation(dp[b][:, 0:2 * P], dp[b][:, 0:2 * P], ACTF.Exp, bias=dmx[b][:, 1:2])
                        done(nc.scalar.activation(dp[b][:, 2 * P:3 * P], dp[b][:, 2 * P:3 * P], ACTF.Exp, bias=dmx[b][:, 0:1]))
                    elif kind == "d_pT":
                        _, hd = step
                        if hd >= 2:
                            act.wait_ge(*at(PE, ("d_pv", (hd - 2) // 2)))
                        done(nc.scalar.activation(dpT[hd % 2][:, :], psum(step)[:, 0:3 * P], ACTF.Copy))
                    elif kind == "d_pv":
                        _, hp = step
                        ins = nc.scalar.activation(catT[:, NH + hp, :], psum(step)[:, 0:T], ACTF.Copy)
                        done(ins)
                        if hp == 3:
                            act.wait_ge(*at(PE, ("d_scores", NA - 1)))
                            gains(0, 0)
                    elif kind == "vnew":
                        _, c = step
                        done(nc.scalar.activation(vn[:, c], psum(step).rearrange("p (a b) -> p a b", a=NH), ACTF.Copy))
                    elif kind == "state":
                        done(nc.scalar.activation(st, psum(step).rearrange("p (a b) -> p a b", a=NH), ACTF.Copy))
                    elif kind == "qstate":
                        act.wait_ge(*at(DVE, ("cols",)))
                        act.wait_ge(*at(PE, ("inv_x", 5, 1)))
                        act.wait_ge(*at(PE, ("inv_u", 6, 1)))
                        for hd in range(NH):
                            ins = nc.scalar.activation(tmpo[:, hd, :], psum(step)[:, hd * P:(hd + 1) * P], ACTF.Copy,
                                                       scale=egq[:, 1, hd:hd + 1])
                        done(ins)
                    elif kind == "osq":
                        _, c = step
                        act.wait_ge(*at(DVE, ("o", c)))
                        act.wait_ge(*at(PE, ("inv_u", 6, 1)))
                        for hd in range(NH):
                            ins = nc.scalar.activation(sqo[:, hd, :], o_sb[:, c, hd, :], ACTF.Square,
                                                       accum_out=rms[:, c, hd:hd + 1])
                        link(ins)
                        link(nc.scalar.activation(rms[:, c, :], rms[:, c, :], ACTF.Ln, scale=1.0 / DH, bias=small[:, 0:1]))
                        done(nc.scalar.activation(rms[:, c, :], rms[:, c, :], ACTF.Exp, scale=-0.5))
                    elif kind == "xk":
                        _, l, m = step
                        done(nc.scalar.activation(xkT[:, 2 * m:2 * m + 2, :], psum(step).rearrange("p (a b) -> p a b", a=2),
                                                  ACTF.Copy))
                    elif kind == "xq":
                        _, l, m = step
                        done(nc.scalar.activation(xqT[:, 2 * m:2 * m + 2, :], psum(step).rearrange("p (a b) -> p a b", a=2),
                                                  ACTF.Copy, scale=float(D // XH) ** -0.5))
                    elif kind == "xs":
                        _, l, hd = step
                        act.wait_ge(*at(DVE, step))
                        b = hd % 2
                        if hd >= 2:
                            act.wait_ge(*at(PE, ("xp", l, hd - 2)))
                        for t in range(NT):
                            ins = nc.scalar.activation(xpr[b][:, t, :], psum(step)[:, t * T:(t + 1) * T], ACTF.Exp,
                                                       bias=xmx[b][:, t:t + 1], accum_out=xden[b][:, t:t + 1])
                        done(ins)
                    elif kind == "xo":
                        _, l, hd = step
                        done(nc.scalar.activation(xoT[:, 2 * hd:2 * hd + 2, :], psum(step).rearrange("p (a b) -> p a b", a=2),
                                                  ACTF.Copy))
                        if hd == 0:
                            for t in range(NT):
                                act.wait_ge(*at(POOL, ("ln_h", l, 0, t)))
                            gains(l, 1)
                    elif kind == "route_soft":
                        _, l = step
                        act.wait_ge(*at(DVE, ("route_t", l)))
                        done(nc.scalar.activation(sc, lg, ACTF.Exp))
                        for t in range(NT):
                            act.wait_ge(*at(POOL, ("ln_h", l, 1, t)))
                        gains(l, 2)
                    elif kind == "sc_c":
                        _, half, m = step
                        if half:
                            act.wait_ge(*at(DVE, ("sc_h", 0, 1)))
                        if (half, m) == (0, 0):
                            for t in range(NT):
                                act.wait_ge(*at(DVE, ("hT", 0, 2, t, 1)))
                        done(nc.scalar.activation(sc_u[:, 2 * m:2 * m + 2, :], psum(step).rearrange("p (a b) -> p a b", a=2),
                                                  ACTF.Copy))
                        if (half, m) == (1, 1):
                            for t in range(NT):
                                act.wait_ge(*at(POOL, ("ln_h", 0, 2, t)))
                            gains(1, 0)
                    else:
                        raise AssertionError(kind)

        @block.vector
        def _(dve):
            own = [0]
            V = nc.vector

            def link(ins):
                own[0] += 1
                ins.then_inc(dve_own, 1)
                dve.wait_ge(dve_own, own[0])

            def done(ins):
                ins.then_inc(steps_sem[DVE], 1)

            def gain_col(l, s, k):
                c = (3 * l + s) * KD + k
                return par[:, 1, c:c + 1]

            def bias_col(l, s, k):
                c = 48 + (3 * l + s) * KD + k
                return par[:, 1, c:c + 1]

            def psum(step):
                return ps[:, bank_of[step], :]

            def over_slots(v):
                return v.unsqueeze(3).to_broadcast([P, NT, 2, SLOTS])

            def slots_over():
                return slot_no[:].unsqueeze(1).unsqueeze(1).to_broadcast([P, NT, 2, SLOTS])

            def build_onehot(p):
                return V.tensor_tensor(onehot, slots_over(), over_slots(posm[:, :, bass.ds(2 * p, 2)]), ALU.is_equal)

            def gathered_cols(l, bank, k0):
                for k in range(4):
                    ins = V.tensor_scalar(xgT[:, k0 + k, :], ps[:, bank, k * P:(k + 1) * P],
                                          gain_col(l, 1, k0 + k), bias_col(l, 1, k0 + k), ALU.mult, ALU.add)
                return ins

            def experts(l):
                def gather_out(p):
                    dve.wait_ge(ex_pe, n_pe(l, "X1", p))
                    V.tensor_copy(xg[:, BANK:D], ps[:, BK["X1"], :]).then_inc(ex_dve, 1)

                def gatherT_out(p):
                    dve.wait_ge(ex_pe, n_pe(l, "XT1", p))
                    gathered_cols(l, BK["XT1"], 4).then_inc(ex_dve, 1)

                def add_out(p):
                    for i in range(4):
                        t, half = i // 2, i % 2
                        dve.wait_ge(ex_pe, n_pe(l, f"Y{i}", p))
                        hv = h[:, t, half * BANK:(half + 1) * BANK]
                        V.tensor_tensor(hv, hv, ps[:, BK[f"Y{i}"], :], ALU.add).then_inc(ex_dve, 1)
                        if last(p):
                            dve.wait_ge(ex_dve, n_dve(l, f"Y{i}", p))
                            ins = V.bn_stats(lnb[:, t, half, :], hv)
                    if last(p):
                        link(ins)

                def pair(p):
                    if not first(p):
                        dve.wait_ge(ex_pe, n_pe(l, "PT", p - 1))
                    dve.wait_ge(ex_dve, n_dve(l, "onehot", p))
                    V.tensor_tensor(gated, onehot, over_slots(gates[:, :, bass.ds(2 * p, 2)]),
                                    ALU.mult).then_inc(ex_dve, 1)
                    if not last(p):
                        dve.wait_ge(ex_dve, n_dve(l, "gated", p))
                        dve.wait_ge(ex_pe, n_pe(l, "X1", p))
                        build_onehot(p + 1).then_inc(ex_dve, 1)
                    dve.wait_ge(ex_act, n_act(l, "silu", p))
                    dve.wait_ge(ex_pe, n_pe(l, "U", p))
                    V.tensor_tensor(hid, silu, ps[:, BK["U"], :], ALU.mult).then_inc(ex_dve, 1)
                    if not first(p):
                        add_out(p - 1)
                    if not last(p):
                        gather_out(p + 1)
                    dve.wait_ge(ex_pe, n_pe(l, "PT", p))
                    V.tensor_copy(gatedT, ps[:, BK["PT"], 0:T]).then_inc(ex_dve, 1)
                    if not last(p):
                        gatherT_out(p + 1)

                dve.wait_ge(*at(DVE, ("place", l)))
                build_onehot(0).then_inc(ex_dve, 1)
                for i in range(1, 4):
                    ins = V.tensor_scalar(maxc[:, i:i + 1], maxc[:, 0:1], float(i * SLOTS), None, ALU.is_gt)
                link(ins)
                link(V.tensor_reduce(maxc[:, 0:1], maxc[:, 1:4], AX, ALU.add))
                V.tensor_scalar(rounds[:], maxc[:, 0:1], 1.0, None, ALU.add).then_inc(rounds_known, 1)
                gather_out(0)
                gatherT_out(0)
                for t in range(NT):
                    dve.wait_ge(*at(POOL, ("ln_h", l, 1, t)))
                V.tensor_scalar(h[:], h[:], ALPHA, None, ALU.mult).then_inc(ex_dve, 1)
                dve.wait_ge(ex_dve, n_dve(l, "scaled", 0))
                pair(0)
                with dve.Fori(1, PAIRS - 1) as p:
                    pair(p)
                pair(PAIRS - 1)
                add_out(PAIRS - 1)
                dve.wait_ge(rounds_known, l + 1)
                nr = dve.value_load(rounds[0:1, 0:1], min_val=1, max_val=4)
                with dve.If(nr > 1):
                    o = of[l]
                    V.memset(maxc[:, 1:2], 0.0).then_inc(o["dve"], 1)
                    with dve.Fori(1, nr) as b:
                        V.tensor_scalar(posm, posm, float(-SLOTS), None, ALU.add).then_inc(o["shift"], 1)
                        with dve.Fori(0, PAIRS) as p:
                            i = (b - 1) * PAIRS + p
                            n_o, n_p = i * 9 + 1, i * 7
                            dve.wait_ge(o["shift"], b)
                            build_onehot(p)
                            V.tensor_tensor(gated, slots_over(), over_slots(posm[:, :, bass.ds(2 * p, 2)]),
                                            ALU.is_equal).then_inc(o["dve"], 1)
                            dve.wait_ge(o["dve"], n_o + 1)
                            V.tensor_tensor(gated, gated, over_slots(gates[:, :, bass.ds(2 * p, 2)]),
                                            ALU.mult).then_inc(o["dve"], 1)
                            dve.wait_ge(o["pe"], n_p + 1)
                            V.tensor_copy(xg.rearrange("p (a b) -> p a b", a=2), ps[:, 2:4, :]).then_inc(o["dve"], 1)
                            dve.wait_ge(o["pe"], n_p + 2)
                            gathered_cols(l, BK["XT0"], 0)
                            gathered_cols(l, BK["XT1"], 4).then_inc(o["dve"], 1)
                            dve.wait_ge(o["pe"], n_p + 3)
                            V.tensor_copy(gatedT, ps[:, BK["PT"], 0:T]).then_inc(o["dve"], 1)
                            dve.wait_ge(o["act"], i + 1)
                            dve.wait_ge(o["pe"], n_p + 4)
                            V.tensor_tensor(hid, silu, ps[:, BK["U"], :], ALU.mult).then_inc(o["dve"], 1)
                            dve.wait_ge(o["pe"], n_p + 5)
                            V.tensor_copy(hidT, ps[:, BK["HT"], :].rearrange("p (a b) -> p a b", a=4)).then_inc(o["dve"], 1)
                            dve.wait_ge(o["pe"], n_p + 6)
                            V.tensor_copy(outp.rearrange("p (a b) -> p a b", a=2), ps[:, 6:8, :]).then_inc(o["dve"], 1)
                            dve.wait_ge(o["pe"], n_p + 7)
                            for t in range(NT):
                                ins = V.tensor_tensor(h[:, t, :].rearrange("p (a b) -> p a b", a=2),
                                                      h[:, t, :].rearrange("p (a b) -> p a b", a=2), ps[:, 4 + 2 * t:6 + 2 * t, :], ALU.add)
                            ins.then_inc(o["dve"], 1)
                            dve.wait_ge(o["dve"], n_o + 9)
                    for i in range(4):
                        ins = V.bn_stats(lnb[:, i // 2, i % 2, :], h[:, i // 2, (i % 2) * BANK:(i % 2 + 1) * BANK])
                    ins.then_inc(o["end"], 1)
                    dve.wait_ge(o["end"], 1)

            for n, seg in enumerate(segments):
                if n:
                    experts(n - 1)
                for step in seg:
                    if DVE not in takes(step):
                        continue
                    kind = step[0]
                    if PE in takes(step):
                        dve.wait_ge(*at(PE, step))
                    if kind == "levels":
                        V.memset(small[:, 0:1], RMS_EPS)
                        V.memset(gain[:], 0.0)
                        dve.wait_ge(*at(POOL, ("masks",)))
                        link(V.tensor_tensor(di[:, 0:P], di[:, 0:P], di[:, P:2 * P], ALU.bitwise_xor))
                        for k in range(7):
                            link(V.tensor_scalar(di[:, P:2 * P], di[:, 0:P], k, None, ALU.logical_shift_right))
                            link(V.tensor_scalar(levels[:, k, :], di[:, P:2 * P], 1, None, ALU.is_equal))
                        link(V.tensor_scalar(di[:, :], dj[:, :], 3, None, ALU.bitwise_and))
                        link(V.tensor_scalar(df, di[:, :], 0, None, ALU.is_equal))
                        link(V.tensor_scalar(di[:, :], dj[:, :], 15, None, ALU.bitwise_and))
                        link(V.tensor_scalar(dg, di[:, :], 0, None, ALU.is_equal))
                        link(V.tensor_tensor(df, df, dg, ALU.add))
                        link(V.tensor_scalar(dg, dj[:, :], P, None, ALU.is_le))
                        link(V.tensor_tensor(df, df, dg, ALU.add))
                        link(V.tensor_scalar(dg, dj[:, :], 0, None, ALU.is_ge))
                        link(V.tensor_tensor(df, df, dg, ALU.mult))
                        V.tensor_copy(times[:], df)
                        done(V.tensor_scalar(shut[:], df, 0.0, NEG, ALU.is_equal, ALU.mult))
                    elif kind == "params":
                        V.tensor_copy(par[:, 0, 0:72], psum(step)[:, 0:72])
                        done(V.tensor_copy(par[:, 1, 0:96], psum(step)[:, P:P + 96]))
                    elif kind in ("xT", "memT"):
                        _, t, g = step
                        dst = (hT if kind == "xT" else memT)[:, 4 * g:4 * g + 4, t * P:(t + 1) * P]
                        done(V.tensor_copy(dst, psum(step).rearrange("p (a b) -> p a b", a=4)))
                    elif kind == "hT":
                        _, l, s, t, g = step
                        for k in range(4):
                            ins = V.tensor_scalar(hT[:, 4 * g + k, t * P:(t + 1) * P], psum(step)[:, k * P:(k + 1) * P],
                                                  gain_col(l, s, 4 * g + k), bias_col(l, s, 4 * g + k), ALU.mult, ALU.add)
                        done(ins)
                    elif kind == "ba":
                        link(V.tensor_copy(ba, psum(step)[:, 0:NT * 2 * NH].rearrange("p (a b) -> p a b", a=NT)))
                        dve.wait_ge(decay_in, 32)
                        link(V.tensor_tensor(ba[:, :, NH:], ba[:, :, NH:], dtb[:, 0:1, :].to_broadcast([P, NT, NH]), ALU.add))
                        done(V.scalar_tensor_tensor(gb, ba[:, :, NH:], -1.0, ba[:, :, NH:], ALU.mult, ALU.max))
                    elif kind == "gates":
                        dve.wait_ge(*at(ACT, step))
                        link(V.tensor_scalar(beta, beta, 1.0, None, ALU.add))
                        V.reciprocal(beta, beta)
                        link(V.scalar_tensor_tensor(gb, ba[:, :, NH:], 0.0, ga, ALU.max, ALU.add))
                        done(V.scalar_tensor_tensor(graw, gb, -1.0, ea.unsqueeze(1).to_broadcast([P, NT, NH]),
                                                    ALU.mult, ALU.mult))
                    elif kind == "qkv":
                        _, s, m = step
                        dve.wait_ge(*at(DVE, ("params",)))
                        for i in range(2):
                            c = 4 * s + 2 * m + i
                            src, dst = psum(step)[:, i * T:(i + 1) * T], qkv[:, c, :]

                            def tap(k):
                                return par[:, 0, k * 12 + c:k * 12 + c + 1]
                            link(V.tensor_scalar(dst, src, tap(TAPS - 1), None, ALU.mult))
                            for k in range(1, TAPS):
                                ins = V.scalar_tensor_tensor(dst[:, k:], src[:, :T - k], tap(TAPS - 1 - k), dst[:, k:],
                                                             ALU.mult, ALU.add)
                                if k < TAPS - 1 or i == 0:
                                    link(ins)
                        done(ins)
                    elif kind == "cumsum":
                        done(V.tensor_copy(gcol, psum(step)[:, 0:NT * NH].rearrange("p (a b) -> p a b", a=NT)))
                    elif kind == "cols":
                        dve.wait_ge(*at(ACT, step))
                        dve.wait_ge(*at(DVE, ("cumsum",)))
                        V.scalar_tensor_tensor(hcol, lss[:, :, NH:2 * NH], -0.5, gcol, ALU.mult, ALU.subtract)
                        link(V.tensor_scalar(qs, qs, float(DH) ** -0.5, None, ALU.mult))
                        link(V.tensor_tensor(bk, beta, rk, ALU.mult))
                        V.scalar_tensor_tensor(nc1, bk, -1.0, eg, ALU.mult, ALU.mult)
                        done(V.tensor_tensor(egq, eg, qs, ALU.mult))
                    elif kind == "rowg":
                        _, t = step
                        if t == 0:
                            link(V.tensor_copy(glast, psum(step)[:, P - 1:NH * P:P]))
                            dve.wait_ge(*at(DVE, ("cols",)))
                            V.tensor_tensor(kdec, glast, hcol[:, 0, :], ALU.add)
                        done(V.tensor_tensor(DU[:, t], psum(step).rearrange("p (a b) -> p a b", a=NH),
                                             shutU.unsqueeze(1).to_broadcast([P, NH, P]), ALU.add))
                    elif kind == "rowh":
                        _, t = step
                        done(V.tensor_tensor(DL[:, t], psum(step).rearrange("p (a b) -> p a b", a=NH),
                                             shutL.unsqueeze(1).to_broadcast([P, NH, P]), ALU.add))
                    elif kind == "gram":
                        _, t = step
                        dve.wait_ge(*at(ACT, ("rowh", t)))
                        for hd in range(NH):
                            ins = V.scalar_tensor_tensor(DL[:, t, hd, :], psum(step)[:, hd * P:(hd + 1) * P],
                                                         bk[:, t, hd:hd + 1], DL[:, t, hd, :], ALU.mult, ALU.mult)
                        done(ins)
                    elif kind == "qk":
                        _, t = step
                        dve.wait_ge(*at(ACT, ("rowg", t)))
                        done(V.tensor_tensor(DU[:, t], psum(step).rearrange("p (a b) -> p a b", a=NH), DU[:, t], ALU.mult))
                    elif kind == "inv0":
                        _, t = step
                        dve.wait_ge(*at(PE, ("sumsq",)))
                        dve.wait_ge(*at(POOL, ("blk", 0, t)))
                        eye = ident[:].unsqueeze(1).to_broadcast([P, NH, P])
                        V.scalar_tensor_tensor(X[:, t], Bm[:, t], -1.0, eye, ALU.mult, ALU.add)
                        done(V.scalar_tensor_tensor(U[:, t], psum(step).rearrange("p (a b) -> p a b", a=NH), -1.0, eye,
                                                    ALU.mult, ALU.add))
                    elif kind in ("inv_u", "inv_x"):
                        _, k, t = step
                        m = U if kind == "inv_u" else X
                        prev = ("inv0", t) if k == 1 else (kind, k - 1, t)
                        dve.wait_ge(*at(DVE, prev))
                        done(V.tensor_tensor(m[:, t], m[:, t], psum(step).rearrange("p (a b) -> p a b", a=NH), ALU.subtract))
                    elif kind == "vd":
                        done(V.tensor_copy(vd[:, step[1], :], psum(step)))
                    elif kind == "d_scores":
                        _, hd = step
                        b = hd % 2
                        dve.wait_ge(*at(DVE, ("levels",)))
                        if hd >= 2:
                            dve.wait_ge(*at(PE, ("d_pT", hd - 2)))
                        link(V.tensor_tensor(dp[b][:, :], psum(step)[:, 0:3 * P], shut[:], ALU.add))
                        V.tensor_reduce(dmx[b][:, 1:2], dp[b][:, 0:2 * P], AX, ALU.max, negate=True)
                        done(V.tensor_reduce(dmx[b][:, 0:1], dp[b][:, 2 * P:3 * P], AX, ALU.max, negate=True))
                    elif kind == "d_probs":
                        _, hd = step
                        b = hd % 2
                        dve.wait_ge(*at(ACT, step))
                        v1, v0 = dp[b][:, 0:2 * P], dp[b][:, 2 * P:3 * P]
                        V.scalar_tensor_tensor(v1, v1, 1.0, times[:, 0:2 * P], ALU.mult, ALU.mult, accum_out=dden[b][:, 1:2])
                        link(V.scalar_tensor_tensor(v0, v0, 1.0, times[:, 2 * P:3 * P], ALU.mult, ALU.mult,
                                                    accum_out=dden[b][:, 0:1]))
                        link(V.reciprocal(drec[b], dden[b]))
                        V.tensor_scalar(v1, v1, drec[b][:, 1:2], None, ALU.mult)
                        done(V.tensor_scalar(v0, v0, drec[b][:, 0:1], None, ALU.mult))
                    elif kind == "kstate":
                        dve.wait_ge(*at(ACT, ("vtok", 1)))
                        for hd in range(NH):
                            ins = V.scalar_tensor_tensor(r1[:, hd, :], psum(step)[:, hd * P:(hd + 1) * P],
                                                         nc1[:, 1, hd:hd + 1], vb[:, 1, hd, :], ALU.mult, ALU.add)
                        done(ins)
                    elif kind == "o":
                        _, c = step
                        if c:
                            dve.wait_ge(*at(ACT, ("qstate",)))
                        else:
                            for t in range(NT):
                                dve.wait_ge(*at(PE, ("inv_v", 6, t)))
                        for hd in range(NH):
                            src, scale = psum(step)[:, hd * P:(hd + 1) * P], qs[:, c, hd:hd + 1]
                            if c:
                                ins = V.scalar_tensor_tensor(o_sb[:, c, hd, :], src, scale, tmpo[:, hd, :], ALU.mult, ALU.add)
                            else:
                                ins = V.tensor_scalar(o_sb[:, c, hd, :], src, scale, None, ALU.mult)
                        done(ins)
                    elif kind == "onorm":
                        _, c = step
                        dve.wait_ge(*at(ACT, ("z", c)))
                        if c == 0:
                            dve.wait_ge(vec_in, 48)
                        zv = zs[:, c, :].rearrange("p (a b) -> p a b", a=NH)
                        link(V.tensor_tensor(zv, zv, normw[:].unsqueeze(1).to_broadcast([P, NH, DH]), ALU.mult))
                        dve.wait_ge(*at(ACT, ("osq", c)))
                        for hd in range(NH):
                            ins = V.scalar_tensor_tensor(o_sb[:, c, hd, :], o_sb[:, c, hd, :], rms[:, c, hd:hd + 1],
                                                         zv[:, hd, :], ALU.mult, ALU.mult)
                        done(ins)
                    elif kind == "oT":
                        _, t = step
                        done(V.tensor_copy(catT[:, 0:NH, t * P:(t + 1) * P], psum(step).rearrange("p (a b) -> p a b", a=NH)))
                    elif kind == "y":
                        _, l, s, half, t = step
                        if (l, s) != (0, 0):
                            dve.wait_ge(*at(POOL, ("ln_h", l, s - 1, t) if s else ("ln_h", l - 1, 2, t)))
                        hv = h[:, t, half * BANK:(half + 1) * BANK]
                        link(V.scalar_tensor_tensor(hv, hv, ALPHA, psum(step), ALU.mult, ALU.add))
                        done(V.bn_stats(lnb[:, t, half, :], hv))
                    elif kind == "ln_stats":
                        _, l, s, t = step
                        if s < 2:
                            dve.wait_ge(*at(DVE, ("y", l, s, 1, t)))
                        link(V.bn_aggr(lnm[:, t, 0:2], lnb[:, t].rearrange("p a b -> p (a b)")))
                        done(V.tensor_scalar(lnm[:, t, 3:4], lnm[:, t, 1:2], LN_EPS, None, ALU.add))
                    elif kind == "ln_norm":
                        _, l, s, t = step
                        dve.wait_ge(*at(POOL, ("ln_rstd", l, s, t)))
                        if (l, s) == (0, 0):
                            dve.wait_ge(*at(PE, ("y", 0, 0, 1, 1)))
                        done(V.tensor_scalar(hn[:, t, :], h[:, t, :], lnm[:, t, 0:1], lnm[:, t, 2:3], ALU.subtract, ALU.mult))
                    elif kind == "last":
                        t = step[1]
                        dve.wait_ge(*at(DVE, ("ln_stats", 1, 2, t)))
                        dve.wait_ge(gain_in, 32 * 6)
                        link(V.scalar_tensor_tensor(hn[:, t, :], h[:, t, :], lnm[:, t, 0:1], gain[:, 0, :],
                                                    ALU.subtract, ALU.mult))
                        dve.wait_ge(*at(POOL, ("ln_rstd", 1, 2, t)))
                        done(V.scalar_tensor_tensor(h[:, t, :], hn[:, t, :], lnm[:, t, 2:3], gain[:, 1, :],
                                                    ALU.mult, ALU.add))
                    elif kind == "xv":
                        _, l, half, t = step
                        done(V.tensor_copy(xv[:, t, half * BANK:(half + 1) * BANK], psum(step)))
                    elif kind == "xs":
                        _, l, hd = step
                        if hd >= 2:
                            dve.wait_ge(*at(ACT, ("xs", l, hd - 2)))
                        done(V.tensor_reduce(xmx[hd % 2], psum(step).rearrange("p (a b) -> p a b", a=NT), AX, ALU.max,
                                             negate=True))
                    elif kind == "xn":
                        _, l, hd = step
                        b = hd % 2
                        dve.wait_ge(*at(ACT, ("xs", l, hd)))
                        link(V.reciprocal(xrec[b], xden[b]))
                        V.tensor_scalar(xpr[b][:, 0, :], xpr[b][:, 0, :], xrec[b][:, 0:1], None, ALU.mult)
                        done(V.tensor_scalar(xpr[b][:, 1, :], xpr[b][:, 1, :], xrec[b][:, 1:2], None, ALU.mult))
                    elif kind == "xp":
                        _, l, hd = step
                        b = hd % 2
                        if hd >= 2:
                            dve.wait_ge(*at(PE, ("xo", l, hd - 2)))
                        done(V.tensor_copy(xpT[b], psum(step).rearrange("p (a b) -> p a b", a=NT)))
                    elif kind == "route":
                        done(V.tensor_copy(lgT[0:E, :], psum(step)[0:E, 0:T]))
                    elif kind == "route_t":
                        link(V.tensor_copy(lg, psum(step)[:, 0:NT * E].rearrange("p (a b) -> p a b", a=NT)))
                        link(V.tensor_reduce(s1, lg, AX, ALU.max))
                        done(V.tensor_tensor(lg, lg, s1.unsqueeze(2).to_broadcast([P, NT, E]), ALU.subtract))
                    elif kind == "route_soft":
                        dve.wait_ge(*at(ACT, step))
                        link(V.tensor_reduce(s1, sc, AX, ALU.add))
                        link(V.reciprocal(s2, s1))
                        link(V.tensor_tensor(sc, sc, s2.unsqueeze(2).to_broadcast([P, NT, E]), ALU.mult))
                        dve.wait_ge(vec_in, 48)
                        done(V.tensor_tensor(sel, sc, rb[:].unsqueeze(1).to_broadcast([P, NT, E]), ALU.add))
                    elif kind == "route_top":
                        _, l = step
                        dve.wait_ge(*at(DVE, ("route_soft", l)))
                        four = sel.rearrange("p t (g a b) -> p (t g) a b", g=G, b=2)
                        V.tensor_tensor(hi, four[:, :, :, 0], four[:, :, :, 1], ALU.max)
                        link(V.tensor_tensor(lo, four[:, :, :, 0], four[:, :, :, 1], ALU.min))
                        fl = lambda v: v.rearrange("p a b -> p (a b)")
                        V.tensor_tensor(fl(g1), hi[:, :, 0], hi[:, :, 1], ALU.max)
                        V.tensor_tensor(fl(g2), hi[:, :, 0], hi[:, :, 1], ALU.min)
                        link(V.tensor_tensor(fl(g3), lo[:, :, 0], lo[:, :, 1], ALU.max))
                        link(V.tensor_tensor(g2, g2, g3, ALU.max))
                        link(V.tensor_tensor(g1, g1, g2, ALU.add))

                        def first_max(mark, v, weights, n, top, tmp):
                            link(V.tensor_reduce(top, v, AX, ALU.max))
                            link(V.tensor_tensor(tmp, v, top.unsqueeze(2).to_broadcast([P, NT, n]), ALU.is_equal))
                            link(V.tensor_tensor(tmp, tmp, weights, ALU.mult))
                            link(V.tensor_reduce(top, tmp, AX, ALU.max))
                            link(V.tensor_tensor(mark, tmp, top.unsqueeze(2).to_broadcast([P, NT, n]), ALU.is_equal))

                        first_max(g4, g1, gidx[:], G, s1, g3)
                        inside = fl(g4).unsqueeze(2).to_broadcast([P, NT * G, E // G])
                        by4 = lambda v: v.rearrange("p t (g a) -> p (t g) a", g=G)
                        V.tensor_tensor(by4(ta), by4(sel), inside, ALU.mult)
                        link(V.tensor_scalar(g3, g4, 1.0, -NEG, ALU.subtract, ALU.mult))
                        link(V.tensor_tensor(by4(ta), by4(ta), fl(g3).unsqueeze(2).to_broadcast([P, NT * G, E // G]), ALU.add))
                        first_max(oh1, ta, eidx[:], E, s1, tb)
                        link(V.scalar_tensor_tensor(ta, oh1, NEG, ta, ALU.mult, ALU.add))
                        first_max(tc, ta, eidx[:], E, s1, tb)
                        done(V.tensor_tensor(oh1, oh1, tc, ALU.add))
                    elif kind == "weights":
                        _, l = step
                        dve.wait_ge(*at(DVE, ("route_top", l)))
                        link(V.tensor_tensor(tb, sc, oh1, ALU.mult))
                        link(V.tensor_reduce(s1, tb, AX, ALU.add))
                        link(V.reciprocal(s2, s1))
                        done(V.tensor_tensor(gates, tb, s2.unsqueeze(2).to_broadcast([P, NT, E]), ALU.mult))
                    elif kind == "place":
                        _, l = step
                        pv = psum(step)[:, 0:NT * E].rearrange("p (a b) -> p a b", a=NT)
                        V.scalar_tensor_tensor(posm, pv, 1.0, oh1, ALU.add, ALU.mult)
                        done(V.tensor_reduce(maxc[:, 0:1], psum(step)[:, NT * E:(NT + 1) * E], AX, ALU.max))
                    elif kind == "sc_h":
                        _, half, m = step
                        dve.wait_ge(*at(ACT, ("sc_c", half, m)))
                        u = sc_u[:, 2 * m:2 * m + 2, :]
                        link(V.tensor_tensor(u, u, psum(step).rearrange("p (a b) -> p a b", a=2), ALU.mult))
                        for i in range(2):
                            c = 2 * m + i

                            def tap(k):
                                return par[:, 0, 48 + k * KD + 4 * half + c:48 + k * KD + 4 * half + c + 1]
                            src, dst = sc_u[:, c, :], sc_a[:, c, :]
                            link(V.tensor_scalar(dst, src, tap(STAPS - 1), None, ALU.mult))
                            for k in range(1, STAPS):
                                ins = V.scalar_tensor_tensor(dst[:, k:], src[:, :T - k], tap(STAPS - 1 - k), dst[:, k:],
                                                             ALU.mult, ALU.add)
                                if k < STAPS - 1 or i == 0:
                                    link(ins)
                        done(ins)
                    elif kind == "sc_b":
                        _, half, m = step
                        dve.wait_ge(*at(DVE, ("sc_h", half, m)))
                        done(V.tensor_tensor(sc_y[:, 4 * half + 2 * m:4 * half + 2 * m + 2, :],
                                             psum(step).rearrange("p (a b) -> p a b", a=2),
                                             sc_a[:, 2 * m:2 * m + 2, :], ALU.mult))
                    else:
                        raise AssertionError(kind)

        @block.tensor
        def _(pe):
            M = nc.tensor.matmul

            def done(ins):
                ins.then_inc(steps_sem[PE], 1)

            def arrived(step):
                for n in slot_reader[step]:
                    pe.wait_ge(slot_full[n % RING], 16 * fill_no[n])
                return wide(ring[:, slot_reader[step][-1] % RING, :])

            def chain(dst, pairs):
                for i, (a, b) in enumerate(pairs):
                    ins = M(dst, a, b, start=i == 0, stop=i == len(pairs) - 1)
                return ins

            def heads(dst, stationary, moving):
                for hd in range(NH):
                    ins = M(dst[:, hd * P:(hd + 1) * P], stationary(hd), moving(hd), start=True, stop=True)
                return ins

            def transposes(dst, srcs):
                for i, src in enumerate(srcs):
                    ins = nc.tensor.transpose(dst[:, i * P:(i + 1) * P], src, ident[:])
                return ins

            def by_feature(step, m, lhs, rhs):
                w = arrived(step)
                b = ps[:, bank_of[step], :]
                for i in range(2):
                    c = (2 * (m % 2) + i) * P
                    ins = chain(b[:, i * T:(i + 1) * T], [(w[:, k, c:c + P], rhs[:, k, :]) for k in range(KD)])
                done(ins)

            def by_token(step, src, t):
                w = arrived(step)
                done(chain(ps[:, bank_of[step], :], [(src[:, k, t * P:(t + 1) * P], w[:, k, :]) for k in range(KD)]))

            def early(s):
                return range(NH, NH + 3) if s == 0 else range(4)

            def have_hT(l, s):
                for t in range(NT):
                    pe.wait_ge(*at(ACT, ("hT", l, s, t, 0)))
                    pe.wait_ge(*at(DVE, ("hT", l, s, t, 1)))

            def slot_of(l, part, j):
                s = ring[:, ring_at(l, part, j), :]
                return tall(s) if part == 2 else wide(s)

            def gather(half, ):
                return chain(ps[:, BK[f"X{half}"], :],
                             [(onehot[:, t].rearrange("p a b -> p (a b)"), hn[:, t, half * BANK:(half + 1) * BANK])
                              for t in range(NT)])

            def gather_T(half):
                return transposes(ps[:, BK[f"XT{half}"], :],
                                  [xg[:, (4 * half + k) * P:(4 * half + k + 1) * P] for k in range(4)])

            def up_product(l, part, odd=False):
                w = [wide(odd_gate[:, j, :]) if odd and part == 0 else slot_of(l, part, j) for j in range(2)]
                b = ps[:, BK["GU"[part]], :]
                for k in range(KD):
                    for j in range(2):
                        r = slice(j * SLOTS, (j + 1) * SLOTS)
                        ins = M(b[r, :], xgT[:, k, r], w[j][:, k, :], start=k == 0, stop=k == KD - 1)
                return ins

            def down_product(l, half):
                b = ps[:, BK[f"O{half}"], :]
                for k in range(4):
                    for j in range(2):
                        r = slice(j * SLOTS, (j + 1) * SLOTS)
                        ins = M(b[r, :], hidT[:, k, r], slot_of(l, 2, j)[:, k, half * BANK:(half + 1) * BANK],
                                start=k == 0, stop=k == 3)
                return ins

            def hidden_T():
                return transposes(ps[:, BK["HT"], :], [hid[:, k * P:(k + 1) * P] for k in range(4)])

            def gated_T():
                return transposes(ps[:, BK["PT"], :], [gated[:, t].rearrange("p a b -> p (a b)") for t in range(NT)])

            def scatter(i):
                t, half = i // 2, i % 2
                return M(ps[:, BK[f"Y{i}"], :], gatedT[:, t * P:(t + 1) * P], outp[:, half * BANK:(half + 1) * BANK],
                         start=True, stop=True)

            def experts(l):
                def weights(part, n):
                    for j in range(2):
                        pe.wait_ge(slot_full[ring_at(l, part, j)], 16 * (n + (uses_before[l, part, j] + 1)))

                def gate_weights(odd, turn):
                    if odd:
                        for j in range(2):
                            pe.wait_ge(odd_full[j], 16 * (turn + (l * (PAIRS // 2) + 1)))
                    else:
                        weights(0, turn)

                def gathered(p):
                    pe.wait_ge(ex_dve, n_dve(l, "onehot", p))
                    if not first(p):
                        pe.wait_ge(ex_act, n_act(l, "XT0", p - 1))
                        pe.wait_ge(ex_dve, n_dve(l, "XT1", p - 1))
                    gather(0).then_inc(ex_pe, 1)
                    gather(1).then_inc(ex_pe, 1)

                def gathered_T(p):
                    pe.wait_ge(ex_act, n_act(l, "X0", p))
                    pe.wait_ge(ex_dve, n_dve(l, "X1", p))
                    gather_T(0).then_inc(ex_pe, 1)
                    gather_T(1).then_inc(ex_pe, 1)

                def scattered(p):
                    pe.wait_ge(ex_act, n_act(l, "O1", p))
                    pe.wait_ge(ex_dve, n_dve(l, "PT", p))
                    for i in range(4):
                        scatter(i).then_inc(ex_pe, 1)

                def pair(p, odd, turn):
                    pe.wait_ge(ex_act, n_act(l, "XT0", p))
                    pe.wait_ge(ex_dve, n_dve(l, "XT1", p))
                    gate_weights(odd, turn)
                    up_product(l, 0, odd).then_inc(ex_pe, 1)
                    weights(1, p)
                    up_product(l, 1).then_inc(ex_pe, 1)
                    if not first(p):
                        scattered(p - 1)
                    if not last(p):
                        gathered(p + 1)
                    pe.wait_ge(ex_dve, n_dve(l, "hid", p))
                    if not first(p):
                        pe.wait_ge(ex_dve, n_dve(l, "Y0", p - 1))
                    hidden_T().then_inc(ex_pe, 1)
                    if not first(p):
                        pe.wait_ge(ex_dve, n_dve(l, "Y1", p - 1))
                    gated_T().then_inc(ex_pe, 1)
                    if not last(p):
                        gathered_T(p + 1)
                    pe.wait_ge(ex_act, n_act(l, "HT", p))
                    for half in range(2):
                        if half:
                            for j in range(2):
                                pe.wait_ge(right_full[j], 16 * (p + (l * PAIRS + 1)))
                        else:
                            weights(2, p)
                        if not first(p):
                            pe.wait_ge(ex_dve, n_dve(l, f"Y{2 + half}", p - 1))
                        down_product(l, half).then_inc(ex_pe, 1)

                for s in segments[l][-12:]:
                    if PE in takes(s):
                        pe.wait_ge(*at(empties(s), s))
                gathered(0)
                gathered_T(0)
                pair(0, False, 0)
                with pe.Fori(0, PAIRS // 2 - 1) as q:
                    pair(2 * q + 1, True, q)
                    pair(2 * q + 2, False, q + 1)
                pair(PAIRS - 1, True, PAIRS // 2 - 1)
                scattered(PAIRS - 1)
                pe.wait_ge(rounds_known, l + 1)
                nr = pe.value_load(rounds[0:1, 0:1], min_val=1, max_val=4)
                with pe.If(nr > 1):
                    o = of[l]
                    pe.wait_ge(ex_dve, (l + 1) * DVE_ALL)
                    with pe.Fori(1, nr) as b:
                        with pe.Fori(0, PAIRS) as p:
                            i = (b - 1) * PAIRS + p
                            n_d = i * 9 + 1
                            pe.wait_ge(o["dve"], n_d + 2)
                            gather(0)
                            gather(1).then_inc(o["pe"], 1)
                            pe.wait_ge(o["dve"], n_d + 3)
                            gather_T(0)
                            gather_T(1).then_inc(o["pe"], 1)
                            pe.wait_ge(o["dve"], n_d + 4)
                            gated_T().then_inc(o["pe"], 1)
                            pe.wait_ge(o["dve"], n_d + 5)
                            pe.wait_ge(o["slots"], (i + 1) * 96)
                            up_product(l, 0)
                            up_product(l, 1).then_inc(o["pe"], 1)
                            pe.wait_ge(o["dve"], n_d + 6)
                            hidden_T().then_inc(o["pe"], 1)
                            pe.wait_ge(o["dve"], n_d + 7)
                            down_product(l, 0)
                            down_product(l, 1).then_inc(o["pe"], 1)
                            pe.wait_ge(o["dve"], n_d + 8)
                            for k in range(4):
                                ins = scatter(k)
                            ins.then_inc(o["pe"], 1)
                    pe.wait_ge(o["end"], 1)

            for n, seg in enumerate(segments):
                if n:
                    experts(n - 1)
                for step in seg:
                    if PE not in takes(step):
                        continue
                    kind = step[0]
                    b = ps[:, bank_of[step], :]
                    prev = before[step]
                    if prev == "experts":
                        bank = bank_of[step]
                        pe.wait_ge(*{0: (ex_act, n_act(n - 1, "silu", PAIRS - 1)), 1: (ex_dve, n_dve(n - 1, "hid", PAIRS - 1)),
                                     2: (ex_act, n_act(n - 1, "XT0", PAIRS - 1)), 3: (ex_dve, n_dve(n - 1, "XT1", PAIRS - 1)),
                                     }.get(bank, (ex_dve, n * DVE_ALL)))
                    elif prev is not None:
                        pe.wait_ge(*at(empties(prev), prev))
                    if kind == "params":
                        pe.wait_ge(rows_in, 64)
                        rows = TAPS * 12 + STAPS * KD
                        nc.tensor.transpose(b[:, 0:rows], par_rows[0:rows, 0, :], ident[0:rows, 0:rows])
                        done(nc.tensor.transpose(b[:, P:P + 96], par_rows[0:96, 1, :], ident[0:96, 0:96]))
                    elif kind == "xT":
                        _, t, g = step
                        pe.wait_ge(*at(POOL, ("ident",)))
                        pe.wait_ge(x_in[t], 16)
                        done(transposes(b, [h[:, t, (4 * g + k) * P:(4 * g + k + 1) * P] for k in range(4)]))
                    elif kind == "memT":
                        _, t, g = step
                        pe.wait_ge(mem_in, 16)
                        done(transposes(b, [memtok[:, t, (4 * g + k) * P:(4 * g + k + 1) * P] for k in range(4)]))
                    elif kind == "ba":
                        pe.wait_ge(wba_in, 16)
                        for t in range(NT):
                            ins = chain(b[:, t * 2 * NH:(t + 1) * 2 * NH],
                                        [(hT[:, k, t * P:(t + 1) * P], wba[:, k, :]) for k in range(KD)])
                        done(ins)
                    elif kind == "qkv":
                        if step == ("qkv", 0, 0):
                            for t in range(NT):
                                pe.wait_ge(*at(ACT, ("xT", t, 0)))
                                pe.wait_ge(*at(DVE, ("xT", t, 1)))
                        if step == ("qkv", 0, 1):
                            pe.wait_ge(first_full, 16)
                        by_feature(step, step[2], None, hT)
                    elif kind in ("qd", "kd"):
                        by_feature(step, step[1], None, hT)
                    elif kind in ("z", "vd"):
                        by_token(step, hT, step[1])
                    elif kind == "sumsq":
                        pe.wait_ge(*at(POOL, step))
                        for t in range(NT):
                            for i in range(8):
                                ins = M(b[:, 8 * t + i:8 * t + i + 1], sq[:, i, t * P:(t + 1) * P], ones[:, 0:1],
                                        start=True, stop=True)
                        done(ins)
                    elif kind == "cumsum":
                        pe.wait_ge(*at(POOL, ("masks",)))
                        pe.wait_ge(*at(DVE, ("gates",)))
                        done(M(b[:, 0:NT * NH], upto[:], graw.rearrange("p a b -> p (a b)"), start=True, stop=True))
                    elif kind == "rowg":
                        t = step[1]
                        done(heads(b, lambda hd: graw[:, t, hd:hd + 1].to_broadcast([P, P]), lambda hd: upto[:]))
                    elif kind == "rowh":
                        t = step[1]
                        pe.wait_ge(*at(DVE, ("cols",)))
                        done(heads(b, lambda hd: hcol[:, t, hd:hd + 1].to_broadcast([P, P]), lambda hd: ident[:]))
                    elif kind == "gram":
                        t = step[1]
                        kv = lambda hd: qkv[:, NH + hd, t * P:(t + 1) * P]
                        done(heads(b, kv, kv))
                    elif kind == "qk":
                        t = step[1]
                        done(heads(b, lambda hd: qkv[:, NH + hd, t * P:(t + 1) * P],
                                   lambda hd: qkv[:, hd, t * P:(t + 1) * P]))
                    elif kind == "inv0":
                        t = step[1]
                        pe.wait_ge(*at(POOL, ("blk", 0, t)))
                        done(transposes(b, [Bm[:, t, hd, :] for hd in range(NH)]))
                    elif kind == "ktok":
                        done(transposes(b, [qkv[:, NH + hd, 0:P] for hd in range(NH)]))
                    elif kind == "vtok":
                        t = step[1]
                        pe.wait_ge(*at(ACT, ("qkv", 2, 1)))
                        done(transposes(b, [qkv[:, 2 * NH + hd, t * P:(t + 1) * P] for hd in range(NH)]))
                    elif kind == "inv_v":
                        _, k, t = step
                        pe.wait_ge(*at(POOL, ("blk", k, t)))
                        pe.wait_ge(*at(DVE, ("inv0", t) if k == 1 else ("inv_u", k - 1, t)))
                        done(heads(b, lambda hd: Bm[:, t, hd, :], lambda hd: U[:, t, hd, :]))
                    elif kind == "inv_u":
                        _, k, t = step
                        pe.wait_ge(*at(ACT, ("inv_v", k, t)))
                        pe.wait_ge(*at(DVE, ("inv0", t) if k == 1 else ("inv_x", k - 1, t)))
                        done(heads(b, lambda hd: X[:, t, hd, :], lambda hd: Vt[:, t, hd, :]))
                    elif kind == "inv_x":
                        _, k, t = step
                        done(heads(b, lambda hd: Vt[:, t, hd, :], lambda hd: X[:, t, hd, :]))
                    elif kind == "vnew":
                        _, c = step
                        pe.wait_ge(*at(DVE, ("inv_u", 6, c)))
                        if c:
                            pe.wait_ge(*at(DVE, ("kstate",)))
                        else:
                            pe.wait_ge(*at(ACT, ("vtok", 0)))
                        rhs = r1 if c else vb[:, 0]
                        done(heads(b, lambda hd: U[:, c, hd, :], lambda hd: rhs[:, hd, :]))
                    elif kind == "state":
                        pe.wait_ge(*at(ACT, ("vnew", 0)))
                        done(heads(b, lambda hd: ktok[:, hd, :], lambda hd: vn[:, 0, hd, :]))
                    elif kind == "kstate":
                        pe.wait_ge(*at(ACT, ("state",)))
                        done(heads(b, lambda hd: qkv[:, NH + hd, P:T], lambda hd: st[:, hd, :]))
                    elif kind == "qstate":
                        done(heads(b, lambda hd: qkv[:, hd, P:T], lambda hd: st[:, hd, :]))
                    elif kind == "o":
                        c = step[1]
                        pe.wait_ge(*at(ACT, ("vnew", c)))
                        pe.wait_ge(*at(DVE, ("qk", c)))
                        done(heads(b, lambda hd: DU[:, c, hd, :], lambda hd: vn[:, c, hd, :]))
                    elif kind == "oT":
                        t = step[1]
                        pe.wait_ge(*at(DVE, ("onorm", t)))
                        done(transposes(b, [o_sb[:, t, hd, :] for hd in range(NH)]))
                    elif kind == "d_scores":
                        hd = step[1]
                        m = hd // 4
                        pe.wait_ge(*at(ACT, ("qd", m)))
                        pe.wait_ge(*at(ACT, ("kd", m)))
                        M(b[:, 0:T], qdT[:, hd // 2, P:T], kdz[:, hd, :], start=True, stop=True)
                        done(M(b[:, T:T + P], qdT[:, hd // 2, 0:P], kdz[:, hd, 0:P], start=True, stop=True))
                    elif kind == "d_pT":
                        hd = step[1]
                        pe.wait_ge(*at(DVE, ("d_probs", hd)))
                        v = dp[hd % 2]
                        done(transposes(b, [v[:, 2 * P:3 * P], v[:, 0:P], v[:, P:2 * P]]))
                    elif kind == "d_pv":
                        hp = step[1]
                        for j in range(2):
                            hd = 2 * hp + j
                            pe.wait_ge(*at(ACT, ("d_pT", hd)))
                            if hp == 0:
                                pe.wait_ge(*at(DVE, ("vd", j)))
                            r = slice(j * AH, (j + 1) * AH)
                            M(b[r, 0:T], vd[:, 0, hd * AH:(hd + 1) * AH], dpT[j][:, 0:T], start=True, stop=False)
                            ins = M(b[r, P:T], vd[:, 1, hd * AH:(hd + 1) * AH], dpT[j][:, T:T + P], start=False, stop=True)
                        done(ins)
                    elif kind == "y_first":
                        _, l, s, half, t = step
                        pe.wait_ge(*at(ACT, ("xo", l, 1) if s else ("d_pv", 2)))
                        w = arrived(("y", l, s, half, t))
                        src = xoT if s else catT
                        for k in early(s):
                            ins = M(b, src[:, k, t * P:(t + 1) * P], w[:, k, :], start=k == early(s)[0], stop=False)
                        done(ins)
                    elif kind == "y" and ("y_first", *step[1:]) in count:
                        _, l, s, half, t = step
                        if s:
                            pe.wait_ge(*at(ACT, ("xo", l, XH - 1)))
                        else:
                            pe.wait_ge(*at(DVE, ("oT", t)))
                            pe.wait_ge(*at(ACT, ("d_pv", 3)))
                        w = arrived(step)
                        src = xoT if s else catT
                        late = [k for k in range(KD) if k not in early(s)]
                        for k in late:
                            ins = M(b, src[:, k, t * P:(t + 1) * P], w[:, k, :], start=False, stop=k == late[-1])
                        done(ins)
                    elif kind == "y":
                        _, l, s, half, t = step
                        if (l, s) == (0, 0):
                            src = catT
                        elif s == 0:
                            src = sc_y
                            pe.wait_ge(*at(DVE, ("sc_b", 1, 1)))
                        else:
                            src = xoT
                            pe.wait_ge(*at(ACT, ("xo", l, XH - 1)))
                        by_token(step, src, t)
                    elif kind == "hT":
                        _, l, s, t, g = step
                        pe.wait_ge(*at(DVE, ("ln_norm", l, s, t)))
                        done(transposes(b, [hn[:, t, (4 * g + k) * P:(4 * g + k + 1) * P] for k in range(4)]))
                    elif kind == "xk":
                        for t in range(NT):
                            pe.wait_ge(*at(ACT, ("memT", t, 0)))
                            pe.wait_ge(*at(DVE, ("memT", t, 1)))
                        by_feature(step, step[2], None, memT)
                    elif kind == "xv":
                        by_token(step, memT, step[3])
                    elif kind == "xq":
                        have_hT(step[1], 0)
                        by_feature(step, step[2], None, hT)
                    elif kind == "xs":
                        _, l, hd = step
                        pe.wait_ge(*at(ACT, ("xk", l, hd)))
                        pe.wait_ge(*at(ACT, ("xq", l, hd)))
                        for t in range(NT):
                            ins = chain(b[:, t * T:(t + 1) * T],
                                        [(xqT[:, 2 * hd + i, t * P:(t + 1) * P], xkT[:, 2 * hd + i, :]) for i in range(2)])
                        done(ins)
                    elif kind == "xp":
                        _, l, hd = step
                        pe.wait_ge(*at(DVE, ("xn", l, hd)))
                        v = xpr[hd % 2]
                        done(transposes(b, [v[:, t, mt * P:(mt + 1) * P] for mt in range(NT) for t in range(NT)]))
                    elif kind == "xo":
                        _, l, hd = step
                        pe.wait_ge(*at(DVE, ("xp", l, hd)))
                        for half in range(2):
                            for t in range(NT):
                                pe.wait_ge(*at(DVE, ("xv", l, half, t)))
                        for i in range(2):
                            c = (2 * hd + i) * P
                            ins = chain(b[:, i * T:(i + 1) * T],
                                        [(xv[:, mt, c:c + P], xpT[hd % 2][:, mt, :]) for mt in range(NT)])
                        done(ins)
                    elif kind == "route":
                        l = step[1]
                        pe.wait_ge(vec_in, 48)
                        for t in range(NT):
                            pe.wait_ge(*at(ACT, ("hT", l, 1, t, 0)))
                            pe.wait_ge(*at(DVE, ("hT", l, 1, t, 1)))
                            ins = chain(b[0:E, t * P:(t + 1) * P], [(wr[:, k, :], hT[:, k, t * P:(t + 1) * P]) for k in range(KD)])
                        done(ins)
                    elif kind == "route_t":
                        pe.wait_ge(*at(DVE, ("route", step[1])))
                        for t in range(NT):
                            ins = nc.tensor.transpose(b[:, t * E:(t + 1) * E], lgT[0:E, t * P:(t + 1) * P], ident[0:E, 0:E])
                        done(ins)
                    elif kind == "place":
                        pe.wait_ge(*at(DVE, ("route_top", step[1])))
                        M(b[:, 0:2 * E], below[:], oh1.rearrange("p a b -> p (a b)"), start=True, stop=False)
                        M(b[:, E:2 * E], ones[:], oh1[:, 0, :], start=False, stop=True)
                        done(chain(b[:, 2 * E:3 * E], [(ones[:], oh1[:, 0, :]), (ones[:], oh1[:, 1, :])]))
                    elif kind in ("sc_c", "sc_h", "sc_b"):
                        have_hT(0, 2)
                        by_feature(step, step[2], None, hT)
                    else:
                        raise AssertionError(kind)


_INS = ["x", "mem", "ab_w_in", "ab_conv_w", "ab_a_log", "ab_dt_bias", "ab_norm_w", "ab_w_out", "sc_w_in", "sc_conv_w",
        "sc_w_out", "xa_w_q", "xa_w_kv", "xa_w_o", "router_w", "router_b", "moe_w_gate", "moe_w_up", "moe_w_down",
        "ln_g", "ln_b"]


def kernel(**inputs):
    import concourse.bacc as bacc
    from concourse.bass_utils import run_bass_kernel_spmd

    nc = bacc.Bacc("TRN2", target_bir_lowering=False, num_devices=1)
    arrays, args = {}, []
    for name in _INS:
        a = np.ascontiguousarray(inputs[name])
        arrays[f"in_{name}"] = a
        args.append(nc.dram_tensor(f"in_{name}", a.shape, mybir.dt.from_np(a.dtype), kind="ExternalInput").ap())
    shape = inputs["x"].shape
    result = nc.dram_tensor("out_h", shape, F32, kind="ExternalOutput").ap()
    trunk_kernel(nc, *args, result)
    r = run_bass_kernel_spmd(nc, [arrays], core_ids=[0])
    return r.results[0]["out_h"]
```

```python
from contextlib import ExitStack

import numpy as np

import concourse.bass as bass
from concourse import mybir

F32 = mybir.dt.float32
BF16 = mybir.dt.bfloat16
I32 = mybir.dt.int32
R32 = mybir.dt.float32r
ALU = mybir.AluOpType
ACTF = mybir.ActivationFunctionType
AX = mybir.AxisListType.X

P = 128
PE, ACT, DVE, POOL = "pe", "act", "dve", "pool"
BANKS = 8
BANK = 512
NEG = -1.0e30
DMA_SCRATCH = 2048


def is_split(step):
    kind, l = step[0], step[1] if len(step) > 1 else 0
    if kind == "qkv":
        return step != ("qkv", 0, 0)
    if kind == "xk":
        return l == 0
    if kind == "xq":
        return step[2] > 0
    return kind in ("qd", "kd", "vd", "xv", "sc_c", "sc_h", "sc_b")


def x_split(source, l):
    return [("x_split", source, l, g) for g in range(2)]


def with_weight_splits(steps):
    out, before = [], []
    for s in steps:
        if is_split(s):
            ahead = before[-2] if len(before) > 1 and not is_split(before[-2]) else before[-1]
            out.insert(out.index(ahead), ("w_split", s))
        if s[0] in ("qkv", "qd", "kd", "vd", "xk", "xv", "xq", "sc_c", "sc_h", "sc_b", "y"):
            before.append(s)
        out.append(s)
    return out


def trunk_steps():
    def transposed(kind, *who):
        return [(kind, *who, t, g) for t in range(2) for g in range(2)]

    def normed(l, s):
        out = []
        for t in range(2):
            out += [("ln_stats", l, s, t), ("ln_rstd", l, s, t), ("ln_norm", l, s, t)]
        for t in range(2):
            out += [("hT", l, s, t, g) for g in range(2)]
        return out + [("ln_h", l, s, t) for t in range(2)]

    def cross_kv(l):
        return ([("xk", l, m) for m in range(4)] + [("xv", l, half, t) for half in range(2) for t in range(2)])

    def cross(l):
        return [("xq", l, 0), ("xq", l, 1), ("xs", l, 0), ("xq", l, 2), ("xn", l, 0), ("xs", l, 1), ("xp", l, 0),
                ("xq", l, 3), ("xo", l, 0), ("xn", l, 1), ("xs", l, 2), ("xp", l, 1), ("xs", l, 3), ("xo", l, 1),
                ("xn", l, 2), ("xp", l, 2), ("y_first", l, 1, 0, 0), ("xn", l, 3), ("xo", l, 2), ("xp", l, 3),
                ("y_first", l, 1, 1, 0), ("xo", l, 3)]

    def projected(l, s):
        return [("y", l, s, half, t) for half in range(2) for t in range(2)]

    def projected_normed(l, s, *between):
        def ln(t):
            return [("ln_stats", l, s, t), ("ln_rstd", l, s, t), ("ln_norm", l, s, t)]

        def hT(t):
            return [("hT", l, s, t, g) for g in range(2)]
        return ([("y", l, s, 0, 0), ("y", l, s, 1, 0)] + ln(0) + [("y", l, s, 0, 1)] + hT(0) + [("y", l, s, 1, 1)] + ln(1)
                + list(between) + hT(1) + [("ln_h", l, s, t) for t in range(2)])

    a = [("ident",)] + transposed("xT") + [("masks",), ("params",)] + x_split("x", 0)
    a += [("qkv", 0, 0), ("ba",), ("qkv", 0, 1), ("silu", 0, 0), ("gates",), ("qkv", 1, 0), ("silu", 0, 1), ("qkv", 1, 1),
          ("silu", 1, 0), ("qkv", 2, 0), ("silu", 1, 1), ("cumsum",), ("qkv", 2, 1), ("silu", 2, 0), ("qd", 0),
          ("silu", 2, 1), ("levels", 0), ("sumsq",), ("cols",), ("qd", 1), ("levels", 1), ("vd", 0), ("levels", 2),
          ("vd", 1), ("levels", 3), ("kd", 0), ("kd", 1)]
    a += [("rowg", t) for t in range(2)] + [("rowh", t) for t in range(2)]
    a += [("gram", t) for t in range(2)] + [("qk", t) for t in range(2)]
    a += [("blk", 0, t) for t in range(2)]
    a += [("ktok",)] + [("vtok", t) for t in range(2)] + [("inv0", t) for t in range(2)]
    memT = transposed("memT")
    heads = [[("d_scores", 0)],
             [("d_probs", 0), ("d_scores", 1)] + memT[0:2],
             [("d_pT", 0), ("d_probs", 1), ("d_scores", 2)] + memT[2:4],
             [("d_pT", 1), ("d_probs", 2), ("d_scores", 3), ("d_pv", 0)],
             [("d_pT", 2), ("d_probs", 3), ("d_scores", 4)],
             [("d_pT", 3), ("d_probs", 4), ("d_scores", 5), ("d_pv", 1)]]
    for k in range(1, 7):
        a += [("blk", k, t) for t in range(2)]
        a += [("inv_v", k, t) for t in range(2)]
        a += heads[k - 1]
        a += [("inv_u", k, t) for t in range(2)]
        if k < 6:
            a += [("inv_x", k, t) for t in range(2)]
    a += [("d_pT", 4), ("d_probs", 5), ("d_scores", 6), ("vnew", 0), ("state",), ("o", 0), ("kstate",), ("qstate",),
          ("d_pT", 5), ("d_probs", 6), ("osq", 0), ("z", 0), ("d_pv", 2), ("d_scores", 7), ("vnew", 1), ("d_pT", 6),
          ("o", 1), ("d_probs", 7), ("onorm", 0), ("osq", 1), ("z", 1), ("oT", 0), ("d_pT", 7), ("y_first", 0, 0, 0, 0),
          ("onorm", 1), ("d_pv", 3), ("y_first", 0, 0, 0, 1), ("oT", 1)]
    ln, kv = normed(0, 0), cross_kv(0)
    y = projected(0, 0)
    a += y[:1] + x_split("mem", 0) + y[1:] + ln[:6] + kv[:-1] + ln[6:] + kv[-1:] + x_split("xq", 0) + cross(0)
    a += projected_normed(0, 1, ("xk", 1, 0)) + [("route", 0), ("route_t", 0), ("route_soft", 0), ("xk", 1, 1),
                                                 ("route_top", 0), ("weights", 0), ("place", 0)]

    ln = normed(0, 2)
    b = ln[:6] + [("xk", 1, 2)] + ln[6:10] + x_split("sc", 0) + [("xk", 1, 3)] + ln[10:]
    for half in range(2):
        b += [(kind, half, m) for kind in ("sc_c", "sc_h", "sc_b") for m in range(2)]
    y = projected_normed(1, 0, ("xv", 1, 0, 0), ("xv", 1, 0, 1), ("xv", 1, 1, 0))
    b += y[:1] + x_split("mem", 1) + y[1:] + [("xv", 1, 1, 1)] + x_split("xq", 1)
    b += cross(1) + projected_normed(1, 1)
    b += [(kind, 1) for kind in ("route", "route_t", "route_soft", "route_top", "weights", "place")]

    c = [(kind, 1, 2, t) for kind in ("ln_stats", "ln_rstd") for t in range(2)] + [("last", t) for t in range(2)]
    return with_weight_splits(a), with_weight_splits(b), c


TAKES = {
    "ident": (POOL,), "masks": (POOL,), "levels": (DVE,), "silu": (ACT,), "last": (DVE,), "params": (PE, DVE), "ba": (PE, DVE), "gates": (DVE, ACT), "qkv": (PE, DVE),
    "sumsq": (POOL, PE, ACT), "cumsum": (PE, DVE), "cols": (DVE, ACT), "rowg": (PE, DVE, ACT), "rowh": (PE, DVE, ACT),
    "gram": (PE, DVE), "qk": (PE, DVE), "blk": (POOL,), "z": (PE, ACT), "inv0": (PE, DVE), "ktok": (PE, ACT),
    "vtok": (PE, ACT), "inv_v": (PE, ACT), "inv_u": (PE, DVE), "inv_x": (PE, DVE), "qd": (PE, ACT), "kd": (PE, ACT),
    "vd": (PE, DVE), "d_scores": (PE, DVE), "d_probs": (ACT, DVE), "d_pT": (PE, ACT), "d_pv": (PE, ACT),
    "vnew": (PE, ACT), "state": (PE, ACT), "kstate": (PE, DVE), "qstate": (PE, ACT), "o": (PE, DVE),
    "osq": (ACT,), "onorm": (DVE,), "oT": (PE, DVE), "y_first": (PE,), "y": (PE, DVE), "ln_stats": (DVE,), "ln_rstd": (POOL,), "ln_norm": (DVE,),
    "ln_h": (POOL,), "xk": (PE, ACT), "xv": (PE, DVE), "xq": (PE, ACT), "xs": (PE, DVE, ACT), "xn": (DVE,), "xp": (PE, DVE),
    "xo": (PE, ACT), "route": (PE, DVE), "route_t": (PE, DVE), "weights": (DVE,), "route_soft": (ACT, DVE), "route_top": (DVE,), "place": (PE, DVE),
    "x_split": (ACT, DVE), "w_split": (ACT, DVE), "sc_c": (PE, ACT), "sc_h": (PE, DVE), "sc_b": (PE, DVE),
}
EMPTIES = {"rowg": DVE, "rowh": DVE, "xs": ACT}


def takes(step):
    if step[0] == "w_split" and step[1][0] == "qkv":
        return (ACT, DVE, POOL)
    if step[0] in ("xT", "memT", "hT"):
        return (PE, ACT) if step[-1] == 0 else (PE, DVE)
    return TAKES[step[0]]


def empties(step):
    return EMPTIES.get(step[0]) or takes(step)[-1]


def trunk_kernel(nc, x, mem, ab_w_in, ab_conv_w, ab_a_log, ab_dt_bias, ab_norm_w, ab_w_out, sc_w_in, sc_conv_w,
                 sc_w_out, xa_w_q, xa_w_kv, xa_w_o, router_w, router_b, moe_w_gate, moe_w_up, moe_w_down,
                 ln_g, ln_b, out):
    _, T, D = x.shape
    NT = T // P
    KD = D // P
    DEPTH, E, _, F = moe_w_gate.shape
    NH = ab_a_log.shape[1]
    DH = ab_norm_w.shape[1]
    W = NH * DH
    NA = 8
    AH = W // NA
    XH = 4
    G = 4
    PAIRS = E // 2
    SLOTS = 64
    ALPHA = float((2 * DEPTH) ** 0.25)
    LN_EPS, RMS_EPS = 1e-5, 1e-6
    TAPS, STAPS = ab_conv_w.shape[1], sc_conv_w.shape[1]
    assert (T, D, DEPTH, E, F, NH, DH, NT) == (256, 1024, 2, 16, 512, 4, 128, 2)

    segments = trunk_steps()
    steps = [s for seg in segments for s in seg]
    count = {}
    totals = {e: 0 for e in (PE, ACT, DVE, POOL)}
    for s in steps:
        assert s not in count, s
        count[s] = {}
        for e in takes(s):
            totals[e] += 1
            count[s][e] = totals[e]
    bank_of, before = {}, {}
    for n, seg in enumerate(segments):
        filled = [s for s in seg if PE in takes(s) and s[0] != "y_first"]
        for i, s in enumerate(filled):
            bank_of[s] = i % BANKS
            before[s] = filled[i - BANKS] if i >= BANKS else None
            if before[s] is None and n:
                before[s] = "experts"
        for s in seg:
            if s[0] == "y_first":
                y = ("y", *s[1:])
                bank_of[s], before[s] = bank_of[y], before[y]
                assert seg.index(before[y]) < seg.index(s) < seg.index(y)

    split_steps = [s for s in steps if is_split(s)]
    split_no = {s: i for i, s in enumerate(split_steps)}

    def cols(w, c0):
        return w[:, c0:c0 + BANK].rearrange("(k p) n -> p k n", p=P)

    q0, z0, ba0, d0 = 0, 3 * W, 4 * W, 4 * W + 2 * NH
    slot_reader = {}
    stream = []

    def slot(src, *readers):
        for r in readers:
            slot_reader.setdefault(r, []).append(len(stream))
        stream.append((src, readers[-1]))

    def experts_slots(l):
        for _ in range(3 * E):
            stream.append(None)

    w_in = ab_w_in[0]
    slot(cols(w_in, 0), ("qkv", 0, 0), ("qkv", 0, 1))
    slot(cols(w_in, W), ("qkv", 1, 0), ("qkv", 1, 1))
    slot(cols(w_in, 2 * W), ("qkv", 2, 0), ("qkv", 2, 1))
    slot(cols(w_in, d0), ("qd", 0), ("qd", 1))
    slot(cols(w_in, d0 + 2 * W), ("vd", 0), ("vd", 1))
    slot(cols(w_in, d0 + W), ("kd", 0), ("kd", 1))
    slot(cols(w_in, z0), ("z", 0), ("z", 1))

    def out_slots(w, l, s):
        for half in range(2):
            slot(cols(w, half * BANK), ("y", l, s, half, 0), ("y", l, s, half, 1))

    def k_slot(l, m):
        slot(cols(xa_w_kv[l], m * BANK), ("xk", l, 2 * m), ("xk", l, 2 * m + 1))

    def v_slot(l, half):
        slot(cols(xa_w_kv[l], D + half * BANK), ("xv", l, half, 0), ("xv", l, half, 1))

    def q_slots(l):
        for m in range(2):
            slot(cols(xa_w_q[l], m * BANK), ("xq", l, 2 * m), ("xq", l, 2 * m + 1))

    out_slots(ab_w_out[0], 0, 0)
    k_slot(0, 0)
    k_slot(0, 1)
    v_slot(0, 0)
    v_slot(0, 1)
    q_slots(0)
    out_slots(xa_w_o[0], 0, 1)
    k_slot(1, 0)
    first_expert_slot = [len(stream)]
    experts_slots(0)
    k_slot(1, 1)
    for half in range(2):
        for kind, part in (("sc_c", 1), ("sc_h", 2), ("sc_b", 0)):
            slot(cols(sc_w_in[0], part * D + half * BANK), (kind, half, 0), (kind, half, 1))
    v_slot(1, 0)
    out_slots(sc_w_out[0], 1, 0)
    v_slot(1, 1)
    q_slots(1)
    out_slots(xa_w_o[1], 1, 1)
    first_expert_slot.append(len(stream))
    experts_slots(1)
    RING = 6

    with ExitStack() as ctx:
        def sb(name, shape, dt=F32):
            return ctx.enter_context(nc.sbuf_tensor(name, shape, dt))

        def sem(name):
            return ctx.enter_context(nc.semaphore(name))

        def shared(name, shape, dt=F32):
            with nc.sbuf_tensor(name, shape, dt) as v:
                return v

        ps = ctx.enter_context(nc.psum_tensor("ps", [P, BANKS, BANK], F32))

        ring = shared("ring", [P, RING, KD * BANK])
        ring_low = [sb(f"ring_low{i}", [P, KD * BANK], R32) for i in range(RING)]
        h = sb("h", [P, NT, D])
        hn = sb("hn", [P, NT, D])
        hT = sb("hT", [P, KD, T])
        memT = sb("memT", [P, KD, T])
        gain = sb("gain", [P, 2, D])
        ident = sb("ident", [P, P])
        ones = sb("ones", [P, P])
        upto = sb("upto", [P, P])
        below = sb("below", [P, P])
        slot_no = sb("slot_no", [P, SLOTS])
        par_rows = sb("par_rows", [P, 2, P])
        par = sb("par", [P, 2, P])
        small = sb("small", [P, 16])
        wba = sb("wba", [P, KD, 2 * NH])
        wr = sb("wr", [P, KD, E])
        rb = sb("rb", [P, E])
        dtb = sb("dtb", [P, 2, NH])
        normw = sb("normw", [P, DH])
        ARENA = 19480
        arena = shared("arena", [P, ARENA])
        at_odd = ARENA - 2 * KD * BANK
        sb("arena_start", [P, at_odd])
        split = sb("split", [P, 2 * KD * BANK], R32)
        taken = [0]

        def carve(*shape, at=None):
            n = int(np.prod(shape))
            o = taken[0] if at is None else at
            taken[0] = max(taken[0], o + n)
            assert taken[0] <= ARENA, taken[0]
            v = arena[:, o:o + n]
            if len(shape) == 2:
                v = v.rearrange("p (a b) -> p a b", a=shape[0])
            if len(shape) == 3:
                v = v.rearrange("p (a b c) -> p a b c", a=shape[0], b=shape[1])
            return v

        qkv = carve(12, T)
        at_x = taken[0]
        X = carve(NT, NH, P)
        U = carve(NT, NH, P)
        sq = carve(8, T, at=at_x)
        st = carve(NH, P, at=at_x)
        r1 = carve(NH, P, at=at_x + NH * P)
        at_z = taken[0]
        zs = carve(NT, W)
        qdT = carve(4, T)
        vd = carve(NT, W)
        at_k = taken[0]
        ktok = carve(NH, P)
        vb = carve(NT, NH, P)
        dpT = [carve(384) for _ in range(2)]
        ba = carve(NT, 2 * NH)
        beta = carve(NT, NH)
        ga, gb, graw, gcol, hcol, bk, rk, qs, eg, egq, nc1 = (carve(NT, NH) for _ in range(11))
        lss = carve(NT, 8)
        glast, kdec, ea = (carve(NH) for _ in range(3))
        rms = carve(NT, NH)
        dmx = [carve(2) for _ in range(2)]
        dden = [carve(2) for _ in range(2)]
        drec = [carve(2) for _ in range(2)]
        assert taken[0] <= at_odd
        taken[0] = at_odd
        DU = carve(NT, NH, P)
        DL = carve(NT, NH, P)
        at_b = taken[0]
        Bm = carve(NT, NH, P)
        o_sb = carve(NT, NH, P, at=at_b)
        at_v = taken[0]
        Vt = carve(NT, NH, P)
        tmpo = carve(NH, P, at=at_v)
        sqo = carve(NH, P, at=at_v + NH * P)
        vn = DL
        dp = [carve(384) for _ in range(2)]
        kdz = gain.rearrange("p a b -> p (a b)").rearrange("p (a b) -> p a b", a=NA)
        catT = hn.rearrange("p a b -> p (a b)").rearrange("p (a b) -> p a b", a=KD)
        memtok = carve(NT, D)
        levels = sb("levels", [P, 7, P], BF16)
        times = sb("times", [P, 384], BF16)
        shut = sb("shut", [P, 384], BF16)
        shutU = dpT[0][:, 0:P]
        shutL = dpT[1][:, 0:P]
        di = carve(384, at=at_z).bitcast(I32)
        dj = carve(384, at=at_z + 384).bitcast(I32)
        df = carve(384, at=at_k)
        dg = carve(384, at=at_k + 384)

        taken[0] = 0
        xkT = carve(KD, T)
        xv = carve(NT, D)
        lnb = carve(NT, 2, 6)
        lnm = carve(NT, 4)
        at_sc = taken[0]
        xoT = carve(KD, T)
        xqT = carve(KD, T)
        xpr = [carve(NT, T) for _ in range(2)]
        xpT = [carve(NT, T) for _ in range(2)]
        xmx = [carve(NT) for _ in range(2)]
        xden = [carve(NT) for _ in range(2)]
        xrec = [carve(NT) for _ in range(2)]
        sc_y = carve(KD, T, at=at_sc)
        sc_u = carve(4, T, at=at_sc + KD * T)
        sc_a = carve(4, T, at=at_sc + (KD + 4) * T)
        taken[0] = at_sc
        onehot = carve(NT, 2, SLOTS)
        gated = carve(NT, 2, SLOTS)
        gatedT = carve(T)
        hidT = carve(4, P)
        silu = carve(F, at=KD * T)
        hid = carve(F, at=KD * T + F)
        outp = carve(D, at=KD * T + 2 * F)
        spare = hT[:].rearrange("p k t -> p (k t)")
        xgT = spare[:, 0:D].rearrange("p (k t) -> p k t", k=KD)
        lg = carve(NT, E)
        sc = carve(NT, E)
        sel = carve(NT, E)
        gates = carve(NT, E)
        ta, tb, tc, oh1, posm = (carve(NT, E) for _ in range(5))
        hi, lo = carve(NT * G, 2), carve(NT * G, 2)
        g1, g2, g3, g4 = (carve(NT, G) for _ in range(4))
        s1, s2 = carve(NT), carve(NT)
        maxc = carve(4)
        lgT = carve(T)
        assert taken[0] <= at_odd - KD * BANK, (taken[0], at_odd)
        odd_gate = carve(2, KD * BANK, at=at_odd)
        odd_up = carve(KD * BANK, at=at_odd - KD * BANK)
        x_high, x_low, w_high0, w_high1 = (
            split[:, i * KD * T:(i + 1) * KD * T].rearrange("p (k t) -> p k t", k=KD) for i in range(4))
        w_high = [w_high0, w_high1]
        gidx = sb("gidx", [P, NT, G])
        eidx = sb("eidx", [P, NT, E])
        rounds = sb("rounds", [P, 1], I32)
        nexp = sb("nexp", [P, 1])

        steps_sem = {PE: sem("pe_steps"), ACT: sem("act_steps"), DVE: sem("dve_steps"), POOL: sem("pool_steps")}
        dve_own, act_own, pool_own = sem("dve_own"), sem("act_own"), sem("pool_own")
        slot_full = [sem(f"slot_full{i}") for i in range(RING)]
        odd_full = [sem(f"odd_full{j}") for j in range(2)]
        odd_up_full = sem("odd_up_full")
        right_full = [sem(f"right_full{j}") for j in range(2)]
        gate_halfway = sem("gate_halfway")
        lower_full = [sem(f"lower_full{j}") for j in range(2)]
        odd_lower_full = [sem(f"odd_lower_full{j}") for j in range(2)]
        first_full = sem("first_full")
        x_in = [sem(f"x_in{t}") for t in range(NT)]
        mem_in, rows_in, wba_in, vec_in, gain_in = (
            sem(n) for n in ("mem_in", "rows_in", "wba_in", "vec_in", "gain_in"))
        decay_in = sem("decay_in")
        stored = sem("stored")
        rounds_known = sem("rounds_known")
        ex_pe, ex_act, ex_dve = sem("ex_pe"), sem("ex_act"), sem("ex_dve")
        of = [{n: sem(f"of{l}_{n}") for n in ("slots", "pe", "act", "dve", "shift", "end")} for l in range(DEPTH)]

        def split_cols(step):
            n = slot_reader[step][-1]
            c = step[-1] % 2 * T
            return n, wide(ring[:, n % RING, :])[:, :, c:c + T], wide(ring_low[n % RING][:])[:, :, c:c + T]

        def x_source(source):
            return memT if source == "mem" else hT

        def at(engine, step):
            return steps_sem[engine], count[step][engine]

        PE_PAIR, ACT_PAIR, DVE_PAIR = 12, 5, 9
        PE_ALL, ACT_ALL, DVE_ALL = PAIRS * PE_PAIR, PAIRS * ACT_PAIR, PAIRS * DVE_PAIR + 1

        def p_is(p, n):
            return isinstance(p, int) and p == n

        def first(p):
            return p_is(p, 0)

        def last(p):
            return p_is(p, PAIRS - 1)

        def n_pe(l, kind, p):
            if kind in ("XT0", "XT1") and first(p):
                return l * PE_ALL + 1 + int(kind[2])
            start = l * PE_ALL + PE_PAIR * p - 2
            if kind in ("G", "U"):
                return start + (4 if first(p) else 0) + (1 if kind == "G" else 2)
            if kind[0] == "Y":
                if last(p):
                    return l * PE_ALL + PE_ALL - 4 + 1 + int(kind[1])
                return start + PE_PAIR + 3 + int(kind[1])
            if kind[0] == "X":
                return start - PE_PAIR + {"XT0": 7, "XT1": 8}[kind]
            return start + {"HT": 9, "PT": 10, "O0": 11, "O1": 12}[kind] - (2 if last(p) else 0)

        def n_act(l, kind, p):
            if kind == "XT0":
                return l * ACT_ALL + (1 if first(p) else ACT_PAIR * (p - 1) + 3)
            return (l * ACT_ALL + ACT_PAIR * p + {"silu": 2, "HT": 4, "O0": 5, "O1": 6}[kind]
                    - (1 if last(p) and kind != "silu" else 0))

        def n_dve(l, kind, p):
            if first(p) and kind in ("onehot", "XT1", "scaled"):
                return l * DVE_ALL + 1 + ("onehot", "XT1", "scaled").index(kind)
            start = l * DVE_ALL + DVE_PAIR * p - 1
            if kind in ("onehot", "XT1"):
                return start - DVE_PAIR + {"onehot": 2, "XT1": 8}[kind] + (4 if kind == "onehot" and p_is(p, 1) else 0)
            if kind[0] == "Y":
                if last(p):
                    return l * DVE_ALL + DVE_ALL - 4 + 1 + int(kind[1])
                return start + DVE_PAIR + 4 + int(kind[1]) - (1 if p_is(p, PAIRS - 2) else 0)
            return (start + {"gated": 1, "hid": 3, "PT": 9}[kind] + (4 if first(p) and kind != "PT" else 0)
                    - ({"gated": 0, "hid": 1, "PT": 2}[kind] if last(p) else 0))

        BK = {"G": 0, "U": 1, "XT0": 2, "XT1": 3, "HT": 4, "PT": 5, "O0": 6, "O1": 7,
              "Y0": 4, "Y1": 5, "Y2": 6, "Y3": 7}

        def ring_at(l, part, j):
            return (first_expert_slot[l] + 2 * part + j) % RING

        fill_no, uses_before, fills = {}, {}, [0] * RING
        for n, entry in enumerate(stream):
            if entry is not None:
                fills[n % RING] += 1
                fill_no[n] = fills[n % RING]
            elif n in first_expert_slot:
                l = first_expert_slot.index(n)
                for part in range(3):
                    for j in range(2):
                        uses_before[l, part, j] = fills[ring_at(l, part, j)]
                        fills[ring_at(l, part, j)] += PAIRS // 2 if part == 0 or (part, j) == (1, 0) else PAIRS

        def wide(v):
            return v.rearrange("p (k n) -> p k n", k=KD)

        def tall(v):
            return v.rearrange("p (k n) -> p k n", k=4)

        block = ctx.enter_context(nc.Block())

        @block.sync
        def _(sp):
            def expert_src(l, part, e):
                w = (moe_w_gate, moe_w_up, moe_w_down)[part]
                return w[l, e].rearrange("(k p) n -> p k n", p=P)

            def expert_dst(l, part, j):
                s = ring[:, ring_at(l, part, j), :]
                return tall(s) if part == 2 else wide(s)

            def load_gate(l, p, odd, low):
                k = slice(KD // 2, KD) if low else slice(0, KD // 2)
                for j in range(2):
                    if first(p) and not low:
                        sp.wait_ge(*at(PE, stream[first_expert_slot[l] + j - RING][1]))
                    if odd:
                        dst, full = wide(odd_gate[:, j, :]), (odd_lower_full if low else odd_full)[j]
                    else:
                        dst, full = expert_dst(l, 0, j), lower_full[j] if low else slot_full[ring_at(l, 0, j)]
                    sp.dma_start(dst[:, k, :], expert_src(l, 0, 2 * p + j)[:, k, :]).then_inc(full, 16)

            def load_up(l, p, j, odd=False):
                if first(p):
                    sp.wait_ge(*at(PE, stream[first_expert_slot[l] + 2 + j - RING][1]))
                dst, full = (wide(odd_up), odd_up_full) if odd else (expert_dst(l, 1, j), slot_full[ring_at(l, 1, j)])
                sp.dma_start(dst, expert_src(l, 1, 2 * p + j)).then_inc(full, 16)

            def load_down(l, p):
                for half in range(2):
                    c = slice(half * BANK, (half + 1) * BANK)
                    for j in range(2):
                        if first(p) and half == 0:
                            sp.wait_ge(*at(PE, stream[first_expert_slot[l] + 4 + j - RING][1]))
                        full = right_full[j] if half else slot_full[ring_at(l, 2, j)]
                        sp.dma_start(expert_dst(l, 2, j)[:, :, c], expert_src(l, 2, 2 * p + j)[:, :, c]).then_inc(full, 16)

            def load_next_gate(l, p, odd):
                sp.wait_ge(gate_halfway, p - 1 + l * PAIRS)
                load_gate(l, p, odd, False)
                sp.wait_ge(ex_pe, n_pe(l, "G", p - 2))
                load_gate(l, p, odd, True)

            def load_next(l, p, odd):
                def own_up():
                    sp.wait_ge(ex_pe, n_pe(l, "U", p - 1))
                    load_up(l, p, 1)

                def own_down():
                    sp.wait_ge(ex_pe, n_pe(l, "O1", p - 1))
                    load_down(l, p)

                def next_up():
                    sp.wait_ge(ex_pe, n_pe(l, "U", p - 1))
                    load_up(l, p + 1, 0, not odd)

                if p_is(p, 1):
                    load_next_gate(l, p + 1, not odd)
                    own_up()
                    next_up()
                    own_down()
                elif last(p):
                    own_up()
                    own_down()
                else:
                    own_up()
                    load_next_gate(l, p + 1, not odd)
                    own_down()
                    next_up()

            def overflow(l):
                sp.wait_ge(rounds_known, l + 1)
                nr = sp.value_load(rounds[0:1, 0:1], min_val=1, max_val=4)
                with sp.If(nr > 1):
                    sp.wait_ge(ex_pe, (l + 1) * PE_ALL)
                    with sp.Fori(1, nr) as b:
                        with sp.Fori(0, PAIRS) as p:
                            i = (b - 1) * PAIRS + p
                            sp.wait_ge(of[l]["dve"], i * 8 + 1)
                            for part in range(3):
                                for j in range(2):
                                    sp.dma_start(expert_dst(l, part, j), expert_src(l, part, 2 * p + j)).then_inc(
                                        of[l]["slots"], 16)
                    sp.wait_ge(of[l]["end"], 1)

            for t in range(NT):
                sp.dma_start(h[:, t, :], x[0].rearrange("(t p) d -> p t d", p=P)[:, t, :]).then_inc(x_in[t], 16)
            sp.dma_start(wba[:], ab_w_in[0][:, ba0:ba0 + 2 * NH].rearrange("(k p) n -> p k n", p=P)).then_inc(wba_in, 16)
            l = -1
            i = 0
            while i < len(stream):
                if i == RING + 5:
                    sp.wait_ge(*at(PE, ("kd", 1)))
                    sp.dma_start(memtok, mem[0].rearrange("(t p) d -> p t d", p=P)).then_inc(mem_in, 16)
                if stream[i] is None:
                    l += 1
                    for low in (False, True):
                        load_gate(l, 0, False, low)
                    for j in range(2):
                        load_up(l, 0, j)
                    sp.wait_ge(*at(PE, ("xo", l, XH - 1)))
                    for low in (False, True):
                        load_gate(l, 1, True, low)
                    load_up(l, 1, 0, True)
                    load_down(l, 0)
                    load_next(l, 1, True)
                    with sp.Fori(1, PAIRS // 2 - 1) as q:
                        load_next(l, 2 * q, False)
                        load_next(l, 2 * q + 1, True)
                    load_next(l, PAIRS - 2, False)
                    load_next(l, PAIRS - 1, True)
                    overflow(l)
                    i += 3 * E
                    continue
                if i >= RING:
                    if stream[i - RING] is None:
                        j = i - RING - first_expert_slot[l]
                        part = (j % 6) // 2
                        sp.wait_ge(ex_pe, n_pe(l, ("G", "U", "O1")[part], PAIRS - 2 if j % 6 < 3 else PAIRS - 1))
                    else:
                        sp.wait_ge(*at(PE, stream[i - RING][1]))
                dst, src = wide(ring[:, i % RING, :]), stream[i][0]
                if i == 0:
                    sp.dma_start(dst[:, :, 0:T], src[:, :, 0:T]).then_inc(slot_full[0], 16)
                    sp.dma_start(dst[:, :, T:], src[:, :, T:]).then_inc(first_full, 16)
                else:
                    sp.dma_start(dst, src).then_inc(slot_full[i % RING], 16)
                i += 1
            for t in range(NT):
                sp.wait_ge(*at(DVE, ("last", t)))
                sp.dma_start(out[0].rearrange("(t p) d -> p t d", p=P)[:, t, :], h[:, t, :]).then_inc(stored, 16)
            sp.wait_ge(stored, 16 * NT)

        @block.gpsimd
        def _(pool):
            own = [0]

            def link(ins):
                own[0] += 1
                ins.then_inc(pool_own, 1)
                pool.wait_ge(pool_own, own[0])

            def done(ins):
                ins.then_inc(steps_sem[POOL], 1)

            for step in steps:
                if POOL not in takes(step):
                    continue
                kind = step[0]
                if kind == "ident":
                    link(nc.gpsimd.memset(ones[:], 1.0))
                    done(nc.gpsimd.affine_select(out=ident[:], in_=ones[:], compare_op=ALU.is_equal, fill=0.0, base=0,
                                                 pattern=[[-1, P]], channel_multiplier=1))
                    pool.dma_start(wr[:], router_w.rearrange("(k p) e -> p k e", p=P)).then_inc(vec_in, 16)
                    pool.dma_start(rb[:], router_b.unsqueeze(0).to_broadcast([P, E])).then_inc(vec_in, 16)
                    pool.dma_start(normw[:], ab_norm_w[0:1, :].to_broadcast([P, DH])).then_inc(vec_in, 16)
                elif kind == "masks":
                    nc.gpsimd.memset(shutL, 0.0)
                    nc.gpsimd.memset(nexp[:], -0.5)
                    nc.gpsimd.memset(gain[:], 0.0)
                    nc.gpsimd.iota(slot_no[:], [[1, SLOTS]], base=1, channel_multiplier=0,
                                   allow_small_or_imprecise_dtypes=True)
                    nc.gpsimd.iota(gidx[:], [[0, NT], [-1, G]], base=G, channel_multiplier=0,
                                   allow_small_or_imprecise_dtypes=True)
                    nc.gpsimd.iota(eidx[:], [[0, NT], [-1, E]], base=E, channel_multiplier=0,
                                   allow_small_or_imprecise_dtypes=True)
                    nc.gpsimd.iota(di[:, 0:P], [[0, P]], base=0, channel_multiplier=1)
                    nc.gpsimd.iota(dj[:, 0:2 * P], [[-1, 2 * P]], base=P, channel_multiplier=1)
                    link(nc.gpsimd.iota(dj[:, 2 * P:3 * P], [[-1, P]], base=0, channel_multiplier=1))
                    nc.gpsimd.affine_select(out=upto[:], in_=ones[:], compare_op=ALU.is_ge, fill=0.0, base=0,
                                            pattern=[[1, P]], channel_multiplier=-1)
                    nc.gpsimd.affine_select(out=below[:], in_=ones[:], compare_op=ALU.is_gt, fill=0.0, base=0,
                                            pattern=[[1, P]], channel_multiplier=-1)
                    nc.gpsimd.affine_select(out=shutU, in_=shutL, compare_op=ALU.is_ge, fill=NEG, base=0,
                                            pattern=[[1, P]], channel_multiplier=-1)
                    link(nc.gpsimd.iota(di[:, P:2 * P], [[1, P]], base=0, channel_multiplier=0))
                    done(nc.gpsimd.affine_select(out=shutL, in_=shutL, compare_op=ALU.is_gt, fill=NEG, base=0,
                                                 pattern=[[-1, P]], channel_multiplier=1))
                elif kind == "sumsq":
                    pool.wait_ge(*at(ACT, ("silu", 1, 1)))
                    for i in range(4):
                        v = sq[:, 2 * i:2 * i + 2, :]
                        ins = nc.gpsimd.tensor_tensor(v, qkv[:, 2 * i:2 * i + 2, :], qkv[:, 2 * i:2 * i + 2, :], ALU.mult)
                    done(ins)
                elif kind == "w_split":
                    pool.wait_ge(*at(ACT, step))
                    n, w, low = split_cols(step[1])
                    k = slice(KD // 2, KD)
                    done(nc.gpsimd.tensor_tensor(low[:, k, :], w[:, k, :],
                                                 w_high[split_no[step[1]] % 2][:, k, :].bitcast(F32), ALU.subtract))
                elif kind == "blk":
                    _, k, t = step
                    pool.wait_ge(*at(DVE, ("gram", t)))
                    if k > 0:
                        pool.wait_ge(*at(PE, ("inv_v", k - 1, t) if k > 1 else ("inv0", t)))
                        pool.wait_ge(*at(DVE, ("inv0", t)))
                    done(nc.gpsimd.tensor_tensor(Bm[:, t], DL[:, t],
                                                 levels[:, k:k + 1, :].to_broadcast([P, NH, P]), ALU.mult))
                elif kind == "ln_rstd":
                    _, l, s, t = step
                    pool.wait_ge(*at(DVE, ("ln_stats", l, s, t)))
                    done(nc.gpsimd.tensor_tensor(lnm[:, t, 2:3], lnm[:, t, 3:4], nexp[:], ALU.pow))
                elif kind == "ln_h":
                    _, l, s, t = step
                    pool.wait_ge(*at(DVE, ("ln_norm", l, s, t)))
                    pool.wait_ge(gain_in, 32 * (3 * l + s + 1))
                    link(nc.gpsimd.tensor_tensor(h[:, t, :], hn[:, t, :], gain[:, 0, :], ALU.mult))
                    done(nc.gpsimd.tensor_tensor(h[:, t, :], h[:, t, :], gain[:, 1, :], ALU.add))
            assert own[0] < 4096

        @block.scalar
        def _(act):
            own = [0]

            def link(ins):
                own[0] += 1
                ins.then_inc(act_own, 1)
                act.wait_ge(act_own, own[0])

            def done(ins):
                ins.then_inc(steps_sem[ACT], 1)

            def gains(l, s):
                for i, w in enumerate((ln_g, ln_b)):
                    act.dma_start(gain[:, i, :], w[l, s:s + 1, :].to_broadcast([P, D])).then_inc(gain_in, 16)

            act.dma_start(par_rows[0:TAPS * 12, 0, :],
                          ab_conv_w[0].rearrange("a (c p) -> (a c) p", p=P)).then_inc(rows_in, 16)
            act.dma_start(par_rows[48:48 + STAPS * KD, 0, :],
                          sc_conv_w[0].rearrange("a (c p) -> (a c) p", p=P)).then_inc(rows_in, 16)
            act.dma_start(par_rows[0:48, 1, :], ln_g.rearrange("l s (k p) -> (l s k) p", p=P)).then_inc(rows_in, 16)
            act.dma_start(par_rows[48:96, 1, :], ln_b.rearrange("l s (k p) -> (l s k) p", p=P)).then_inc(rows_in, 16)
            act.dma_start(dtb[:, 0, :], ab_dt_bias[0:1, :].to_broadcast([P, NH])).then_inc(decay_in, 16)
            act.dma_start(dtb[:, 1, :], ab_a_log[0:1, :].to_broadcast([P, NH])).then_inc(decay_in, 16)

            def experts(l):
                def gatherT_out(p):
                    act.wait_ge(ex_pe, n_pe(l, "XT0", p))
                    for k in range(4):
                        ins = nc.scalar.activation(xgT[:, k, :], ps[:, BK["XT0"], k * P:(k + 1) * P], ACTF.Identity,
                                                   bias=bias_col(l, 1, k), scale=gain_col(l, 1, k))
                    ins.then_inc(ex_act, 1)

                def pair(p):
                    act.wait_ge(ex_pe, n_pe(l, "G", p))
                    if not first(p):
                        act.wait_ge(ex_dve, n_dve(l, "hid", p - 1))
                    nc.scalar.activation(silu, ps[:, BK["G"], :], ACTF.Silu).then_inc(ex_act, 1)
                    if not last(p):
                        gatherT_out(p + 1)
                    act.wait_ge(ex_pe, n_pe(l, "HT", p))
                    nc.scalar.activation(hidT, ps[:, BK["HT"], :].rearrange("p (a b) -> p a b", a=4),
                                         ACTF.Copy).then_inc(ex_act, 1)
                    for half in range(2):
                        act.wait_ge(ex_pe, n_pe(l, f"O{half}", p))
                        nc.scalar.activation(outp[:, half * BANK:(half + 1) * BANK], ps[:, BK[f"O{half}"], :],
                                             ACTF.Copy).then_inc(ex_act, 1)

                gatherT_out(0)
                pair(0)
                with act.Fori(1, PAIRS - 1) as p:
                    pair(p)
                pair(PAIRS - 1)
                act.wait_ge(rounds_known, l + 1)
                nr = act.value_load(rounds[0:1, 0:1], min_val=1, max_val=4)
                with act.If(nr > 1):
                    with act.Fori(1, nr) as b:
                        with act.Fori(0, PAIRS) as p:
                            act.wait_ge(of[l]["pe"], ((b - 1) * PAIRS + p) * 6 + 3)
                            nc.scalar.activation(silu, ps[:, BK["G"], :], ACTF.Silu).then_inc(of[l]["act"], 1)

            def gain_col(l, s, k):
                c = (3 * l + s) * KD + k
                return par[:, 1, c:c + 1]

            def bias_col(l, s, k):
                c = 48 + (3 * l + s) * KD + k
                return par[:, 1, c:c + 1]

            def psum(step):
                return ps[:, bank_of[step], :]

            for n, seg in enumerate(segments):
                if n:
                    experts(n - 1)
                for step in seg:
                    kind = step[0]
                    if ACT not in takes(step):
                        continue
                    if PE in takes(step):
                        act.wait_ge(*at(PE, step))
                    if kind in ("xT", "memT"):
                        _, t, g = step
                        dst = (hT if kind == "xT" else memT)[:, 4 * g:4 * g + 4, t * P:(t + 1) * P]
                        done(nc.scalar.activation(dst, psum(step).rearrange("p (a b) -> p a b", a=4), ACTF.Copy))
                    elif kind == "hT":
                        _, l, s, t, g = step
                        act.wait_ge(*at(DVE, ("params",)))
                        for k in range(4):
                            ins = nc.scalar.activation(hT[:, 4 * g + k, t * P:(t + 1) * P], psum(step)[:, k * P:(k + 1) * P],
                                                       ACTF.Identity, bias=bias_col(l, s, 4 * g + k),
                                                       scale=gain_col(l, s, 4 * g + k))
                        done(ins)
                    elif kind == "gates":
                        act.wait_ge(*at(DVE, ("ba",)))
                        nc.scalar.activation(beta, ba[:, :, 0:NH], ACTF.Exp, scale=-1.0)
                        nc.scalar.activation(ea, dtb[:, 1, :], ACTF.Exp)
                        link(nc.scalar.activation(ga, gb, ACTF.Exp, scale=-1.0))
                        done(nc.scalar.activation(ga, ga, ACTF.Ln, bias=ones[:, 0:1]))
                    elif kind == "silu":
                        _, s, m = step
                        act.wait_ge(*at(DVE, ("qkv", s, m)))
                        v = qkv[:, 4 * s + 2 * m:4 * s + 2 * m + 2, :]
                        done(nc.scalar.activation(v, v, ACTF.Silu))
                    elif kind == "sumsq":
                        done(nc.scalar.activation(lss, psum(step)[:, 0:NT * 8].rearrange("p (a b) -> p a b", a=NT),
                                                  ACTF.Ln, bias=small[:, 0:1]))
                    elif kind == "cols":
                        act.wait_ge(*at(DVE, ("cumsum",)))
                        act.wait_ge(*at(ACT, ("sumsq",)))
                        nc.scalar.activation(rk, lss[:, :, NH:2 * NH], ACTF.Exp, scale=-0.5)
                        nc.scalar.activation(qs, lss[:, :, 0:NH], ACTF.Exp, scale=-0.5)
                        done(nc.scalar.activation(eg, gcol, ACTF.Exp))
                    elif kind in ("rowg", "rowh"):
                        _, t = step
                        act.wait_ge(*at(DVE, step))
                        m, col = (DU, hcol) if kind == "rowg" else (DL, gcol)
                        for hd in range(NH):
                            ins = nc.scalar.activation(m[:, t, hd, :], m[:, t, hd, :], ACTF.Exp, bias=col[:, t, hd:hd + 1])
                        done(ins)
                    elif kind == "z":
                        done(nc.scalar.activation(zs[:, step[1], :], psum(step), ACTF.Silu))
                    elif kind == "ktok":
                        act.wait_ge(*at(DVE, ("rowg", 0)))
                        link(nc.scalar.activation(kdec, kdec, ACTF.Exp))
                        for hd in range(NH):
                            ins = nc.scalar.activation(ktok[:, hd, :], psum(step)[:, hd * P:(hd + 1) * P], ACTF.Copy,
                                                       scale=kdec[:, hd:hd + 1])
                        done(ins)
                    elif kind == "vtok":
                        _, t = step
                        act.wait_ge(*at(DVE, ("gates",)))
                        act.wait_ge(*at(DVE, ("levels", 3)))
                        for hd in range(NH):
                            ins = nc.scalar.activation(vb[:, t, hd, :], psum(step)[:, hd * P:(hd + 1) * P], ACTF.Copy,
                                                       scale=beta[:, t, hd:hd + 1])
                        done(ins)
                    elif kind == "inv_v":
                        _, k, t = step
                        done(nc.scalar.activation(Vt[:, t], psum(step).rearrange("p (a b) -> p a b", a=NH), ACTF.Copy))
                    elif kind == "qd":
                        _, m = step
                        done(nc.scalar.activation(qdT[:, 2 * m:2 * m + 2, :], psum(step).rearrange("p (a b) -> p a b", a=2),
                                                  ACTF.Copy, scale=float(AH) ** -0.5))
                    elif kind == "kd":
                        _, m = step
                        act.wait_ge(*at(DVE, ("levels", 3)))
                        src = psum(step).rearrange("p (a b) -> p a b", a=2)
                        nc.scalar.activation(kdz[0:AH, 4 * m:4 * m + 4:2, :], src[0:AH], ACTF.Copy)
                        done(nc.scalar.activation(kdz[AH:P, 4 * m + 1:4 * m + 4:2, :], src[AH:P], ACTF.Copy))
                    elif kind == "d_probs":
                        _, hd = step
                        act.wait_ge(*at(DVE, ("d_scores", hd)))
                        b = hd % 2
                        nc.scalar.activation(dp[b][:, 0:2 * P], dp[b][:, 0:2 * P], ACTF.Exp, bias=dmx[b][:, 1:2])
                        done(nc.scalar.activation(dp[b][:, 2 * P:3 * P], dp[b][:, 2 * P:3 * P], ACTF.Exp, bias=dmx[b][:, 0:1]))
                    elif kind == "d_pT":
                        _, hd = step
                        if hd >= 2:
                            act.wait_ge(*at(PE, ("d_pv", (hd - 2) // 2)))
                        done(nc.scalar.activation(dpT[hd % 2][:, :], psum(step)[:, 0:3 * P], ACTF.Copy))
                    elif kind == "d_pv":
                        _, hp = step
                        ins = nc.scalar.activation(catT[:, NH + hp, :], psum(step)[:, 0:T], ACTF.Copy)
                        done(ins)
                        if hp == 3:
                            act.wait_ge(*at(PE, ("d_scores", NA - 1)))
                            gains(0, 0)
                    elif kind == "vnew":
                        _, c = step
                        done(nc.scalar.activation(vn[:, c], psum(step).rearrange("p (a b) -> p a b", a=NH), ACTF.Copy))
                    elif kind == "state":
                        done(nc.scalar.activation(st, psum(step).rearrange("p (a b) -> p a b", a=NH), ACTF.Copy))
                    elif kind == "qstate":
                        act.wait_ge(*at(DVE, ("cols",)))
                        act.wait_ge(*at(PE, ("inv_x", 5, 1)))
                        act.wait_ge(*at(PE, ("inv_u", 6, 1)))
                        for hd in range(NH):
                            ins = nc.scalar.activation(tmpo[:, hd, :], psum(step)[:, hd * P:(hd + 1) * P], ACTF.Copy,
                                                       scale=egq[:, 1, hd:hd + 1])
                        done(ins)
                    elif kind == "osq":
                        _, c = step
                        act.wait_ge(*at(DVE, ("o", c)))
                        act.wait_ge(*at(PE, ("inv_u", 6, 1)))
                        for hd in range(NH):
                            ins = nc.scalar.activation(sqo[:, hd, :], o_sb[:, c, hd, :], ACTF.Square,
                                                       accum_out=rms[:, c, hd:hd + 1])
                        link(ins)
                        link(nc.scalar.activation(rms[:, c, :], rms[:, c, :], ACTF.Ln, scale=1.0 / DH, bias=small[:, 0:1]))
                        done(nc.scalar.activation(rms[:, c, :], rms[:, c, :], ACTF.Exp, scale=-0.5))
                    elif kind == "x_split":
                        _, source, l, g = step
                        for t in range(NT):
                            src_step = (f"{source}T", t) if source in ("mem", "x") else ("hT", *{"xq": (l, 0), "sc": (0, 2)}[source], t)
                            act.wait_ge(*(at(DVE, (*src_step, 1)) if g else at(ACT, (*src_step, 0))))
                        if source != "x":
                            act.wait_ge(*{("mem", 0): at(PE, ("y", 0, 0, 0, 0)), ("xq", 0): at(PE, ("xv", 0, 1, 1)),
                                          ("sc", 0): (ex_pe, n_pe(0, "G", PAIRS - 1)), ("mem", 1): at(PE, ("sc_b", 1, 1)),
                                          ("xq", 1): at(PE, ("xv", 1, 1, 1))}[source, l])
                        k = slice(4 * g, 4 * g + 4)
                        done(nc.scalar.activation(x_high[:, k, :], x_source(source)[:, k, :], ACTF.Copy))
                    elif kind == "w_split":
                        i = split_no[step[1]]
                        n, w, low = split_cols(step[1])
                        if n == 0:
                            act.wait_ge(first_full, 16)
                        else:
                            act.wait_ge(slot_full[n % RING], 16 * fill_no[n])
                        if step[1] in (("xk", 0, 0), ("xk", 0, 1)):
                            act.wait_ge(*at(PE, ("y", 0, 0, 0, 0)))
                        if i >= 2:
                            act.wait_ge(*at(PE, split_steps[i - 2]))
                        if step[1][0] == "sc_c":
                            act.wait_ge(ex_pe, n_pe(0, "G", PAIRS - 1))
                        done(nc.scalar.activation(w_high[i % 2], w, ACTF.Copy))
                    elif kind == "xk":
                        _, l, m = step
                        done(nc.scalar.activation(xkT[:, 2 * m:2 * m + 2, :], psum(step).rearrange("p (a b) -> p a b", a=2),
                                                  ACTF.Copy))
                    elif kind == "xq":
                        _, l, m = step
                        done(nc.scalar.activation(xqT[:, 2 * m:2 * m + 2, :], psum(step).rearrange("p (a b) -> p a b", a=2),
                                                  ACTF.Copy, scale=float(D // XH) ** -0.5))
                    elif kind == "xs":
                        _, l, hd = step
                        act.wait_ge(*at(DVE, step))
                        b = hd % 2
                        if hd >= 2:
                            act.wait_ge(*at(PE, ("xp", l, hd - 2)))
                        for t in range(NT):
                            ins = nc.scalar.activation(xpr[b][:, t, :], psum(step)[:, t * T:(t + 1) * T], ACTF.Exp,
                                                       bias=xmx[b][:, t:t + 1], accum_out=xden[b][:, t:t + 1])
                        done(ins)
                    elif kind == "xo":
                        _, l, hd = step
                        done(nc.scalar.activation(xoT[:, 2 * hd:2 * hd + 2, :], psum(step).rearrange("p (a b) -> p a b", a=2),
                                                  ACTF.Copy))
                        if hd == 0:
                            for t in range(NT):
                                act.wait_ge(*at(POOL, ("ln_h", l, 0, t)))
                            gains(l, 1)
                    elif kind == "route_soft":
                        _, l = step
                        act.wait_ge(*at(DVE, ("route_t", l)))
                        done(nc.scalar.activation(sc, lg, ACTF.Exp))
                        for t in range(NT):
                            act.wait_ge(*at(POOL, ("ln_h", l, 1, t)))
                        gains(l, 2)
                    elif kind == "sc_c":
                        _, half, m = step
                        if half:
                            act.wait_ge(*at(DVE, ("sc_h", 0, 1)))
                        if (half, m) == (0, 0):
                            for t in range(NT):
                                act.wait_ge(*at(DVE, ("hT", 0, 2, t, 1)))
                        done(nc.scalar.activation(sc_u[:, 2 * m:2 * m + 2, :], psum(step).rearrange("p (a b) -> p a b", a=2),
                                                  ACTF.Copy))
                        if (half, m) == (1, 1):
                            for t in range(NT):
                                act.wait_ge(*at(POOL, ("ln_h", 0, 2, t)))
                            gains(1, 0)
                    else:
                        raise AssertionError(kind)

        @block.vector
        def _(dve):
            own = [0]
            V = nc.vector

            def link(ins):
                own[0] += 1
                ins.then_inc(dve_own, 1)
                dve.wait_ge(dve_own, own[0])

            def done(ins):
                ins.then_inc(steps_sem[DVE], 1)

            def gain_col(l, s, k):
                c = (3 * l + s) * KD + k
                return par[:, 1, c:c + 1]

            def bias_col(l, s, k):
                c = 48 + (3 * l + s) * KD + k
                return par[:, 1, c:c + 1]

            def psum(step):
                return ps[:, bank_of[step], :]

            def over_slots(v):
                return v.unsqueeze(3).to_broadcast([P, NT, 2, SLOTS])

            def slots_over():
                return slot_no[:].unsqueeze(1).unsqueeze(1).to_broadcast([P, NT, 2, SLOTS])

            def build_onehot(p):
                return V.tensor_tensor(onehot, slots_over(), over_slots(posm[:, :, bass.ds(2 * p, 2)]), ALU.is_equal)

            def gathered_cols(l, bank, k0):
                for k in range(4):
                    ins = V.tensor_scalar(xgT[:, k0 + k, :], ps[:, bank, k * P:(k + 1) * P],
                                          gain_col(l, 1, k0 + k), bias_col(l, 1, k0 + k), ALU.mult, ALU.add)
                return ins

            def experts(l):
                def gatherT_out(p):
                    dve.wait_ge(ex_pe, n_pe(l, "XT1", p))
                    gathered_cols(l, BK["XT1"], 4).then_inc(ex_dve, 1)

                def add_out(p):
                    for i in range(4):
                        t, half = i // 2, i % 2
                        dve.wait_ge(ex_pe, n_pe(l, f"Y{i}", p))
                        hv = h[:, t, half * BANK:(half + 1) * BANK]
                        V.tensor_tensor(hv, hv, ps[:, BK[f"Y{i}"], :], ALU.add).then_inc(ex_dve, 1)
                        if last(p):
                            dve.wait_ge(ex_dve, n_dve(l, f"Y{i}", p))
                            ins = V.bn_stats(lnb[:, t, half, :], hv)
                    if last(p):
                        link(ins)

                def pair(p):
                    if not first(p):
                        dve.wait_ge(ex_pe, n_pe(l, "PT", p - 1))
                    dve.wait_ge(ex_dve, n_dve(l, "onehot", p))
                    V.tensor_tensor(gated, onehot, over_slots(gates[:, :, bass.ds(2 * p, 2)]),
                                    ALU.mult).then_inc(ex_dve, 1)
                    if not last(p):
                        dve.wait_ge(ex_dve, n_dve(l, "gated", p))
                        dve.wait_ge(ex_pe, n_pe(l, "XT1", p))
                        build_onehot(p + 1).then_inc(ex_dve, 1)
                    dve.wait_ge(ex_act, n_act(l, "silu", p))
                    dve.wait_ge(ex_pe, n_pe(l, "U", p))
                    V.tensor_tensor(hid, silu, ps[:, BK["U"], :], ALU.mult).then_inc(ex_dve, 1)
                    if not first(p):
                        add_out(p - 1)
                    if not last(p):
                        gatherT_out(p + 1)
                    dve.wait_ge(ex_pe, n_pe(l, "PT", p))
                    V.tensor_copy(gatedT, ps[:, BK["PT"], 0:T]).then_inc(ex_dve, 1)

                dve.wait_ge(*at(DVE, ("place", l)))
                build_onehot(0).then_inc(ex_dve, 1)
                for i in range(1, 4):
                    ins = V.tensor_scalar(maxc[:, i:i + 1], maxc[:, 0:1], float(i * SLOTS), None, ALU.is_gt)
                link(ins)
                link(V.tensor_reduce(maxc[:, 0:1], maxc[:, 1:4], AX, ALU.add))
                V.tensor_scalar(rounds[:], maxc[:, 0:1], 1.0, None, ALU.add).then_inc(rounds_known, 1)
                gatherT_out(0)
                for t in range(NT):
                    dve.wait_ge(*at(POOL, ("ln_h", l, 1, t)))
                V.tensor_scalar(h[:], h[:], ALPHA, None, ALU.mult).then_inc(ex_dve, 1)
                dve.wait_ge(ex_dve, n_dve(l, "scaled", 0))
                pair(0)
                with dve.Fori(1, PAIRS - 1) as p:
                    pair(p)
                pair(PAIRS - 1)
                add_out(PAIRS - 1)
                dve.wait_ge(rounds_known, l + 1)
                nr = dve.value_load(rounds[0:1, 0:1], min_val=1, max_val=4)
                with dve.If(nr > 1):
                    o = of[l]
                    V.memset(maxc[:, 1:2], 0.0).then_inc(o["dve"], 1)
                    with dve.Fori(1, nr) as b:
                        V.tensor_scalar(posm, posm, float(-SLOTS), None, ALU.add).then_inc(o["shift"], 1)
                        with dve.Fori(0, PAIRS) as p:
                            i = (b - 1) * PAIRS + p
                            n_o, n_p = i * 8 + 1, i * 6
                            dve.wait_ge(o["shift"], b)
                            build_onehot(p)
                            V.tensor_tensor(gated, slots_over(), over_slots(posm[:, :, bass.ds(2 * p, 2)]),
                                            ALU.is_equal).then_inc(o["dve"], 1)
                            dve.wait_ge(o["dve"], n_o + 1)
                            V.tensor_tensor(gated, gated, over_slots(gates[:, :, bass.ds(2 * p, 2)]),
                                            ALU.mult).then_inc(o["dve"], 1)
                            dve.wait_ge(o["pe"], n_p + 1)
                            gathered_cols(l, BK["XT0"], 0)
                            gathered_cols(l, BK["XT1"], 4).then_inc(o["dve"], 1)
                            dve.wait_ge(o["pe"], n_p + 2)
                            V.tensor_copy(gatedT, ps[:, BK["PT"], 0:T]).then_inc(o["dve"], 1)
                            dve.wait_ge(o["act"], i + 1)
                            dve.wait_ge(o["pe"], n_p + 3)
                            V.tensor_tensor(hid, silu, ps[:, BK["U"], :], ALU.mult).then_inc(o["dve"], 1)
                            dve.wait_ge(o["pe"], n_p + 4)
                            V.tensor_copy(hidT, ps[:, BK["HT"], :].rearrange("p (a b) -> p a b", a=4)).then_inc(o["dve"], 1)
                            dve.wait_ge(o["pe"], n_p + 5)
                            V.tensor_copy(outp.rearrange("p (a b) -> p a b", a=2), ps[:, 6:8, :]).then_inc(o["dve"], 1)
                            dve.wait_ge(o["pe"], n_p + 6)
                            for t in range(NT):
                                ins = V.tensor_tensor(h[:, t, :].rearrange("p (a b) -> p a b", a=2),
                                                      h[:, t, :].rearrange("p (a b) -> p a b", a=2), ps[:, 4 + 2 * t:6 + 2 * t, :], ALU.add)
                            ins.then_inc(o["dve"], 1)
                            dve.wait_ge(o["dve"], n_o + 8)
                    for i in range(4):
                        ins = V.bn_stats(lnb[:, i // 2, i % 2, :], h[:, i // 2, (i % 2) * BANK:(i % 2 + 1) * BANK])
                    ins.then_inc(o["end"], 1)
                    dve.wait_ge(o["end"], 1)

            for n, seg in enumerate(segments):
                if n:
                    experts(n - 1)
                for step in seg:
                    if DVE not in takes(step):
                        continue
                    kind = step[0]
                    if PE in takes(step):
                        dve.wait_ge(*at(PE, step))
                    if kind == "levels":
                        dve.wait_ge(*at(POOL, ("masks",)))
                        part = step[1]
                        if part == 0:
                            link(V.tensor_tensor(di[:, 0:P], di[:, 0:P], di[:, P:2 * P], ALU.bitwise_xor))
                        if part < 2:
                            for k in range(4) if part == 0 else range(4, 7):
                                link(V.tensor_scalar(di[:, P:2 * P], di[:, 0:P], k, None, ALU.logical_shift_right))
                                ins = V.tensor_scalar(levels[:, k, :], di[:, P:2 * P], 1, None, ALU.is_equal)
                                if k not in (3, 6):
                                    link(ins)
                        elif part == 2:
                            dve.wait_ge(*at(DVE, ("levels", 1)))
                            link(V.tensor_scalar(di[:, :], dj[:, :], 3, None, ALU.bitwise_and))
                            link(V.tensor_scalar(df, di[:, :], 0, None, ALU.is_equal))
                            link(V.tensor_scalar(di[:, :], dj[:, :], 15, None, ALU.bitwise_and))
                            link(V.tensor_scalar(dg, di[:, :], 0, None, ALU.is_equal))
                            ins = V.tensor_tensor(df, df, dg, ALU.add)
                        else:
                            dve.wait_ge(*at(DVE, ("levels", 2)))
                            link(V.tensor_scalar(dg, dj[:, :], P, None, ALU.is_le))
                            link(V.tensor_tensor(df, df, dg, ALU.add))
                            link(V.tensor_scalar(dg, dj[:, :], 0, None, ALU.is_ge))
                            link(V.tensor_tensor(df, df, dg, ALU.mult))
                            V.tensor_copy(times[:], df)
                            ins = V.tensor_scalar(shut[:], df, 0.0, NEG, ALU.is_equal, ALU.mult)
                        done(ins)
                    elif kind == "params":
                        V.memset(small[:, 0:1], RMS_EPS)
                        V.tensor_copy(par[:, 0, 0:72], psum(step)[:, 0:72])
                        done(V.tensor_copy(par[:, 1, 0:96], psum(step)[:, P:P + 96]))
                    elif kind in ("xT", "memT"):
                        _, t, g = step
                        dst = (hT if kind == "xT" else memT)[:, 4 * g:4 * g + 4, t * P:(t + 1) * P]
                        done(V.tensor_copy(dst, psum(step).rearrange("p (a b) -> p a b", a=4)))
                    elif kind == "hT":
                        _, l, s, t, g = step
                        for k in range(4):
                            ins = V.tensor_scalar(hT[:, 4 * g + k, t * P:(t + 1) * P], psum(step)[:, k * P:(k + 1) * P],
                                                  gain_col(l, s, 4 * g + k), bias_col(l, s, 4 * g + k), ALU.mult, ALU.add)
                        done(ins)
                    elif kind == "ba":
                        link(V.tensor_copy(ba, psum(step)[:, 0:NT * 2 * NH].rearrange("p (a b) -> p a b", a=NT)))
                        dve.wait_ge(decay_in, 32)
                        link(V.tensor_tensor(ba[:, :, NH:], ba[:, :, NH:], dtb[:, 0:1, :].to_broadcast([P, NT, NH]), ALU.add))
                        done(V.scalar_tensor_tensor(gb, ba[:, :, NH:], -1.0, ba[:, :, NH:], ALU.mult, ALU.max))
                    elif kind == "gates":
                        dve.wait_ge(*at(ACT, step))
                        link(V.tensor_scalar(beta, beta, 1.0, None, ALU.add))
                        V.reciprocal(beta, beta)
                        link(V.scalar_tensor_tensor(gb, ba[:, :, NH:], 0.0, ga, ALU.max, ALU.add))
                        done(V.scalar_tensor_tensor(graw, gb, -1.0, ea.unsqueeze(1).to_broadcast([P, NT, NH]),
                                                    ALU.mult, ALU.mult))
                    elif kind == "qkv":
                        _, s, m = step
                        dve.wait_ge(*at(DVE, ("params",)))
                        for i in range(2):
                            c = 4 * s + 2 * m + i
                            src, dst = psum(step)[:, i * T:(i + 1) * T], qkv[:, c, :]

                            def tap(k):
                                return par[:, 0, k * 12 + c:k * 12 + c + 1]
                            link(V.tensor_scalar(dst, src, tap(TAPS - 1), None, ALU.mult))
                            for k in range(1, TAPS):
                                ins = V.scalar_tensor_tensor(dst[:, k:], src[:, :T - k], tap(TAPS - 1 - k), dst[:, k:],
                                                             ALU.mult, ALU.add)
                                if k < TAPS - 1 or i == 0:
                                    link(ins)
                        done(ins)
                    elif kind == "cumsum":
                        done(V.tensor_copy(gcol, psum(step)[:, 0:NT * NH].rearrange("p (a b) -> p a b", a=NT)))
                    elif kind == "cols":
                        dve.wait_ge(*at(ACT, step))
                        dve.wait_ge(*at(DVE, ("cumsum",)))
                        V.scalar_tensor_tensor(hcol, lss[:, :, NH:2 * NH], -0.5, gcol, ALU.mult, ALU.subtract)
                        link(V.tensor_scalar(qs, qs, float(DH) ** -0.5, None, ALU.mult))
                        link(V.tensor_tensor(bk, beta, rk, ALU.mult))
                        V.scalar_tensor_tensor(nc1, bk, -1.0, eg, ALU.mult, ALU.mult)
                        done(V.tensor_tensor(egq, eg, qs, ALU.mult))
                    elif kind == "rowg":
                        _, t = step
                        if t == 0:
                            link(V.tensor_copy(glast, psum(step)[:, P - 1:NH * P:P]))
                            dve.wait_ge(*at(DVE, ("cols",)))
                            V.tensor_tensor(kdec, glast, hcol[:, 0, :], ALU.add)
                        done(V.tensor_tensor(DU[:, t], psum(step).rearrange("p (a b) -> p a b", a=NH),
                                             shutU.unsqueeze(1).to_broadcast([P, NH, P]), ALU.add))
                    elif kind == "rowh":
                        _, t = step
                        done(V.tensor_tensor(DL[:, t], psum(step).rearrange("p (a b) -> p a b", a=NH),
                                             shutL.unsqueeze(1).to_broadcast([P, NH, P]), ALU.add))
                    elif kind == "gram":
                        _, t = step
                        dve.wait_ge(*at(ACT, ("rowh", t)))
                        for hd in range(NH):
                            ins = V.scalar_tensor_tensor(DL[:, t, hd, :], psum(step)[:, hd * P:(hd + 1) * P],
                                                         bk[:, t, hd:hd + 1], DL[:, t, hd, :], ALU.mult, ALU.mult)
                        done(ins)
                    elif kind == "qk":
                        _, t = step
                        dve.wait_ge(*at(ACT, ("rowg", t)))
                        done(V.tensor_tensor(DU[:, t], psum(step).rearrange("p (a b) -> p a b", a=NH), DU[:, t], ALU.mult))
                    elif kind == "inv0":
                        _, t = step
                        dve.wait_ge(*at(PE, ("sumsq",)))
                        dve.wait_ge(*at(POOL, ("blk", 0, t)))
                        eye = ident[:].unsqueeze(1).to_broadcast([P, NH, P])
                        V.scalar_tensor_tensor(X[:, t], Bm[:, t], -1.0, eye, ALU.mult, ALU.add)
                        done(V.scalar_tensor_tensor(U[:, t], psum(step).rearrange("p (a b) -> p a b", a=NH), -1.0, eye,
                                                    ALU.mult, ALU.add))
                    elif kind in ("inv_u", "inv_x"):
                        _, k, t = step
                        m = U if kind == "inv_u" else X
                        prev = ("inv0", t) if k == 1 else (kind, k - 1, t)
                        dve.wait_ge(*at(DVE, prev))
                        done(V.tensor_tensor(m[:, t], m[:, t], psum(step).rearrange("p (a b) -> p a b", a=NH), ALU.subtract))
                    elif kind == "vd":
                        c0 = step[1] * T
                        done(V.tensor_copy(vd[:, :, c0:c0 + T], psum(step).rearrange("p (a b) -> p a b", a=NT)))
                    elif kind == "d_scores":
                        _, hd = step
                        b = hd % 2
                        dve.wait_ge(*at(DVE, ("levels", 3)))
                        if hd >= 2:
                            dve.wait_ge(*at(PE, ("d_pT", hd - 2)))
                        link(V.tensor_tensor(dp[b][:, :], psum(step)[:, 0:3 * P], shut[:], ALU.add))
                        V.tensor_reduce(dmx[b][:, 1:2], dp[b][:, 0:2 * P], AX, ALU.max, negate=True)
                        done(V.tensor_reduce(dmx[b][:, 0:1], dp[b][:, 2 * P:3 * P], AX, ALU.max, negate=True))
                    elif kind == "d_probs":
                        _, hd = step
                        b = hd % 2
                        dve.wait_ge(*at(ACT, step))
                        v1, v0 = dp[b][:, 0:2 * P], dp[b][:, 2 * P:3 * P]
                        V.scalar_tensor_tensor(v1, v1, 1.0, times[:, 0:2 * P], ALU.mult, ALU.mult, accum_out=dden[b][:, 1:2])
                        link(V.scalar_tensor_tensor(v0, v0, 1.0, times[:, 2 * P:3 * P], ALU.mult, ALU.mult,
                                                    accum_out=dden[b][:, 0:1]))
                        link(V.reciprocal(drec[b], dden[b]))
                        V.tensor_scalar(v1, v1, drec[b][:, 1:2], None, ALU.mult)
                        done(V.tensor_scalar(v0, v0, drec[b][:, 0:1], None, ALU.mult))
                    elif kind == "kstate":
                        dve.wait_ge(*at(ACT, ("vtok", 1)))
                        for hd in range(NH):
                            ins = V.scalar_tensor_tensor(r1[:, hd, :], psum(step)[:, hd * P:(hd + 1) * P],
                                                         nc1[:, 1, hd:hd + 1], vb[:, 1, hd, :], ALU.mult, ALU.add)
                        done(ins)
                    elif kind == "o":
                        _, c = step
                        if c:
                            dve.wait_ge(*at(ACT, ("qstate",)))
                        else:
                            for t in range(NT):
                                dve.wait_ge(*at(PE, ("inv_v", 6, t)))
                        for hd in range(NH):
                            src, scale = psum(step)[:, hd * P:(hd + 1) * P], qs[:, c, hd:hd + 1]
                            if c:
                                ins = V.scalar_tensor_tensor(o_sb[:, c, hd, :], src, scale, tmpo[:, hd, :], ALU.mult, ALU.add)
                            else:
                                ins = V.tensor_scalar(o_sb[:, c, hd, :], src, scale, None, ALU.mult)
                        done(ins)
                    elif kind == "onorm":
                        _, c = step
                        dve.wait_ge(*at(ACT, ("z", c)))
                        if c == 0:
                            dve.wait_ge(vec_in, 48)
                        zv = zs[:, c, :].rearrange("p (a b) -> p a b", a=NH)
                        link(V.tensor_tensor(zv, zv, normw[:].unsqueeze(1).to_broadcast([P, NH, DH]), ALU.mult))
                        dve.wait_ge(*at(ACT, ("osq", c)))
                        for hd in range(NH):
                            ins = V.scalar_tensor_tensor(o_sb[:, c, hd, :], o_sb[:, c, hd, :], rms[:, c, hd:hd + 1],
                                                         zv[:, hd, :], ALU.mult, ALU.mult)
                        done(ins)
                    elif kind == "oT":
                        _, t = step
                        done(V.tensor_copy(catT[:, 0:NH, t * P:(t + 1) * P], psum(step).rearrange("p (a b) -> p a b", a=NH)))
                    elif kind == "y":
                        _, l, s, half, t = step
                        if (l, s) != (0, 0):
                            dve.wait_ge(*at(POOL, ("ln_h", l, s - 1, t) if s else ("ln_h", l - 1, 2, t)))
                        hv = h[:, t, half * BANK:(half + 1) * BANK]
                        link(V.scalar_tensor_tensor(hv, hv, ALPHA, psum(step), ALU.mult, ALU.add))
                        done(V.bn_stats(lnb[:, t, half, :], hv))
                    elif kind == "ln_stats":
                        _, l, s, t = step
                        if s < 2:
                            dve.wait_ge(*at(DVE, ("y", l, s, 1, t)))
                        link(V.bn_aggr(lnm[:, t, 0:2], lnb[:, t].rearrange("p a b -> p (a b)")))
                        done(V.tensor_scalar(lnm[:, t, 3:4], lnm[:, t, 1:2], LN_EPS, None, ALU.add))
                    elif kind == "ln_norm":
                        _, l, s, t = step
                        dve.wait_ge(*at(POOL, ("ln_rstd", l, s, t)))
                        if (l, s) == (0, 0):
                            dve.wait_ge(*at(PE, ("y", 0, 0, 1, 1)))
                        done(V.tensor_scalar(hn[:, t, :], h[:, t, :], lnm[:, t, 0:1], lnm[:, t, 2:3], ALU.subtract, ALU.mult))
                    elif kind == "last":
                        t = step[1]
                        dve.wait_ge(*at(DVE, ("ln_stats", 1, 2, t)))
                        dve.wait_ge(gain_in, 32 * 6)
                        link(V.scalar_tensor_tensor(hn[:, t, :], h[:, t, :], lnm[:, t, 0:1], gain[:, 0, :],
                                                    ALU.subtract, ALU.mult))
                        dve.wait_ge(*at(POOL, ("ln_rstd", 1, 2, t)))
                        done(V.scalar_tensor_tensor(h[:, t, :], hn[:, t, :], lnm[:, t, 2:3], gain[:, 1, :],
                                                    ALU.mult, ALU.add))
                    elif kind == "x_split":
                        _, source, l, g = step
                        dve.wait_ge(*at(ACT, step))
                        k = slice(4 * g, 4 * g + 4)
                        done(V.tensor_tensor(x_low[:, k, :], x_source(source)[:, k, :], x_high[:, k, :].bitcast(F32), ALU.subtract))
                    elif kind == "w_split":
                        dve.wait_ge(*at(ACT, step))
                        i = split_no[step[1]]
                        n, w, low = split_cols(step[1])
                        k = slice(0, KD // 2 if POOL in takes(step) else KD)
                        done(V.tensor_tensor(low[:, k, :], w[:, k, :], w_high[i % 2][:, k, :].bitcast(F32), ALU.subtract))
                    elif kind == "xv":
                        _, l, half, c = step
                        c0 = half * BANK + c * T
                        done(V.tensor_copy(xv[:, :, c0:c0 + T], psum(step).rearrange("p (a b) -> p a b", a=NT)))
                    elif kind == "xs":
                        _, l, hd = step
                        if hd >= 2:
                            dve.wait_ge(*at(ACT, ("xs", l, hd - 2)))
                        done(V.tensor_reduce(xmx[hd % 2], psum(step).rearrange("p (a b) -> p a b", a=NT), AX, ALU.max,
                                             negate=True))
                    elif kind == "xn":
                        _, l, hd = step
                        b = hd % 2
                        dve.wait_ge(*at(ACT, ("xs", l, hd)))
                        link(V.reciprocal(xrec[b], xden[b]))
                        V.tensor_scalar(xpr[b][:, 0, :], xpr[b][:, 0, :], xrec[b][:, 0:1], None, ALU.mult)
                        done(V.tensor_scalar(xpr[b][:, 1, :], xpr[b][:, 1, :], xrec[b][:, 1:2], None, ALU.mult))
                    elif kind == "xp":
                        _, l, hd = step
                        b = hd % 2
                        if hd >= 2:
                            dve.wait_ge(*at(PE, ("xo", l, hd - 2)))
                        done(V.tensor_copy(xpT[b], psum(step).rearrange("p (a b) -> p a b", a=NT)))
                    elif kind == "route":
                        done(V.tensor_copy(lgT[0:E, :], psum(step)[0:E, 0:T]))
                    elif kind == "route_t":
                        link(V.tensor_copy(lg, psum(step)[:, 0:NT * E].rearrange("p (a b) -> p a b", a=NT)))
                        link(V.tensor_reduce(s1, lg, AX, ALU.max))
                        done(V.tensor_tensor(lg, lg, s1.unsqueeze(2).to_broadcast([P, NT, E]), ALU.subtract))
                    elif kind == "route_soft":
                        dve.wait_ge(*at(ACT, step))
                        link(V.tensor_reduce(s1, sc, AX, ALU.add))
                        link(V.reciprocal(s2, s1))
                        link(V.tensor_tensor(sc, sc, s2.unsqueeze(2).to_broadcast([P, NT, E]), ALU.mult))
                        dve.wait_ge(vec_in, 48)
                        done(V.tensor_tensor(sel, sc, rb[:].unsqueeze(1).to_broadcast([P, NT, E]), ALU.add))
                    elif kind == "route_top":
                        _, l = step
                        dve.wait_ge(*at(DVE, ("route_soft", l)))
                        four = sel.rearrange("p t (g a b) -> p (t g) a b", g=G, b=2)
                        V.tensor_tensor(hi, four[:, :, :, 0], four[:, :, :, 1], ALU.max)
                        link(V.tensor_tensor(lo, four[:, :, :, 0], four[:, :, :, 1], ALU.min))
                        fl = lambda v: v.rearrange("p a b -> p (a b)")
                        V.tensor_tensor(fl(g1), hi[:, :, 0], hi[:, :, 1], ALU.max)
                        V.tensor_tensor(fl(g2), hi[:, :, 0], hi[:, :, 1], ALU.min)
                        link(V.tensor_tensor(fl(g3), lo[:, :, 0], lo[:, :, 1], ALU.max))
                        link(V.tensor_tensor(g2, g2, g3, ALU.max))
                        link(V.tensor_tensor(g1, g1, g2, ALU.add))

                        def first_max(mark, v, weights, n, top, tmp):
                            link(V.tensor_reduce(top, v, AX, ALU.max))
                            link(V.tensor_tensor(tmp, v, top.unsqueeze(2).to_broadcast([P, NT, n]), ALU.is_equal))
                            link(V.tensor_tensor(tmp, tmp, weights, ALU.mult))
                            link(V.tensor_reduce(top, tmp, AX, ALU.max))
                            link(V.tensor_tensor(mark, tmp, top.unsqueeze(2).to_broadcast([P, NT, n]), ALU.is_equal))

                        first_max(g4, g1, gidx[:], G, s1, g3)
                        inside = fl(g4).unsqueeze(2).to_broadcast([P, NT * G, E // G])
                        by4 = lambda v: v.rearrange("p t (g a) -> p (t g) a", g=G)
                        V.tensor_tensor(by4(ta), by4(sel), inside, ALU.mult)
                        link(V.tensor_scalar(g3, g4, 1.0, -NEG, ALU.subtract, ALU.mult))
                        link(V.tensor_tensor(by4(ta), by4(ta), fl(g3).unsqueeze(2).to_broadcast([P, NT * G, E // G]), ALU.add))
                        first_max(oh1, ta, eidx[:], E, s1, tb)
                        link(V.scalar_tensor_tensor(ta, oh1, NEG, ta, ALU.mult, ALU.add))
                        first_max(tc, ta, eidx[:], E, s1, tb)
                        done(V.tensor_tensor(oh1, oh1, tc, ALU.add))
                    elif kind == "weights":
                        _, l = step
                        dve.wait_ge(*at(DVE, ("route_top", l)))
                        link(V.tensor_tensor(tb, sc, oh1, ALU.mult))
                        link(V.tensor_reduce(s1, tb, AX, ALU.add))
                        link(V.reciprocal(s2, s1))
                        done(V.tensor_tensor(gates, tb, s2.unsqueeze(2).to_broadcast([P, NT, E]), ALU.mult))
                    elif kind == "place":
                        _, l = step
                        pv = psum(step)[:, 0:NT * E].rearrange("p (a b) -> p a b", a=NT)
                        V.scalar_tensor_tensor(posm, pv, 1.0, oh1, ALU.add, ALU.mult)
                        done(V.tensor_reduce(maxc[:, 0:1], psum(step)[:, NT * E:(NT + 1) * E], AX, ALU.max))
                    elif kind == "sc_h":
                        _, half, m = step
                        dve.wait_ge(*at(ACT, ("sc_c", half, m)))
                        u = sc_u[:, 2 * m:2 * m + 2, :]
                        link(V.tensor_tensor(u, u, psum(step).rearrange("p (a b) -> p a b", a=2), ALU.mult))
                        for i in range(2):
                            c = 2 * m + i

                            def tap(k):
                                return par[:, 0, 48 + k * KD + 4 * half + c:48 + k * KD + 4 * half + c + 1]
                            src, dst = sc_u[:, c, :], sc_a[:, c, :]
                            link(V.tensor_scalar(dst, src, tap(STAPS - 1), None, ALU.mult))
                            for k in range(1, STAPS):
                                ins = V.scalar_tensor_tensor(dst[:, k:], src[:, :T - k], tap(STAPS - 1 - k), dst[:, k:],
                                                             ALU.mult, ALU.add)
                                if k < STAPS - 1 or i == 0:
                                    link(ins)
                        done(ins)
                    elif kind == "sc_b":
                        _, half, m = step
                        dve.wait_ge(*at(DVE, ("sc_h", half, m)))
                        done(V.tensor_tensor(sc_y[:, 4 * half + 2 * m:4 * half + 2 * m + 2, :],
                                             psum(step).rearrange("p (a b) -> p a b", a=2),
                                             sc_a[:, 2 * m:2 * m + 2, :], ALU.mult))
                    else:
                        raise AssertionError(kind)

        @block.tensor
        def _(pe):
            M = nc.tensor.matmul

            def done(ins):
                ins.then_inc(steps_sem[PE], 1)

            def arrived(step):
                for n in slot_reader[step]:
                    pe.wait_ge(slot_full[n % RING], 16 * fill_no[n])
                return wide(ring[:, slot_reader[step][-1] % RING, :])

            def chain(dst, pairs):
                for i, (a, b) in enumerate(pairs):
                    ins = M(dst, a, b, start=i == 0, stop=i == len(pairs) - 1)
                return ins

            def heads(dst, stationary, moving):
                for hd in range(NH):
                    ins = M(dst[:, hd * P:(hd + 1) * P], stationary(hd), moving(hd), start=True, stop=True)
                return ins

            def transposes(dst, srcs):
                for i, src in enumerate(srcs):
                    ins = nc.tensor.transpose(dst[:, i * P:(i + 1) * P], src, ident[:])
                return ins

            def by_feature(step, m, rhs):
                w = arrived(step)
                b = ps[:, bank_of[step], :]
                for i in range(2):
                    c = (2 * (m % 2) + i) * P
                    ins = chain(b[:, i * T:(i + 1) * T], [(w[:, k, c:c + P], rhs[:, k, :]) for k in range(KD)])
                done(ins)

            def split_parts(step):
                for e in takes(("w_split", step)):
                    pe.wait_ge(*at(e, ("w_split", step)))
                kind, l = step[:2]
                source = {"xk": ("mem", 0), "xv": ("mem", l), "xq": ("xq", l), "sc_c": ("sc", 0), "sc_h": ("sc", 0),
                          "sc_b": ("sc", 0)}.get(kind, ("x", 0))
                for g in range(2):
                    pe.wait_ge(*at(DVE, ("x_split", *source, g)))
                return w_high[split_no[step] % 2], split_cols(step)[2]

            def by_feature_split(step):
                high, low = split_parts(step)
                b = ps[:, bank_of[step], :]
                for i in range(2):
                    c = slice(i * P, (i + 1) * P)
                    ins = chain(b[:, i * T:(i + 1) * T],
                                [pair for k in range(KD) for pair in (
                                    (high[:, k, c], x_low[:, k, :]), (high[:, k, c], x_high[:, k, :]),
                                    (low[:, k, c], x_high[:, k, :]))])
                done(ins)

            def by_token_split(step):
                high, low = split_parts(step)
                b = ps[:, bank_of[step], :]
                for t in range(NT):
                    c = slice(t * P, (t + 1) * P)
                    ins = chain(b[:, t * T:(t + 1) * T],
                                [pair for k in range(KD) for pair in (
                                    (x_high[:, k, c], low[:, k, :]), (x_high[:, k, c], high[:, k, :]),
                                    (x_low[:, k, c], high[:, k, :]))])
                done(ins)

            def by_token(step, src, t):
                w = arrived(step)
                done(chain(ps[:, bank_of[step], :], [(src[:, k, t * P:(t + 1) * P], w[:, k, :]) for k in range(KD)]))

            def early(s):
                return range(NH, NH + 3) if s == 0 else range(4)

            def have_hT(l, s):
                for t in range(NT):
                    pe.wait_ge(*at(ACT, ("hT", l, s, t, 0)))
                    pe.wait_ge(*at(DVE, ("hT", l, s, t, 1)))

            def slot_of(l, part, j):
                s = ring[:, ring_at(l, part, j), :]
                return tall(s) if part == 2 else wide(s)

            def gather(half):
                for k in range(4):
                    c = slice((4 * half + k) * P, (4 * half + k + 1) * P)
                    ins = chain(ps[:, BK[f"XT{half}"], k * P:(k + 1) * P],
                                [(hn[:, t, c], onehot[:, t].rearrange("p a b -> p (a b)")) for t in range(NT)])
                return ins

            def up_product(l, part, odd=False, ks=range(KD)):
                b = ps[:, BK["GU"[part]], :]
                w = [slot_of(l, part, j) for j in range(2)]
                if odd:
                    w = [wide(odd_up), w[1]] if part else [wide(odd_gate[:, j, :]) for j in range(2)]
                for k in ks:
                    for j in range(2):
                        r = slice(j * SLOTS, (j + 1) * SLOTS)
                        ins = M(b[r, :], xgT[:, k, r], w[j][:, k, :], start=k == 0, stop=k == KD - 1)
                return ins

            def down_product(l, half):
                b = ps[:, BK[f"O{half}"], :]
                for k in range(4):
                    for j in range(2):
                        r = slice(j * SLOTS, (j + 1) * SLOTS)
                        ins = M(b[r, :], hidT[:, k, r], slot_of(l, 2, j)[:, k, half * BANK:(half + 1) * BANK],
                                start=k == 0, stop=k == 3)
                return ins

            def hidden_T():
                return transposes(ps[:, BK["HT"], :], [hid[:, k * P:(k + 1) * P] for k in range(4)])

            def gated_T():
                return transposes(ps[:, BK["PT"], :], [gated[:, t].rearrange("p a b -> p (a b)") for t in range(NT)])

            def scatter(i):
                t, half = i // 2, i % 2
                return M(ps[:, BK[f"Y{i}"], :], gatedT[:, t * P:(t + 1) * P], outp[:, half * BANK:(half + 1) * BANK],
                         start=True, stop=True)

            def experts(l):
                def weights(part, n):
                    for j in range(2):
                        pe.wait_ge(slot_full[ring_at(l, part, j)], 16 * (n + (uses_before[l, part, j] + 1)))

                def gate_weights(odd, turn):
                    if odd:
                        for j in range(2):
                            pe.wait_ge(odd_full[j], 16 * (turn + (l * (PAIRS // 2) + 1)))
                    else:
                        weights(0, turn)

                def gathered(p):
                    pe.wait_ge(ex_dve, n_dve(l, "onehot", p))
                    if not first(p):
                        pe.wait_ge(ex_act, n_act(l, "XT0", p - 1))
                        pe.wait_ge(ex_dve, n_dve(l, "XT1", p - 1))
                    gather(0).then_inc(ex_pe, 1)
                    gather(1).then_inc(ex_pe, 1)

                def scattered(p):
                    pe.wait_ge(ex_act, n_act(l, "O1", p))
                    pe.wait_ge(ex_dve, n_dve(l, "PT", p))
                    for i in range(4):
                        scatter(i).then_inc(ex_pe, 1)

                def gate_weights_lower(odd, turn):
                    for j in range(2):
                        pe.wait_ge((odd_lower_full if odd else lower_full)[j], 16 * (turn + (l * (PAIRS // 2) + 1)))

                def pair(p, odd, turn):
                    pe.wait_ge(ex_act, n_act(l, "XT0", p))
                    gate_weights(odd, turn)
                    up_product(l, 0, odd, range(KD // 2)).then_inc(gate_halfway, 1)
                    pe.wait_ge(ex_dve, n_dve(l, "XT1", p))
                    gate_weights_lower(odd, turn)
                    up_product(l, 0, odd, range(KD // 2, KD)).then_inc(ex_pe, 1)
                    pe.wait_ge(*((odd_up_full, 16 * (turn + (l * (PAIRS // 2) + 1))) if odd else
                                 (slot_full[ring_at(l, 1, 0)], 16 * (turn + (uses_before[l, 1, 0] + 1)))))
                    pe.wait_ge(slot_full[ring_at(l, 1, 1)], 16 * (p + (uses_before[l, 1, 1] + 1)))
                    up_product(l, 1, odd).then_inc(ex_pe, 1)
                    if not first(p):
                        scattered(p - 1)
                    if not last(p):
                        gathered(p + 1)
                    pe.wait_ge(ex_dve, n_dve(l, "hid", p))
                    if not first(p):
                        pe.wait_ge(ex_dve, n_dve(l, "Y0", p - 1))
                    hidden_T().then_inc(ex_pe, 1)
                    if not first(p):
                        pe.wait_ge(ex_dve, n_dve(l, "Y1", p - 1))
                    gated_T().then_inc(ex_pe, 1)
                    pe.wait_ge(ex_act, n_act(l, "HT", p))
                    for half in range(2):
                        if half:
                            for j in range(2):
                                pe.wait_ge(right_full[j], 16 * (p + (l * PAIRS + 1)))
                        else:
                            weights(2, p)
                        if not first(p):
                            pe.wait_ge(ex_dve, n_dve(l, f"Y{2 + half}", p - 1))
                        down_product(l, half).then_inc(ex_pe, 1)

                for s in segments[l][-12:]:
                    if PE in takes(s):
                        pe.wait_ge(*at(empties(s), s))
                gathered(0)
                pair(0, False, 0)
                with pe.Fori(0, PAIRS // 2 - 1) as q:
                    pair(2 * q + 1, True, q)
                    pair(2 * q + 2, False, q + 1)
                pair(PAIRS - 1, True, PAIRS // 2 - 1)
                scattered(PAIRS - 1)
                pe.wait_ge(rounds_known, l + 1)
                nr = pe.value_load(rounds[0:1, 0:1], min_val=1, max_val=4)
                with pe.If(nr > 1):
                    o = of[l]
                    pe.wait_ge(ex_dve, (l + 1) * DVE_ALL)
                    with pe.Fori(1, nr) as b:
                        with pe.Fori(0, PAIRS) as p:
                            i = (b - 1) * PAIRS + p
                            n_d = i * 8 + 1
                            pe.wait_ge(o["dve"], n_d + 2)
                            gather(0)
                            gather(1).then_inc(o["pe"], 1)
                            pe.wait_ge(o["dve"], n_d + 3)
                            gated_T().then_inc(o["pe"], 1)
                            pe.wait_ge(o["dve"], n_d + 4)
                            pe.wait_ge(o["slots"], (i + 1) * 96)
                            up_product(l, 0)
                            up_product(l, 1).then_inc(o["pe"], 1)
                            pe.wait_ge(o["dve"], n_d + 5)
                            hidden_T().then_inc(o["pe"], 1)
                            pe.wait_ge(o["dve"], n_d + 6)
                            down_product(l, 0)
                            down_product(l, 1).then_inc(o["pe"], 1)
                            pe.wait_ge(o["dve"], n_d + 7)
                            for k in range(4):
                                ins = scatter(k)
                            ins.then_inc(o["pe"], 1)
                    pe.wait_ge(o["end"], 1)

            for n, seg in enumerate(segments):
                if n:
                    experts(n - 1)
                for step in seg:
                    if PE not in takes(step):
                        continue
                    kind = step[0]
                    b = ps[:, bank_of[step], :]
                    prev = before[step]
                    if prev == "experts":
                        bank = bank_of[step]
                        pe.wait_ge(*{0: (ex_act, n_act(n - 1, "silu", PAIRS - 1)), 1: (ex_dve, n_dve(n - 1, "hid", PAIRS - 1)),
                                     2: (ex_act, n_act(n - 1, "XT0", PAIRS - 1)), 3: (ex_dve, n_dve(n - 1, "XT1", PAIRS - 1)),
                                     }.get(bank, (ex_dve, n * DVE_ALL)))
                    elif prev is not None:
                        pe.wait_ge(*at(empties(prev), prev))
                    if kind == "params":
                        pe.wait_ge(rows_in, 64)
                        rows = TAPS * 12 + STAPS * KD
                        nc.tensor.transpose(b[:, 0:rows], par_rows[0:rows, 0, :], ident[0:rows, 0:rows])
                        done(nc.tensor.transpose(b[:, P:P + 96], par_rows[0:96, 1, :], ident[0:96, 0:96]))
                    elif kind == "xT":
                        _, t, g = step
                        pe.wait_ge(*at(POOL, ("ident",)))
                        pe.wait_ge(x_in[t], 16)
                        done(transposes(b, [h[:, t, (4 * g + k) * P:(4 * g + k + 1) * P] for k in range(4)]))
                    elif kind == "memT":
                        _, t, g = step
                        pe.wait_ge(mem_in, 16)
                        done(transposes(b, [memtok[:, t, (4 * g + k) * P:(4 * g + k + 1) * P] for k in range(4)]))
                    elif kind == "ba":
                        pe.wait_ge(wba_in, 16)
                        for t in range(NT):
                            ins = chain(b[:, t * 2 * NH:(t + 1) * 2 * NH],
                                        [(hT[:, k, t * P:(t + 1) * P], wba[:, k, :]) for k in range(KD)])
                        done(ins)
                    elif kind == "qkv":
                        if step == ("qkv", 0, 0):
                            for t in range(NT):
                                pe.wait_ge(*at(ACT, ("xT", t, 0)))
                                pe.wait_ge(*at(DVE, ("xT", t, 1)))
                        if is_split(step):
                            by_feature_split(step)
                        else:
                            by_feature(step, step[2], hT)
                    elif kind in ("qd", "kd"):
                        by_feature_split(step)
                    elif kind == "vd":
                        by_token_split(step)
                    elif kind == "z":
                        by_token(step, hT, step[1])
                    elif kind == "sumsq":
                        pe.wait_ge(*at(POOL, step))
                        for t in range(NT):
                            for i in range(8):
                                ins = M(b[:, 8 * t + i:8 * t + i + 1], sq[:, i, t * P:(t + 1) * P], ones[:, 0:1],
                                        start=True, stop=True)
                        done(ins)
                    elif kind == "cumsum":
                        pe.wait_ge(*at(POOL, ("masks",)))
                        pe.wait_ge(*at(DVE, ("gates",)))
                        done(M(b[:, 0:NT * NH], upto[:], graw.rearrange("p a b -> p (a b)"), start=True, stop=True))
                    elif kind == "rowg":
                        t = step[1]
                        done(heads(b, lambda hd: graw[:, t, hd:hd + 1].to_broadcast([P, P]), lambda hd: upto[:]))
                    elif kind == "rowh":
                        t = step[1]
                        pe.wait_ge(*at(DVE, ("cols",)))
                        done(heads(b, lambda hd: hcol[:, t, hd:hd + 1].to_broadcast([P, P]), lambda hd: ident[:]))
                    elif kind == "gram":
                        t = step[1]
                        kv = lambda hd: qkv[:, NH + hd, t * P:(t + 1) * P]
                        done(heads(b, kv, kv))
                    elif kind == "qk":
                        t = step[1]
                        done(heads(b, lambda hd: qkv[:, NH + hd, t * P:(t + 1) * P],
                                   lambda hd: qkv[:, hd, t * P:(t + 1) * P]))
                    elif kind == "inv0":
                        t = step[1]
                        pe.wait_ge(*at(POOL, ("blk", 0, t)))
                        done(transposes(b, [Bm[:, t, hd, :] for hd in range(NH)]))
                    elif kind == "ktok":
                        done(transposes(b, [qkv[:, NH + hd, 0:P] for hd in range(NH)]))
                    elif kind == "vtok":
                        t = step[1]
                        pe.wait_ge(*at(ACT, ("silu", 2, 1)))
                        done(transposes(b, [qkv[:, 2 * NH + hd, t * P:(t + 1) * P] for hd in range(NH)]))
                    elif kind == "inv_v":
                        _, k, t = step
                        pe.wait_ge(*at(POOL, ("blk", k, t)))
                        pe.wait_ge(*at(DVE, ("inv0", t) if k == 1 else ("inv_u", k - 1, t)))
                        done(heads(b, lambda hd: Bm[:, t, hd, :], lambda hd: U[:, t, hd, :]))
                    elif kind == "inv_u":
                        _, k, t = step
                        pe.wait_ge(*at(ACT, ("inv_v", k, t)))
                        pe.wait_ge(*at(DVE, ("inv0", t) if k == 1 else ("inv_x", k - 1, t)))
                        done(heads(b, lambda hd: X[:, t, hd, :], lambda hd: Vt[:, t, hd, :]))
                    elif kind == "inv_x":
                        _, k, t = step
                        done(heads(b, lambda hd: Vt[:, t, hd, :], lambda hd: X[:, t, hd, :]))
                    elif kind == "vnew":
                        _, c = step
                        pe.wait_ge(*at(DVE, ("inv_u", 6, c)))
                        if c:
                            pe.wait_ge(*at(DVE, ("kstate",)))
                        else:
                            pe.wait_ge(*at(ACT, ("vtok", 0)))
                        rhs = r1 if c else vb[:, 0]
                        done(heads(b, lambda hd: U[:, c, hd, :], lambda hd: rhs[:, hd, :]))
                    elif kind == "state":
                        pe.wait_ge(*at(ACT, ("vnew", 0)))
                        done(heads(b, lambda hd: ktok[:, hd, :], lambda hd: vn[:, 0, hd, :]))
                    elif kind == "kstate":
                        pe.wait_ge(*at(ACT, ("state",)))
                        done(heads(b, lambda hd: qkv[:, NH + hd, P:T], lambda hd: st[:, hd, :]))
                    elif kind == "qstate":
                        done(heads(b, lambda hd: qkv[:, hd, P:T], lambda hd: st[:, hd, :]))
                    elif kind == "o":
                        c = step[1]
                        pe.wait_ge(*at(ACT, ("vnew", c)))
                        pe.wait_ge(*at(DVE, ("qk", c)))
                        done(heads(b, lambda hd: DU[:, c, hd, :], lambda hd: vn[:, c, hd, :]))
                    elif kind == "oT":
                        t = step[1]
                        pe.wait_ge(*at(DVE, ("onorm", t)))
                        done(transposes(b, [o_sb[:, t, hd, :] for hd in range(NH)]))
                    elif kind == "d_scores":
                        hd = step[1]
                        m = hd // 4
                        pe.wait_ge(*at(ACT, ("qd", m)))
                        pe.wait_ge(*at(ACT, ("kd", m)))
                        M(b[:, 0:T], qdT[:, hd // 2, P:T], kdz[:, hd, :], start=True, stop=True)
                        done(M(b[:, T:T + P], qdT[:, hd // 2, 0:P], kdz[:, hd, 0:P], start=True, stop=True))
                    elif kind == "d_pT":
                        hd = step[1]
                        pe.wait_ge(*at(DVE, ("d_probs", hd)))
                        v = dp[hd % 2]
                        done(transposes(b, [v[:, 2 * P:3 * P], v[:, 0:P], v[:, P:2 * P]]))
                    elif kind == "d_pv":
                        hp = step[1]
                        for j in range(2):
                            hd = 2 * hp + j
                            pe.wait_ge(*at(ACT, ("d_pT", hd)))
                            if hp == 0:
                                pe.wait_ge(*at(DVE, ("vd", j)))
                            r = slice(j * AH, (j + 1) * AH)
                            M(b[r, 0:T], vd[:, 0, hd * AH:(hd + 1) * AH], dpT[j][:, 0:T], start=True, stop=False)
                            ins = M(b[r, P:T], vd[:, 1, hd * AH:(hd + 1) * AH], dpT[j][:, T:T + P], start=False, stop=True)
                        done(ins)
                    elif kind == "y_first":
                        _, l, s, half, t = step
                        pe.wait_ge(*at(ACT, ("xo", l, 1) if s else ("d_pv", 2)))
                        w = arrived(("y", l, s, half, t))
                        src = xoT if s else catT
                        for k in early(s):
                            ins = M(b, src[:, k, t * P:(t + 1) * P], w[:, k, :], start=k == early(s)[0], stop=False)
                        done(ins)
                    elif kind == "y" and ("y_first", *step[1:]) in count:
                        _, l, s, half, t = step
                        if s:
                            pe.wait_ge(*at(ACT, ("xo", l, XH - 1)))
                        else:
                            pe.wait_ge(*at(DVE, ("oT", t)))
                            pe.wait_ge(*at(ACT, ("d_pv", 3)))
                        w = arrived(step)
                        src = xoT if s else catT
                        late = [k for k in range(KD) if k not in early(s)]
                        for k in late:
                            ins = M(b, src[:, k, t * P:(t + 1) * P], w[:, k, :], start=False, stop=k == late[-1])
                        done(ins)
                    elif kind == "y":
                        _, l, s, half, t = step
                        if (l, s) == (0, 0):
                            src = catT
                        elif s == 0:
                            src = sc_y
                            pe.wait_ge(*at(DVE, ("sc_b", 1, 1)))
                        else:
                            src = xoT
                            pe.wait_ge(*at(ACT, ("xo", l, XH - 1)))
                        by_token(step, src, t)
                    elif kind == "hT":
                        _, l, s, t, g = step
                        pe.wait_ge(*at(DVE, ("ln_norm", l, s, t)))
                        done(transposes(b, [hn[:, t, (4 * g + k) * P:(4 * g + k + 1) * P] for k in range(4)]))
                    elif kind == "xk":
                        for t in range(NT):
                            pe.wait_ge(*at(ACT, ("memT", t, 0)))
                            pe.wait_ge(*at(DVE, ("memT", t, 1)))
                        if is_split(step):
                            by_feature_split(step)
                        else:
                            by_feature(step, step[2], memT)
                    elif kind == "xv":
                        by_token_split(step)
                    elif kind == "xq":
                        have_hT(step[1], 0)
                        if is_split(step):
                            by_feature_split(step)
                        else:
                            by_feature(step, step[2], hT)
                    elif kind == "xs":
                        _, l, hd = step
                        pe.wait_ge(*at(ACT, ("xk", l, hd)))
                        pe.wait_ge(*at(ACT, ("xq", l, hd)))
                        for t in range(NT):
                            ins = chain(b[:, t * T:(t + 1) * T],
                                        [(xqT[:, 2 * hd + i, t * P:(t + 1) * P], xkT[:, 2 * hd + i, :]) for i in range(2)])
                        done(ins)
                    elif kind == "xp":
                        _, l, hd = step
                        pe.wait_ge(*at(DVE, ("xn", l, hd)))
                        v = xpr[hd % 2]
                        done(transposes(b, [v[:, t, mt * P:(mt + 1) * P] for mt in range(NT) for t in range(NT)]))
                    elif kind == "xo":
                        _, l, hd = step
                        pe.wait_ge(*at(DVE, ("xp", l, hd)))
                        for half in range(2):
                            for t in range(NT):
                                pe.wait_ge(*at(DVE, ("xv", l, half, t)))
                        for i in range(2):
                            c = (2 * hd + i) * P
                            ins = chain(b[:, i * T:(i + 1) * T],
                                        [(xv[:, mt, c:c + P], xpT[hd % 2][:, mt, :]) for mt in range(NT)])
                        done(ins)
                    elif kind == "route":
                        l = step[1]
                        pe.wait_ge(vec_in, 48)
                        for t in range(NT):
                            pe.wait_ge(*at(ACT, ("hT", l, 1, t, 0)))
                            pe.wait_ge(*at(DVE, ("hT", l, 1, t, 1)))
                            ins = chain(b[0:E, t * P:(t + 1) * P], [(wr[:, k, :], hT[:, k, t * P:(t + 1) * P]) for k in range(KD)])
                        done(ins)
                    elif kind == "route_t":
                        pe.wait_ge(*at(DVE, ("route", step[1])))
                        for t in range(NT):
                            ins = nc.tensor.transpose(b[:, t * E:(t + 1) * E], lgT[0:E, t * P:(t + 1) * P], ident[0:E, 0:E])
                        done(ins)
                    elif kind == "place":
                        pe.wait_ge(*at(DVE, ("route_top", step[1])))
                        M(b[:, 0:2 * E], below[:], oh1.rearrange("p a b -> p (a b)"), start=True, stop=False)
                        M(b[:, E:2 * E], ones[:], oh1[:, 0, :], start=False, stop=True)
                        done(chain(b[:, 2 * E:3 * E], [(ones[:], oh1[:, 0, :]), (ones[:], oh1[:, 1, :])]))
                    elif kind in ("sc_c", "sc_h", "sc_b"):
                        by_feature_split(step)
                    else:
                        raise AssertionError(kind)


_INS = ["x", "mem", "ab_w_in", "ab_conv_w", "ab_a_log", "ab_dt_bias", "ab_norm_w", "ab_w_out", "sc_w_in", "sc_conv_w",
        "sc_w_out", "xa_w_q", "xa_w_kv", "xa_w_o", "router_w", "router_b", "moe_w_gate", "moe_w_up", "moe_w_down",
        "ln_g", "ln_b"]


def kernel(**inputs):
    import concourse.bacc as bacc
    from concourse.bass_utils import run_bass_kernel_spmd

    nc = bacc.Bacc("TRN2", target_bir_lowering=False, num_devices=1, dynamic_dma_scratch_size=DMA_SCRATCH)
    arrays, args = {}, []
    for name in _INS:
        a = np.ascontiguousarray(inputs[name])
        arrays[f"in_{name}"] = a
        args.append(nc.dram_tensor(f"in_{name}", a.shape, mybir.dt.from_np(a.dtype), kind="ExternalInput").ap())
    shape = inputs["x"].shape
    result = nc.dram_tensor("out_h", shape, F32, kind="ExternalOutput").ap()
    trunk_kernel(nc, *args, result)
    r = run_bass_kernel_spmd(nc, [arrays], core_ids=[0])
    return r.results[0]["out_h"]
```
